# Optimizing a Trainium2 kernel written in Bass

```python
import math
import jax, jax.numpy as jnp
from jax import lax
import numpy as np

D_MODEL = 1024
BATCH = 1
SEQ = 256
DEPTH = 1

GRID_W = 64
CTX_LEN = 256
RMS_EPS = 1e-6
SHORT_CONV = 3
D_HYENA = 512
HYENA_ORDER = 2
HYENA_EMB_BANDS = 16
HYENA_EMB_DIM = 1 + 2 * HYENA_EMB_BANDS
HYENA_FILTER_HIDDEN = 64
HYENA_DECAY_TARGET = 1e-2
HYENA_MIN_DECAY = math.log(HYENA_DECAY_TARGET) / 1.5
HYENA_MAX_DECAY = math.log(HYENA_DECAY_TARGET) / 0.3
MLSTM_HEADS = 4
MLSTM_HEAD_DIM = 128
D_MLSTM = MLSTM_HEADS * MLSTM_HEAD_DIM
MLSTM_CHUNK = 128
N_BRANCHES = 2
HY_COLS = (HYENA_ORDER + 1) * D_HYENA
ML_COLS = 4 * D_MLSTM
GATE_COLS = 4 * MLSTM_HEADS
MERGE_COLS = N_BRANCHES * D_MODEL
ML_START = HY_COLS
GATE_START = ML_START + ML_COLS
MERGE_START = GATE_START + GATE_COLS
D_IN_PROJ = MERGE_START + MERGE_COLS
N_EXPERTS = 16
EC_CAPACITY_FACTOR = 2
D_FF_EXPERT = 2 * D_MODEL


def rmsnorm(x, g):
    x32 = x.astype(jnp.float32)
    y = x32 * lax.rsqrt(jnp.mean(x32 * x32, axis=-1, keepdims=True) + RMS_EPS)
    return y.astype(x.dtype) * g

def modulate(h, shift, scale):
    return h * (1.0 + scale[:, None, :]) + shift[:, None, :]

def short_conv(u, w, rows, row_len):
    B, L, C = u.shape
    K = w.shape[0]
    ur = u.reshape(B, rows, row_len, C)
    up = jnp.pad(ur, ((0, 0), (0, 0), (K // 2, K // 2), (0, 0)))
    y = sum(up[:, :, j:j + row_len] * w[j] for j in range(K))
    return y.reshape(B, L, C)

def hyena_filters(L, w1, b1, w2, b2, w3):
    f32 = lambda a: a.astype(jnp.float32)
    t = jnp.linspace(0.0, 1.0, L, dtype=jnp.float32)[:, None]
    bands = jnp.linspace(1e-4, HYENA_EMB_BANDS - 1, HYENA_EMB_BANDS, dtype=jnp.float32)[None, :]
    ang = (2.0 * math.pi / L) * jnp.arange(L, dtype=jnp.float32)[:, None] * bands
    z = jnp.concatenate([t, jnp.cos(ang), jnp.sin(ang)], axis=-1)
    h = jnp.sin(z @ f32(w1) + f32(b1))
    h = jnp.sin(h @ f32(w2) + f32(b2))
    h = (h @ f32(w3)).reshape(L, HYENA_ORDER, 2, D_HYENA)
    deltas = jnp.abs(jnp.linspace(HYENA_MIN_DECAY, HYENA_MAX_DECAY, D_HYENA, dtype=jnp.float32))
    return h * jnp.exp(-t * deltas)[:, None, None, :]

def bidir_long_conv(u, h, skip):
    B, L, C = u.shape
    k = jnp.concatenate([h[:, 0], jnp.zeros((1, C), h.dtype), h[:0:-1, 1]], axis=0)
    U = jnp.fft.rfft(u.astype(jnp.float32), n=2 * L, axis=1)
    Kf = jnp.fft.rfft(k, n=2 * L, axis=0)
    y = jnp.fft.irfft(U * Kf[None], n=2 * L, axis=1)[:, :L]
    return (y + u.astype(jnp.float32) * skip.astype(jnp.float32)).astype(u.dtype)

def hyena_branch(hy_p, conv_w, f_w1, f_b1, f_w2, f_b2, f_w3, skip, rows, row_len):
    L = hy_p.shape[1]
    parts = jnp.split(short_conv(hy_p, conv_w, rows, row_len), HYENA_ORDER + 1, axis=-1)
    filt = hyena_filters(L, f_w1, f_b1, f_w2, f_b2, f_w3)
    z = parts[0]
    for o in range(HYENA_ORDER):
        z = parts[o + 1] * bidir_long_conv(z, filt[:, o], skip[o])
    return z

def mlstm_chunk_scan(q, k, v, log_i, log_f, state0):
    G, H, L, dh = q.shape
    nc = L // MLSTM_CHUNK

    def chunks(a):
        return jnp.moveaxis(a.reshape(G, H, nc, MLSTM_CHUNK, *a.shape[3:]), 2, 0)

    tril = jnp.tril(jnp.ones((MLSTM_CHUNK, MLSTM_CHUNK), dtype=bool))

    def step(carry, inp):
        C, n, m = carry
        qc, kc, vc, li, lf = inp
        b = jnp.cumsum(lf, axis=-1)
        logw = jnp.where(tril, b[..., :, None] - b[..., None, :] + li[..., None, :], -jnp.inf)
        m_inter = b + m[..., None]
        m_t = jnp.maximum(m_inter, logw.max(-1))
        a_intra = jnp.exp(logw - m_t[..., None]) * jnp.einsum('ghtd,ghsd->ghts', qc, kc)
        a_inter = jnp.exp(m_inter - m_t)
        num = jnp.einsum('ghts,ghse->ghte', a_intra, vc) + a_inter[..., None] * jnp.einsum('ghtd,ghde->ghte', qc, C)
        den = a_intra.sum(-1) + a_inter * jnp.einsum('ghtd,ghd->ght', qc, n)
        h = num / jnp.maximum(jnp.abs(den), jnp.exp(-m_t))[..., None]
        b_end = b[..., -1]
        logw_end = b_end[..., None] - b + li
        m_new = jnp.maximum(b_end + m, logw_end.max(-1))
        w_end = jnp.exp(logw_end - m_new[..., None])
        decay = jnp.exp(b_end + m - m_new)
        C_new = decay[..., None, None] * C + jnp.einsum('ghs,ghsd,ghse->ghde', w_end, kc, vc)
        n_new = decay[..., None] * n + jnp.einsum('ghs,ghsd->ghd', w_end, kc)
        return (C_new, n_new, m_new), h

    state, hs = lax.scan(step, state0, (chunks(q), chunks(k), chunks(v), chunks(log_i), chunks(log_f)))
    return jnp.moveaxis(hs, 0, 2).reshape(G, H, L, dh), state

def mlstm_zero_state(batch):
    g = 2 * batch
    return (jnp.zeros((g, MLSTM_HEADS, MLSTM_HEAD_DIM, MLSTM_HEAD_DIM), jnp.float32),
            jnp.zeros((g, MLSTM_HEADS, MLSTM_HEAD_DIM), jnp.float32),
            jnp.zeros((g, MLSTM_HEADS), jnp.float32))

def mlstm_branch(ml_p, gate_p, conv_w, norm_g, rows, row_len, state0):
    B, L, _ = ml_p.shape
    q_pre, k_pre, v, o = jnp.split(ml_p, 4, axis=-1)
    qk = jax.nn.silu(short_conv(jnp.concatenate([q_pre, k_pre], axis=-1), conv_w, rows, row_len))
    q, k = jnp.split(qk, 2, axis=-1)

    def heads(a):
        return a.reshape(B, L, MLSTM_HEADS, MLSTM_HEAD_DIM).transpose(0, 2, 1, 3).astype(jnp.float32)

    q = heads(q) * (MLSTM_HEAD_DIM ** -0.5)
    k = heads(k)
    v = heads(v)
    g = gate_p.astype(jnp.float32).reshape(B, L, 4, MLSTM_HEADS).transpose(2, 0, 3, 1)
    i_f, f_f, i_b, f_b = g[0], g[1], g[2], g[3]
    flip = lambda a: jnp.flip(a, axis=2)
    q2 = jnp.concatenate([q, flip(q)], axis=0)
    k2 = jnp.concatenate([k, flip(k)], axis=0)
    v2 = jnp.concatenate([v, flip(v)], axis=0)
    log_i = jnp.concatenate([i_f, flip(i_b)], axis=0)
    log_f = jax.nn.log_sigmoid(jnp.concatenate([f_f, flip(f_b)], axis=0))
    h2, state = mlstm_chunk_scan(q2, k2, v2, log_i, log_f, state0)
    h = h2[:B] + flip(h2[B:])
    h = h * lax.rsqrt(jnp.mean(h * h, axis=-1, keepdims=True) + RMS_EPS)
    h = h.transpose(0, 2, 1, 3).reshape(B, L, D_MLSTM).astype(ml_p.dtype) * norm_g
    return h * jax.nn.sigmoid(o), state

def token_mixer(h, w_in, b_in, hy_conv, hy_f_w1, hy_f_b1, hy_f_w2, hy_f_b2, hy_f_w3, hy_skip,
                ml_conv, ml_norm_g, w_branch_hy, w_branch_ml, w_out, rows, row_len, state0):
    p = h @ w_in + b_in
    y_a = hyena_branch(p[..., :ML_START], hy_conv, hy_f_w1, hy_f_b1, hy_f_w2, hy_f_b2, hy_f_w3, hy_skip, rows, row_len)
    y_b, state = mlstm_branch(p[..., ML_START:GATE_START], p[..., GATE_START:MERGE_START], ml_conv, ml_norm_g, rows, row_len, state0)
    g_a, g_b = jnp.split(jax.nn.sigmoid(p[..., MERGE_START:]), N_BRANCHES, axis=-1)
    y = (g_a * (y_a @ w_branch_hy) + g_b * (y_b @ w_branch_ml)) @ w_out
    return y, state

def expert_choice_ffn(h, w_router, w1, w3, w2):
    B, N, D = h.shape
    cap = EC_CAPACITY_FACTOR * N // N_EXPERTS
    aff = jax.nn.softmax((h @ w_router).astype(jnp.float32), axis=-1)
    gate, idx = lax.top_k(jnp.swapaxes(aff, 1, 2), cap)
    bidx = jnp.arange(B)[:, None, None]
    xg = h[bidx, idx]
    a = jnp.einsum('becd,edf->becf', xg, w1)
    b = jnp.einsum('becd,edf->becf', xg, w3)
    ye = jnp.einsum('becf,efd->becd', jax.nn.silu(a) * b, w2) * gate[..., None].astype(h.dtype)
    return jnp.zeros_like(h).at[bidx, idx].add(ye)

def first_inputs(seed: int = 0) -> dict:
    key = jax.random.key(seed)
    ks = jax.random.split(key, 32)
    D = D_MODEL
    nrm = lambda k, shape, scale: jax.random.normal(k, shape, jnp.float32) * scale
    forget_offset = np.zeros((D_IN_PROJ,), np.float32)
    forget_offset[GATE_START + MLSTM_HEADS:GATE_START + 2 * MLSTM_HEADS] = np.linspace(3.0, 6.0, MLSTM_HEADS)
    forget_offset[GATE_START + 3 * MLSTM_HEADS:GATE_START + 4 * MLSTM_HEADS] = np.linspace(3.0, 6.0, MLSTM_HEADS)
    return {
        'x': nrm(ks[0], (BATCH, SEQ, D), 1.0),
        'c': nrm(ks[1], (BATCH, D), 1.0),
        'ctx': nrm(ks[2], (BATCH, CTX_LEN, D), 1.0),
        'c_ctx': nrm(ks[3], (D,), 1.0),
        'w_ada': nrm(ks[4], (DEPTH, D, 6 * D), 0.5 * D ** -0.5),
        'b_ada': nrm(ks[5], (DEPTH, 6 * D), 0.02),
        'norm_mix_g': 1.0 + nrm(ks[6], (DEPTH, D), 0.02),
        'norm_ffn_g': 1.0 + nrm(ks[7], (DEPTH, D), 0.02),
        'w_in': nrm(ks[8], (DEPTH, D, D_IN_PROJ), D ** -0.5),
        'b_in': nrm(ks[9], (DEPTH, D_IN_PROJ), 0.02) + jnp.asarray(forget_offset),
        'hy_conv': nrm(ks[10], (DEPTH, SHORT_CONV, HY_COLS), 0.5),
        'hy_f_w1': nrm(ks[11], (DEPTH, HYENA_EMB_DIM, HYENA_FILTER_HIDDEN), HYENA_EMB_DIM ** -0.5),
        'hy_f_b1': nrm(ks[12], (DEPTH, HYENA_FILTER_HIDDEN), 0.1),
        'hy_f_w2': nrm(ks[13], (DEPTH, HYENA_FILTER_HIDDEN, HYENA_FILTER_HIDDEN), HYENA_FILTER_HIDDEN ** -0.5),
        'hy_f_b2': nrm(ks[14], (DEPTH, HYENA_FILTER_HIDDEN), 0.1),
        'hy_f_w3': nrm(ks[15], (DEPTH, HYENA_FILTER_HIDDEN, HYENA_ORDER * 2 * D_HYENA), 0.03 * HYENA_FILTER_HIDDEN ** -0.5),
        'hy_skip': nrm(ks[16], (DEPTH, HYENA_ORDER, D_HYENA), 1.0),
        'ml_conv': nrm(ks[17], (DEPTH, SHORT_CONV, 2 * D_MLSTM), 0.5),
        'ml_norm_g': 1.0 + nrm(ks[18], (DEPTH, D_MLSTM), 0.02),
        'w_branch_hy': nrm(ks[19], (DEPTH, D_HYENA, D), D_HYENA ** -0.5),
        'w_branch_ml': nrm(ks[20], (DEPTH, D_MLSTM, D), D_MLSTM ** -0.5),
        'w_out': nrm(ks[21], (DEPTH, D, D), D ** -0.5),
        'w_router': nrm(ks[22], (DEPTH, D, N_EXPERTS), D ** -0.5),
        'w_exp1': nrm(ks[23], (DEPTH, N_EXPERTS, D, D_FF_EXPERT), D ** -0.5),
        'w_exp3': nrm(ks[24], (DEPTH, N_EXPERTS, D, D_FF_EXPERT), D ** -0.5),
        'w_exp2': nrm(ks[25], (DEPTH, N_EXPERTS, D_FF_EXPERT, D), D_FF_EXPERT ** -0.5),
        'final_norm_g': 1.0 + nrm(ks[26], (D,), 0.02),
    }

def first_block(x, c, ctx, c_ctx, w_ada, b_ada, norm_mix_g, norm_ffn_g, w_in, b_in,
              hy_conv, hy_f_w1, hy_f_b1, hy_f_w2, hy_f_b2, hy_f_w3, hy_skip,
              ml_conv, ml_norm_g, w_branch_hy, w_branch_ml, w_out,
              w_router, w_exp1, w_exp3, w_exp2, final_norm_g):
    B, L, _ = x.shape
    rows = L // GRID_W
    Lc = ctx.shape[1]
    s_lat = jax.nn.silu(c)
    s_ctx = jax.nn.silu(c_ctx)[None, :]
    for l in range(DEPTH):
        last = l == DEPTH - 1
        ada_x = jnp.split(s_lat @ w_ada[l] + b_ada[l], 6, axis=-1)
        ada_c = jnp.split(s_ctx @ w_ada[l] + b_ada[l], 6, axis=-1)
        mix_params = (w_in[l], b_in[l], hy_conv[l], hy_f_w1[l], hy_f_b1[l], hy_f_w2[l], hy_f_b2[l], hy_f_w3[l],
                      hy_skip[l], ml_conv[l], ml_norm_g[l], w_branch_hy[l], w_branch_ml[l], w_out[l])
        hc = modulate(rmsnorm(ctx, norm_mix_g[l]), ada_c[0], ada_c[1])
        if last:
            pc = hc @ w_in[l][:, ML_START:MERGE_START] + b_in[l][ML_START:MERGE_START]
            _, ctx_state = mlstm_branch(pc[..., :ML_COLS], pc[..., ML_COLS:], ml_conv[l], ml_norm_g[l],
                                        1, Lc, mlstm_zero_state(B))
        else:
            yc, ctx_state = token_mixer(hc, *mix_params, 1, Lc, mlstm_zero_state(B))
            ctx = ctx + ada_c[2][:, None, :] * yc
            hc2 = modulate(rmsnorm(ctx, norm_ffn_g[l]), ada_c[3], ada_c[4])
            ctx = ctx + ada_c[5][:, None, :] * expert_choice_ffn(hc2, w_router[l], w_exp1[l], w_exp3[l], w_exp2[l])
        hx = modulate(rmsnorm(x, norm_mix_g[l]), ada_x[0], ada_x[1])
        yx, _ = token_mixer(hx, *mix_params, rows, GRID_W, ctx_state)
        x = x + ada_x[2][:, None, :] * yx
        hx2 = modulate(rmsnorm(x, norm_ffn_g[l]), ada_x[3], ada_x[4])
        x = x + ada_x[5][:, None, :] * expert_choice_ffn(hx2, w_router[l], w_exp1[l], w_exp3[l], w_exp2[l])
    return rmsnorm(x, final_norm_g)


DEPTH_2 = 2

HEAD_DIM = 64
NSA_HEADS = 8
NSA_KV_GROUPS = 2
NSA_HPG = NSA_HEADS // NSA_KV_GROUPS
MOBA_HEADS = 8
CMP_STRIDE = 16
CMP_LEN = 2 * CMP_STRIDE
CMP_HIDDEN = 128
SEL_BLOCK = 64
SEL_TOPK = 16
WINDOW = 512
MOBA_BLOCK = 256
MOBA_TOPK = 3
Q_CHUNK = 128
ROPE_THETA = 10000.0
D_FF = -(-8 * D_MODEL // (3 * 256)) * 256
NEG = -1e30
FORCE_SCORE = 1e4

NSA_QW = NSA_HEADS * HEAD_DIM
NSA_KVW = NSA_KV_GROUPS * HEAD_DIM
NSA_GATEW = NSA_HEADS * 3
MOBA_W = MOBA_HEADS * HEAD_DIM
BRANCH_GATEW = 2 * D_MODEL
IN_SPLITS = (NSA_QW, NSA_KVW, NSA_KVW, NSA_KVW, NSA_KVW, NSA_KVW, NSA_KVW, NSA_GATEW, MOBA_W, MOBA_W, MOBA_W, BRANCH_GATEW)
IN_COLS = NSA_QW + 6 * NSA_KVW + NSA_GATEW + 3 * MOBA_W + BRANCH_GATEW


def rms_norm(x, g, eps=1e-6):
    x32 = x.astype(jnp.float32)
    y = x32 * lax.rsqrt(jnp.mean(x32 * x32, axis=-1, keepdims=True) + eps)
    return y.astype(x.dtype) * g

def rope_angles(pos):
    inv = 1.0 / (ROPE_THETA ** (jnp.arange(0, HEAD_DIM, 2, dtype=jnp.float32) / HEAD_DIM))
    ang = pos.astype(jnp.float32)[..., None] * inv
    return jnp.cos(ang), jnp.sin(ang)

def apply_rope(x, cos, sin):
    cos = cos.astype(x.dtype)
    sin = sin.astype(x.dtype)
    x1, x2 = jnp.split(x, 2, axis=-1)
    return jnp.concatenate([x1 * cos - x2 * sin, x2 * cos + x1 * sin], axis=-1)

def masked_softmax(s, mask):
    s = jnp.where(mask, s.astype(jnp.float32), NEG)
    return jnp.where(mask, jax.nn.softmax(s, axis=-1), 0.0)

def _heads(t, n):
    b, s, _ = t.shape
    return t.reshape(b, s, n, HEAD_DIM).transpose(0, 2, 1, 3)

def nsa_mixer(q, k_cmp, v_cmp, k_slc, v_slc, k_win, v_win, gate_logits, positions, cos, sin,
              q_gain, k_gain, cmp_pe, ck_w1, ck_w2, cv_w1, cv_w2):
    B, S, _ = q.shape
    G, HPG, DH = NSA_KV_GROUPS, NSA_HPG, HEAD_DIM
    scale = DH ** -0.5
    cs, sn = cos[:, None], sin[:, None]
    q = apply_rope(rms_norm(_heads(q, NSA_HEADS), q_gain), cs, sn).reshape(B, G, HPG, S, DH)
    k_slc = apply_rope(rms_norm(_heads(k_slc, G), k_gain), cs, sn)
    k_win = apply_rope(rms_norm(_heads(k_win, G), k_gain), cs, sn)
    v_slc = _heads(v_slc, G)
    v_win = _heads(v_win, G)

    n_cmp = S // CMP_STRIDE - 1

    def blocks(t):
        tc = t.reshape(B, G, S // CMP_STRIDE, CMP_STRIDE, DH)
        blk = jnp.concatenate([tc[:, :, :-1], tc[:, :, 1:]], axis=3) + cmp_pe
        return blk.reshape(B, G, n_cmp, CMP_LEN * DH)

    k_c = jax.nn.gelu(blocks(_heads(k_cmp, G)) @ ck_w1) @ ck_w2
    v_c = jax.nn.gelu(blocks(_heads(v_cmp, G)) @ cv_w1) @ cv_w2
    cmp_start = jnp.arange(n_cmp) * CMP_STRIDE
    cmp_end = cmp_start + CMP_LEN - 1
    cos_c, sin_c = rope_angles(positions[:, cmp_end])
    k_c = apply_rope(rms_norm(k_c, k_gain), cos_c[:, None], sin_c[:, None])

    n_sb = S // SEL_BLOCK
    n_pick = min(SEL_TOPK, n_sb)
    sel_start = jnp.arange(n_sb) * SEL_BLOCK
    overlap = ((cmp_start[:, None] < sel_start[None, :] + SEL_BLOCK) &
               (cmp_start[:, None] + CMP_LEN > sel_start[None, :])).astype(jnp.float32)
    k_sb = k_slc.reshape(B, G, n_sb, SEL_BLOCK, DH)
    v_sb = v_slc.reshape(B, G, n_sb, SEL_BLOCK, DH)
    k_wp = jnp.pad(k_win, ((0, 0), (0, 0), (WINDOW, 0), (0, 0)))
    v_wp = jnp.pad(v_win, ((0, 0), (0, 0), (WINDOW, 0), (0, 0)))
    gates = jax.nn.sigmoid(gate_logits).reshape(B, S, G, HPG, 3).transpose(0, 2, 3, 1, 4)
    bi = jnp.arange(B)[:, None, None, None]
    gi = jnp.arange(G)[None, :, None, None]
    blk_id = jnp.arange(n_sb)

    def chunk(ci):
        s0 = ci * Q_CHUNK
        t = s0 + jnp.arange(Q_CHUNK)
        qc = lax.dynamic_slice_in_dim(q, s0, Q_CHUNK, axis=3)
        s_c = jnp.einsum('bghqd,bgnd->bghqn', qc, k_c) * scale
        p_c = masked_softmax(s_c, cmp_end[None, :] <= t[:, None])
        o_c = jnp.einsum('bghqn,bgnd->bghqd', p_c.astype(v_c.dtype), v_c)
        imp = jnp.einsum('bghqn,nj->bgqj', p_c, overlap)
        forced = (blk_id[None, :] == 0) | (blk_id[None, :] == (t // SEL_BLOCK)[:, None])
        imp = jnp.where(forced, FORCE_SCORE, imp)
        imp = jnp.where(sel_start[None, :] <= t[:, None], imp, NEG)
        _, idx = lax.top_k(imp, n_pick)
        kg = k_sb[bi, gi, idx]
        vg = v_sb[bi, gi, idx].reshape(B, G, Q_CHUNK, n_pick * SEL_BLOCK, DH)
        tok = idx[..., None] * SEL_BLOCK + jnp.arange(SEL_BLOCK)
        m_s = (tok <= t[:, None, None]).reshape(B, G, 1, Q_CHUNK, n_pick * SEL_BLOCK)
        s_s = jnp.einsum('bghqd,bgqnkd->bghqnk', qc, kg).reshape(B, G, HPG, Q_CHUNK, n_pick * SEL_BLOCK) * scale
        p_s = masked_softmax(s_s, m_s)
        o_s = jnp.einsum('bghqm,bgqmd->bghqd', p_s.astype(vg.dtype), vg)
        kw = lax.dynamic_slice_in_dim(k_wp, s0, Q_CHUNK + WINDOW, axis=2)
        vw = lax.dynamic_slice_in_dim(v_wp, s0, Q_CHUNK + WINDOW, axis=2)
        kpos = s0 - WINDOW + jnp.arange(Q_CHUNK + WINDOW)
        m_w = (kpos[None, :] <= t[:, None]) & (kpos[None, :] > t[:, None] - WINDOW) & (kpos[None, :] >= 0)
        s_w = jnp.einsum('bghqd,bgkd->bghqk', qc, kw) * scale
        p_w = masked_softmax(s_w, m_w)
        o_w = jnp.einsum('bghqk,bgkd->bghqd', p_w.astype(vw.dtype), vw)
        gc = lax.dynamic_slice_in_dim(gates, s0, Q_CHUNK, axis=3)
        return gc[..., 0:1] * o_c + gc[..., 1:2] * o_s + gc[..., 2:3] * o_w

    out = lax.map(chunk, jnp.arange(S // Q_CHUNK))
    return out.transpose(1, 0, 4, 2, 3, 5).reshape(B, S, NSA_HEADS * DH)

def moba_mixer(q, k, v, cos, sin, q_gain, k_gain):
    B, S, _ = q.shape
    H, DH, MB = MOBA_HEADS, HEAD_DIM, MOBA_BLOCK
    scale = DH ** -0.5
    cs, sn = cos[:, None], sin[:, None]
    q = apply_rope(rms_norm(_heads(q, H), q_gain), cs, sn)
    k = apply_rope(rms_norm(_heads(k, H), k_gain), cs, sn)
    v = _heads(v, H)
    n_blk = -(-S // MB)
    pad = n_blk * MB - S
    k_p = jnp.pad(k, ((0, 0), (0, 0), (0, pad), (0, 0)))
    v_p = jnp.pad(v, ((0, 0), (0, 0), (0, pad), (0, 0)))
    k_blk = k_p.reshape(B, H, n_blk, MB, DH)
    v_blk = v_p.reshape(B, H, n_blk, MB, DH)
    k_mean = jnp.mean(k_blk.astype(jnp.float32), axis=3).astype(k.dtype)
    n_pick = min(MOBA_TOPK, n_blk)
    bi = jnp.arange(B)[:, None, None, None]
    hi = jnp.arange(H)[None, :, None, None]
    blk_id = jnp.arange(n_blk)

    def chunk(ci):
        s0 = ci * Q_CHUNK
        t = s0 + jnp.arange(Q_CHUNK)
        own = s0 // MB
        qc = lax.dynamic_slice_in_dim(q, s0, Q_CHUNK, axis=2)
        gate = jnp.einsum('bhqd,bhnd->bhqn', qc, k_mean).astype(jnp.float32)
        _, idx = lax.top_k(jnp.where(blk_id < own, gate, NEG), n_pick)
        m_sel = jnp.repeat(idx < own, MB, axis=-1)
        kg = k_blk[bi, hi, idx]
        vg = v_blk[bi, hi, idx].reshape(B, H, Q_CHUNK, n_pick * MB, DH)
        s_sel = jnp.einsum('bhqd,bhqnkd->bhqnk', qc, kg).reshape(B, H, Q_CHUNK, n_pick * MB) * scale
        ko = lax.dynamic_slice_in_dim(k_p, own * MB, MB, axis=2)
        vo = lax.dynamic_slice_in_dim(v_p, own * MB, MB, axis=2)
        s_own = jnp.einsum('bhqd,bhkd->bhqk', qc, ko) * scale
        m_own = jnp.broadcast_to((own * MB + jnp.arange(MB))[None, :] <= t[:, None], s_own.shape)
        p = masked_softmax(jnp.concatenate([s_sel, s_own], axis=-1),
                           jnp.concatenate([m_sel, m_own], axis=-1)).astype(v.dtype)
        return (jnp.einsum('bhqm,bhqmd->bhqd', p[..., :n_pick * MB], vg) +
                jnp.einsum('bhqk,bhkd->bhqd', p[..., n_pick * MB:], vo))

    out = lax.map(chunk, jnp.arange(S // Q_CHUNK))
    return out.transpose(1, 0, 3, 2, 4).reshape(B, S, H * DH)

def second_inputs(seed: int = 0) -> dict:
    key = jax.random.key(seed)
    ks = jax.random.split(key, 24)

    def nrm(k, shape, s):
        return jax.random.normal(k, shape, jnp.float32) * s

    L, D, DH = DEPTH_2, D_MODEL, HEAD_DIM
    positions = (jnp.arange(SEQ, dtype=jnp.int32)[None, :] +
                 jax.random.randint(ks[2], (BATCH, 1), 0, 1024, dtype=jnp.int32)).astype(jnp.int32)
    return {
        "x": nrm(ks[0], (BATCH, SEQ, D), 1.0),
        "c": nrm(ks[1], (BATCH, D), 1.0),
        "positions": positions,
        "w_ada": nrm(ks[3], (L, D, 6 * D), 0.5 * D ** -0.5),
        "b_ada": nrm(ks[4], (L, 6 * D), 0.02),
        "norm_mix": 1.0 + nrm(ks[5], (L, D), 0.02),
        "norm_ffn": 1.0 + nrm(ks[6], (L, D), 0.02),
        "w_in": nrm(ks[7], (L, D, IN_COLS), D ** -0.5),
        "nsa_q_gain": 1.0 + nrm(ks[8], (L, DH), 0.02),
        "nsa_k_gain": 1.0 + nrm(ks[9], (L, DH), 0.02),
        "nsa_cmp_pe": nrm(ks[10], (L, CMP_LEN, DH), 0.1),
        "nsa_cmp_k_w1": nrm(ks[11], (L, CMP_LEN * DH, CMP_HIDDEN), (CMP_LEN * DH) ** -0.5),
        "nsa_cmp_k_w2": nrm(ks[12], (L, CMP_HIDDEN, DH), CMP_HIDDEN ** -0.5),
        "nsa_cmp_v_w1": nrm(ks[13], (L, CMP_LEN * DH, CMP_HIDDEN), (CMP_LEN * DH) ** -0.5),
        "nsa_cmp_v_w2": nrm(ks[14], (L, CMP_HIDDEN, DH), CMP_HIDDEN ** -0.5),
        "moba_q_gain": 1.0 + nrm(ks[15], (L, DH), 0.02),
        "moba_k_gain": 1.0 + nrm(ks[16], (L, DH), 0.02),
        "w_up_nsa": nrm(ks[17], (L, NSA_QW, D), NSA_QW ** -0.5),
        "w_up_moba": nrm(ks[18], (L, MOBA_W, D), MOBA_W ** -0.5),
        "w_out": nrm(ks[19], (L, D, D), D ** -0.5),
        "w_ffn_in": nrm(ks[20], (L, D, 2 * D_FF), D ** -0.5),
        "w_ffn_out": nrm(ks[21], (L, D_FF, D), D_FF ** -0.5),
    }

def second_block(x, c, positions, w_ada, b_ada, norm_mix, norm_ffn, w_in,
              nsa_q_gain, nsa_k_gain, nsa_cmp_pe, nsa_cmp_k_w1, nsa_cmp_k_w2,
              nsa_cmp_v_w1, nsa_cmp_v_w2, moba_q_gain, moba_k_gain,
              w_up_nsa, w_up_moba, w_out, w_ffn_in, w_ffn_out):
    cos, sin = rope_angles(positions)
    split_at = np.cumsum(IN_SPLITS)[:-1].tolist()
    for l in range(DEPTH_2):
        ada = jax.nn.silu(c) @ w_ada[l] + b_ada[l]
        sh_m, sc_m, g_m, sh_f, sc_f, g_f = jnp.split(ada[:, None, :], 6, axis=-1)
        h = rms_norm(x, norm_mix[l]) * (1.0 + sc_m) + sh_m
        (q_a, kc_a, vc_a, ks_a, vs_a, kw_a, vw_a, g_a,
         q_b, k_b, v_b, g_br) = jnp.split(h @ w_in[l], split_at, axis=-1)
        y_a = nsa_mixer(q_a, kc_a, vc_a, ks_a, vs_a, kw_a, vw_a, g_a, positions, cos, sin,
                        nsa_q_gain[l], nsa_k_gain[l], nsa_cmp_pe[l], nsa_cmp_k_w1[l],
                        nsa_cmp_k_w2[l], nsa_cmp_v_w1[l], nsa_cmp_v_w2[l])
        y_b = moba_mixer(q_b, k_b, v_b, cos, sin, moba_q_gain[l], moba_k_gain[l])
        gate_a, gate_b = jnp.split(jax.nn.sigmoid(g_br), 2, axis=-1)
        merged = gate_a * (y_a @ w_up_nsa[l]) + gate_b * (y_b @ w_up_moba[l])
        x = x + g_m * (merged @ w_out[l])
        h = rms_norm(x, norm_ffn[l]) * (1.0 + sc_f) + sh_f
        gt, up = jnp.split(h @ w_ffn_in[l], 2, axis=-1)
        x = x + g_f * ((jax.nn.silu(gt) * up) @ w_ffn_out[l])
    return x


def setup_inputs(seed=0):
    out = dict(first_inputs(seed))
    for name, value in second_inputs(seed + 1).items():
        if name != "x":
            out[name + "_2"] = value
    return out


def reference(
    x, c, ctx, c_ctx, w_ada, b_ada, norm_mix_g, norm_ffn_g, w_in, b_in, hy_conv, hy_f_w1,
    hy_f_b1, hy_f_w2, hy_f_b2, hy_f_w3, hy_skip, ml_conv, ml_norm_g, w_branch_hy, w_branch_ml,
    w_out, w_router, w_exp1, w_exp3, w_exp2, final_norm_g, c_2, positions_2, w_ada_2, b_ada_2,
    norm_mix_2, norm_ffn_2, w_in_2, nsa_q_gain_2, nsa_k_gain_2, nsa_cmp_pe_2, nsa_cmp_k_w1_2,
    nsa_cmp_k_w2_2, nsa_cmp_v_w1_2, nsa_cmp_v_w2_2, moba_q_gain_2, moba_k_gain_2, w_up_nsa_2,
    w_up_moba_2, w_out_2, w_ffn_in_2, w_ffn_out_2,
):
    x = first_block(
        x, c, ctx, c_ctx, w_ada, b_ada, norm_mix_g, norm_ffn_g, w_in, b_in, hy_conv, hy_f_w1,
        hy_f_b1, hy_f_w2, hy_f_b2, hy_f_w3, hy_skip, ml_conv, ml_norm_g, w_branch_hy,
        w_branch_ml, w_out, w_router, w_exp1, w_exp3, w_exp2, final_norm_g,
    )
    return second_block(
        x, c_2, positions_2, w_ada_2, b_ada_2, norm_mix_2, norm_ffn_2, w_in_2, nsa_q_gain_2,
        nsa_k_gain_2, nsa_cmp_pe_2, nsa_cmp_k_w1_2, nsa_cmp_k_w2_2, nsa_cmp_v_w1_2,
        nsa_cmp_v_w2_2, moba_q_gain_2, moba_k_gain_2, w_up_nsa_2, w_up_moba_2, w_out_2,
        w_ffn_in_2, w_ffn_out_2,
    )


_drawn_inputs = setup_inputs


def setup_inputs(seed=0):
    import zlib

    import numpy as np

    out = dict(_drawn_inputs(seed))
    spreads = {}
    factors = {'b_ada': 3.186,
     'norm_mix_g': 8.0,
     'norm_ffn_g': 7.249,
     'hy_f_b1': 8.0,
     'hy_f_w2': 2.831,
     'hy_f_b2': 7.142,
     'hy_f_w3': 2.928,
     'ml_norm_g': 42.67,
     'final_norm_g': 2.678,
     'norm_mix_2': 8.0,
     'norm_ffn_2': 6.531,
     'nsa_q_gain_2': 8.0,
     'nsa_k_gain_2': 8.0,
     'nsa_cmp_pe_2': 7.87,
     'moba_q_gain_2': 8.0,
     'moba_k_gain_2': 8.0}
    for name, (base, spread) in spreads.items():
        noise = np.random.default_rng([zlib.crc32(name.encode()), seed]).standard_normal(out[name].shape)
        drawn = base * np.exp(spread * noise) if base else spread * noise
        out[name] = __import__('jax').numpy.asarray(drawn.astype(out[name].dtype))
    for name, factor in factors.items():
        out[name] = (out[name] * factor).astype(out[name].dtype)
    return out
```

```python
from contextlib import ExitStack

import numpy as np

import concourse.bass as bass
from concourse import mybir

F32 = mybir.dt.float32
I32 = mybir.dt.int32
ALU = mybir.AluOpType
ACT = mybir.ActivationFunctionType
AX = mybir.AxisListType.X

P = 128
N = 256
NC = N // P
D = 1024
KD = D // P
EPS = 1e-6
HY = 512
HEADS, DH = 4, 128
ML0, GATE0, MERGE0, IN1 = 1536, 3584, 3600, 5648
EXPERTS, CAP, FF1 = 16, 32, 2048
LAYERS = 2
HD = 64
KV0, KW0, QB0, GATES2, MERGE2, IN2 = 512, 1024, 1304, 1280, 2840, 4888
NCMP = N // 16 - 1
FF2 = 2816
FB = FF2 // P
NEG = -1e30
BIG = 1e30
RING, TILE = 4, 4096


class Book:

    def __init__(self):
        self.where, self.per, self.bank, self.loads, self.known = {}, {}, {}, {}, False


class Steps:

    def __init__(self, engine, k):
        self.engine, self.k, self.count, self.cur, self.now = engine, k, {}, None, None

    def stage(self, stage):
        self.cur = f"{stage}_{self.engine}"
        self.count.setdefault(self.cur, 0)

    def step(self, *names):
        self.count[self.cur] += 1
        self.now = (self.cur, self.count[self.cur])
        for n in names:
            self.k.book.where[n] = self.now
        return self.k.sem(self.cur), 1

    def last(self):
        return self.k.value(*self.now)


class Kernel:
    def __init__(self, nc, ctx, book):
        self.nc, self.ctx, self.book, self.sems, self.turn = nc, ctx, book, {}, None
        self.loads = {}

    def sem(self, name):
        if name not in self.sems:
            self.sems[name] = self.ctx.enter_context(self.nc.semaphore(name))
        return self.sems[name]

    def load(self, name):
        self.loads[name] = self.loads.get(name, 0) + 16
        return self.sem(name), 16

    def loaded(self, name):
        return self.sem(name), self.book.loads.get(name, 16)

    def at(self, name, back=0):
        if not self.book.known:
            return self.value(*next(iter(self.book.where.values())), back)
        return self.value(*self.book.where[name], back)

    def value(self, sem, count, back=0):
        if not sem.startswith("expert_"):
            return self.sem(sem), count
        per = self.book.per.get(sem, 1)
        if self.turn is None:
            return self.sem(sem), EXPERTS * per + count
        return self.sem(sem), self.turn * per + (count + (1 - back) * per)


def view(t, off, parts, *dims):
    n = int(np.prod(dims))
    v = t[0:parts, off:off + n]
    if len(dims) == 2:
        return v.rearrange("p (a b) -> p a b", a=dims[0])
    if len(dims) == 3:
        return v.rearrange("p (a b c) -> p a b c", a=dims[0], b=dims[1])
    if len(dims) == 4:
        return v.rearrange("p (a b c d) -> p a b c d", a=dims[0], b=dims[1], c=dims[2])
    return v


def spread(ap, axis, n):
    u = ap.unsqueeze(axis)
    shape = list(u.shape)
    shape[axis] = n
    return u.broadcast_to(shape)


def build(nc, A, out, book):
    ctx = ExitStack()
    with ctx:
        program(nc, ctx, A, out, book)


def program(nc, ctx, A, out, book):
    K = Kernel(nc, ctx, book)
    at = K.at
    PE, AC, DV, SP = (Steps(n, K) for n in ("pe", "act", "dve", "sp"))

    def sb(name, n, parts=P):
        return ctx.enter_context(nc.sbuf_tensor(name, [parts, n], F32))

    ring = sb("ring", RING * TILE)
    xT = view(sb("xT", KD * N), 0, P, KD, N)
    hx = sb("hx", KD * 2 * N)
    scr = sb("scr", KD * 2 * N)
    mg = sb("mg", KD * 2 * N)
    arena = sb("arena", 24504)
    ident, ones = sb("ident", P), sb("ones", N)
    cols = sb("cols", 320)
    ada = sb("ada", 3 * 48 + 16)
    small = sb("small", 460)
    banks = [ctx.enter_context(nc.psum_tensor(f"bank{i}", [P, 512], F32)) for i in range(8)]

    hcx = view(hx, 0, P, KD, 2 * N)
    h2 = view(hx, 0, P, KD, N)
    cmpx = view(hx, KD * N, HD, 4, 2, N)
    gates = view(mg, 0, P, KD, 2, N)
    C0, C1, C2 = cols[:, 0:104], cols[:, 104:212], cols[:, 212:308]
    c_bhy, c_bq, c_bk, c_bo, c_bm, c_hyw, c_mlw = (C0[:, i:] for i in (0, 12, 16, 24, 28, 44, 80))
    c_mix, c_ffn, c_mln, c_fin, c_mix2, c_ffn2, c_bada = (C1[:, i:] for i in (0, 8, 16, 20, 28, 44, 60))
    adaX = [ada[:, 48 * i:48 * i + 48] for i in range(3)]
    adaC = ada[:, 144:160]
    gs = small[:, 0:8]
    gsC = small[:, 8:16]
    cT = view(small, 16, P, KD, 32)
    tokc = view(small, 272, P, 3, 2, 2, 4)
    m0c = view(small, 320, P, 4, 2)
    w4 = small[:, 328:460]

    dftc = view(arena, 0, P, 2, 256)
    dfts = view(arena, 512, P, 2, 256)
    idft = view(arena, 1024, P, 4, 256)
    spec = view(arena, 2048, P, 2, 5, HY)
    hyt = view(arena, 7168, P, NC, 3 * HY)
    kq = view(arena, 10240, P, 2, 4, N)
    vx = view(arena, 12288, P, NC, 4, 130)
    cst = view(arena, 13328, P, 4, 2, 130)
    sgo = view(arena, 14368, P, 4, N)
    mask = view(arena, 15392, P, 2, N)
    selh = view(arena, 15904, 4, 4, P)
    wgate = view(arena, 16416, P, KD, 16)
    bgate = arena[0:16, 16544:16545]
    adarow = view(arena, 16548, P, 2, P)
    pre = view(arena, 16804, P, 2, 4, N)
    post = view(arena, 18852, P, 2, 4, N)
    bvrow = arena[0:1, 23992:24504]
    ctxT = view(arena, 16804, P, KD, N)
    cin = view(arena, 18852, P, NC, D)
    xin = view(arena, 20900, P, NC, D)
    r_g = view(arena, 20900, 4, 2, 2 * N)
    r_t = view(arena, 21924, 4, 2, 2 * N)
    r_M = view(arena, 22948, 4, 2, N)
    r_s = view(arena, 23460, 4, 8, 2)
    gate16 = arena[0:16, 23480:23992]
    r_gate = view(scr, 0, 4, 4, 2 * N)
    r_lf = view(scr, 2048, 4, 2, 2 * N)
    r_b = view(scr, 3072, 4, 2, 2 * N)
    kc = view(mg, 0, P, 4, N)
    vc = view(mg, 1024, P, NC, 4, 130)
    kw = view(scr, 0, P, NC, 2, 4, P)
    U = arena[:, 16804:17572]
    Aw = arena[:, 17572:18340]
    ai = view(arena, 18852, P, 2, N)
    qi = view(arena, 19364, P, 2, N)
    hh = view(arena, 19876, P, NC, 4, P)
    Yf = view(scr, 0, P, 4, HY)
    zc = view(scr, 2048, P, NC, HY)
    t1, t2 = scr[:, 3072:3584], scr[:, 3584:4096]
    yaT = view(arena, 10240, P, 4, N)
    dftn = view(arena, 10240, P, 2, 2, 128)
    decay = view(arena, 10752, P, 2, 2, HY)
    zT = arena[0:33, 12800:13056]
    fw1, fw2 = arena[0:33, 13056:13120], arena[0:64, 13120:13184]
    fb = arena[0:64, 13184:13186]
    hid = view(arena, 13200, 64, 4, N)
    fw3 = view(scr, 0, 64, 4, HY)
    hfil = view(mg, 0, P, 2, 4, HY)
    hsd = view(hx, 0, P, 2, 2, 2, HY)
    skips = arena[0:1, 14368:15392]
    tab = view(scr, 2048, P, 4, P)

    stream = []

    def tiles(key, aps):
        stream.extend((f"{key}{i}", ap) for i, ap in enumerate(aps))

    def wide(w, lo, hi):
        return [(w[:, c:min(c + 512, hi)].rearrange("(k p) n -> p k n", p=P), P, KD, min(512, hi - c))
                for c in range(lo, hi, 512)]

    def deep(w, lo, hi):
        return [(w[r:min(r + 512, hi), :].rearrange("(k p) n -> p k n", p=P), P, (min(r + 512, hi) - r) // P, D)
                for r in range(lo, hi, 512)]

    w_in, w_ada = A["w_in"][0], A["w_ada"][0]
    tiles("ada_a", wide(w_ada, 0, 2048))
    tiles("k", wide(w_in, ML0 + 512, ML0 + 1024))
    tiles("v", wide(w_in, ML0 + 1024, ML0 + 1536))
    tiles("q", wide(w_in, ML0, ML0 + 512))
    tiles("hy", wide(w_in, 0, ML0))
    tiles("o", wide(w_in, ML0 + 1536, ML0 + 2048))
    tiles("merge1_", wide(w_in, MERGE0, IN1))
    tiles("ada_b", wide(w_ada, 2048, 6144))
    tiles("branch_hy", deep(A["w_branch_hy"][0], 0, 512))
    tiles("branch_ml", deep(A["w_branch_ml"][0], 0, 512))
    tiles("out1_", wide(A["w_out"][0], 0, D))
    for l in range(LAYERS):
        tiles(f"ada2_{l}", wide(A["w_ada_2"][l], 0, 6144))
    N_PRE = len(stream)
    N_EXP = 12
    after_experts = []

    def tiles2(key, aps):
        after_experts.extend((f"{key}{i}", ap) for i, ap in enumerate(aps))

    for l in range(LAYERS):
        w2 = A["w_in_2"][l]
        tiles2(f"in{l}_", wide(w2, 0, KW0) + [(w2[:, KW0:QB0].rearrange("(k p) n -> p k n", p=P), P, KD, QB0 - KW0)]
               + wide(w2, QB0, MERGE2))
        for n in "kv":
            w = A[f"nsa_cmp_{n}_w1_2"][l].rearrange("(j d) h -> d j h", d=HD)
            tiles2(f"cmp{n}{l}_", [(w, HD, 32, P)])
        tiles2(f"merge2_{l}", wide(w2, MERGE2, IN2))
        tiles2(f"upa{l}_", deep(A["w_up_nsa_2"][l], 0, 512))
        tiles2(f"upb{l}_", deep(A["w_up_moba_2"][l], 0, 512))
        tiles2(f"out2_{l}", wide(A["w_out_2"][l], 0, D))
        wf = A["w_ffn_in_2"][l]
        gt, up = wide(wf, 0, FF2), wide(wf, FF2, 2 * FF2)
        for i in range(len(gt)):
            tiles2(f"gt{l}_{i}_", gt[i:i + 1])
            tiles2(f"up{l}_{i}_", up[i:i + 1])
        tiles2(f"down{l}_", deep(A["w_ffn_out_2"][l], 0, FF2))

    POST0 = N_PRE + EXPERTS * N_EXP
    where = {key: i for i, (key, _) in enumerate(stream)}
    where.update({key: POST0 + i for i, (key, _) in enumerate(after_experts)})

    def slot(n):
        return n % RING

    def tile_sem(n):
        return K.sem(f"tile_slot{slot(n)}")

    def place(n, parts, a, b):
        return view(ring, slot(n) * TILE, parts, a, b)

    def tile(pe, key):
        n = where[key]
        _, parts, a, b = (stream[n] if n < N_PRE else after_experts[n - POST0])[1]
        pe.wait_ge(tile_sem(n), 16 * (n // RING + 1))
        return place(n, parts, a, b)

    block = ctx.enter_context(nc.Block())

    owner = {}

    def claim(pe, b, key):
        if b in owner:
            pe.wait_ge(*at("free " + owner[b]))
        owner[b] = key
        return banks[b]

    turn = {"w": 0}

    def bank(pe, key):
        b = turn["w"] % 6
        turn["w"] += 1
        book.bank[key] = b
        return claim(pe, b, key)

    def bank_of(key):
        return banks[book.bank.get(key, 0)]

    def act_loads(act):
        def load(sem, dst, src):
            act.dma_start(dst, src).then_inc(*K.load(sem))

        def rowload(j, r, src, n):
            load("load_tables", tab[r:r + n, j, :], src.rearrange("(r p) -> r p", p=P))

        load("load_filter", zT, A["k_zT"])
        load("load_filter", fw1, A["hy_f_w1"][0])
        load("load_filter", fw2, A["hy_f_w2"][0])
        load("load_filter", fb[:, 0:1], A["hy_f_b1"][0].rearrange("(p a) -> p a", a=1))
        load("load_filter", fb[:, 1:2], A["hy_f_b2"][0].rearrange("(p a) -> p a", a=1))
        load("load_filter", ident[:, :], A["k_ident"])
        load("load_filter", fw3, A["hy_f_w3"][0].rearrange("k (a n) -> k a n", a=4))
        rowload(3, 0, A["c"][0], 8)
        rowload(3, 8, A["c_ctx"], 8)
        rowload(3, 16, A["c_2"][0], 8)
        b_in = A["b_in"][0]
        rowload(0, 0, b_in[0:3584], 28)
        rowload(0, 28, b_in[MERGE0:IN1], 16)
        load("load_tables", tab[44:80, 0, :], A["hy_conv"][0].rearrange("j (b p) -> (j b) p", p=P))
        load("load_tables", tab[80:104, 0, :], A["ml_conv"][0].rearrange("j (b p) -> (j b) p", p=P))
        rowload(1, 0, A["norm_mix_g"][0], 8)
        rowload(1, 8, A["norm_ffn_g"][0], 8)
        rowload(1, 16, A["ml_norm_g"][0], 4)
        rowload(1, 20, A["final_norm_g"], 8)
        load("load_tables", tab[28:44, 1, :], A["norm_mix_2"].rearrange("l (r p) -> (l r) p", p=P))
        load("load_tables", tab[44:60, 1, :], A["norm_ffn_2"].rearrange("l (r p) -> (l r) p", p=P))
        rowload(1, 60, A["b_ada"][0], 48)
        load("load_tables", tab[0:96, 2, :], A["b_ada_2"].rearrange("l (r p) -> (l r) p", p=P))
        load("load_dft", decay, A["k_decay"])
        load("load_dft", skips, A["hy_skip"].rearrange("a o n -> a (o n)"))
        load("load_dft", dftc, A["k_dftc"])
        load("load_dft", dfts, A["k_dfts"])
        load("load_dft", dftn, A["k_dftn"])
        load("load_dft", idft, A["k_idft"])
        load("load_ml", mask, A["k_mask"])
        load("load_ml", selh, A["k_selh"])
        load("load_ml", wgate, A["w_in"][0][:, GATE0:MERGE0].rearrange("(k p) n -> p k n", p=P))
        load("load_ml", bgate, b_in[GATE0:MERGE0].rearrange("(p a) -> p a", a=1))

    def dve_reduce(v, r, x, k, quarter=False):
        TURN = 2 * np.pi
        c1 = 6.28125
        c2 = float(np.float32(round((TURN - c1) * 2 ** 20) / 2 ** 20))
        c3 = TURN - c1 - c2
        v.tensor_scalar(k, x, 1 / TURN, 0.25 if quarter else 0.0, ALU.mult, ALU.add).then_inc(*DV.step())
        v.wait_ge(*DV.last())
        v.tensor_scalar(k, k, 12582912.0, 12582912.0, ALU.add, ALU.subtract).then_inc(*DV.step())
        src = x
        for c in (c1, c2, c3):
            v.wait_ge(*DV.last())
            v.scalar_tensor_tensor(r, k, -c, src, ALU.mult, ALU.add).then_inc(*DV.step())
            src = r
        if quarter:
            v.wait_ge(*DV.last())
            v.tensor_scalar(r, r, np.pi / 2, None, ALU.add).then_inc(*DV.step())
        v.wait_ge(*DV.last())
        return v.tensor_scalar(r, r, 3.1415925, -3.1415925, ALU.min, ALU.max).then_inc(*DV.step())

    def pe_filter(pe):
        PE.stage("filter")
        pe.wait_ge(*K.loaded("load_filter"))
        for i in range(2):
            if i:
                pe.wait_ge(*at("filter sin0"))
            b = bank(pe, f"filter{i}")
            pe.matmul(b[0:64, 0:N], (fw1, fw2)[i], (zT, hid[:, 1, :])[i], start=True, stop=True).then_inc(*PE.step(f"full filter{i}"))
        pe.wait_ge(*at("filter sin1"))
        for c in range(NC):
            for a in range(4):
                key = f"filter h{c}{a}"
                b = bank(pe, key)
                pe.matmul(b[:, :], hid[:, 3, c * P:(c + 1) * P], fw3[:, a, :], start=True, stop=True).then_inc(*PE.step("full " + key))
        for o in range(2):
            for i, (m, sd) in enumerate(((lambda c: dftc[:, c, 0:128], 0), (lambda c: dftc[:, c, 128:256], 0),
                                         (lambda c: dftn[:, c, 0, :], 1), (lambda c: dfts[:, c, 128:256], 1),
                                         (lambda c: dftn[:, c, 1, :], 0))):
                if o == 0 and i == 0:
                    pe.wait_ge(*at("filter sums"))
                key = f"spec{o}{i}"
                b = bank(pe, key)
                for c in range(NC):
                    ins = pe.matmul(b[:, :], m(c), hsd[:, c, o, sd, :], start=c == 0, stop=c == NC - 1)
                ins.then_inc(*PE.step("full " + key))

    def act_filter(act):
        AC.stage("filter")
        for i in range(2):
            act.wait_ge(*at(f"filter reduced{i}"))
            act.activation(hid[:, 2 * i + 1, :], hid[:, 2 * i, :], ACT.Sin).then_inc(*AC.step(f"filter sin{i}"))
        for o in range(2):
            for i in range(5):
                key = f"spec{o}{i}"
                act.wait_ge(*at("full " + key))
                b = bank_of(key)
                act.copy(spec[:, o, i, :], b[:, :]).then_inc(*AC.step("free " + key, "spectra"))

    def dve_filter(v):
        DV.stage("filter")
        v.memset(ones[:, :], 1.0).then_inc(*DV.step("ones"))
        v.wait_ge(*K.loaded("load_filter"))
        for i in range(2):
            v.wait_ge(*at(f"full filter{i}"))
            b = bank_of(f"filter{i}")
            x = hid[:, 2 * i, :]
            v.tensor_scalar(x, b[0:64, 0:N], fb[:, i:i + 1], None, ALU.add).then_inc(*DV.step(f"free filter{i}"))
            v.wait_ge(*DV.last())
            dve_reduce_into(v, x, i)
        v.wait_ge(*K.loaded("load_dft"))
        for c in range(NC):
            for a in range(4):
                key = f"filter h{c}{a}"
                v.wait_ge(*at("full " + key))
                b = bank_of(key)
                v.tensor_tensor(hfil[:, c, a, :], b[:, :], decay[:, c, a % 2, :], ALU.mult).then_inc(*DV.step("free " + key))
        v.wait_ge(*DV.last())
        for c in range(NC):
            for o in range(2):
                v.tensor_tensor(hsd[:, c, o, 0, :], hfil[:, c, 2 * o, :], hfil[:, c, 2 * o + 1, :], ALU.add).then_inc(*DV.step())
                v.tensor_tensor(hsd[:, c, o, 1, :], hfil[:, c, 2 * o, :], hfil[:, c, 2 * o + 1, :],
                                          ALU.subtract).then_inc(*DV.step())
        v.wait_ge(*DV.last())
        for o in range(2):
            v.tensor_tensor(hsd[0:1, 0, o, 0, :], hsd[0:1, 0, o, 0, :], skips[:, o * HY:(o + 1) * HY],
                                      ALU.add).then_inc(*DV.step("filter sums"))

    def dve_reduce_into(v, x, i):
        k = w_k
        ins = dve_reduce(v, x, x, k)
        book.where[f"filter reduced{i}"] = DV.now

    w_k = hfil[0:64, 0, 0, 0:N]

    def pe_tables(pe):
        PE.stage("tables")
        pe.wait_ge(*K.loaded("load_tables"))
        pe.wait_ge(*at("silu c"))
        b = bank(pe, "tables")
        for j, n in enumerate((104, 108, 96)):
            pe.transpose(b[:, (0, 104, 212)[j]:(0, 104, 212)[j] + n], tab[0:n, j, :], ident[0:n, 0:n])
        pe.transpose(b[:, 320:344], tab[0:24, 3, :], ident[0:24, 0:24]).then_inc(*PE.step("full tables"))

    def act_tables(act):
        AC.stage("tables")
        act.wait_ge(*K.loaded("load_tables"))
        act.activation(tab[0:24, 3, :], tab[0:24, 3, :], ACT.Silu).then_inc(*AC.step("silu c"))

    def dve_tables(v):
        DV.stage("tables")
        v.memset(cT, 0.0).then_inc(*DV.step())
        v.wait_ge(*at("full tables"))
        b = bank_of("tables")
        v.wait_ge(*DV.last())
        v.tensor_copy(cT[:, :, 0:3], b[:, 320:344].rearrange("p (m k) -> p k m", m=3)).then_inc(*DV.step("c columns"))
        v.tensor_copy(cols[:, 0:308], b[:, 0:308]).then_inc(*DV.step("free tables", "columns"))

    def pe_ada(pe, name, key, tile0, n):
        PE.stage("ada")
        pe.wait_ge(*at("c columns"))
        for t in range(n):
            w = tile(pe, f"{key}{t}")
            b = bank(pe, f"{name} row{tile0 + t}")
            for k in range(KD):
                for j in range(4):
                    ins = pe.matmul(b[32 * j:32 * j + 32, 0:P], cT[:, k, :], w[:, k, j * P:(j + 1) * P],
                                        start=k == 0, stop=k == KD - 1)
            ins.then_inc(*PE.step(f"full {name} row{tile0 + t}"))
            mark_used(pe, f"{key}{t}")
            if t:
                ada_turn(pe, name, tile0 + t - 1)
        ada_turn(pe, name, tile0 + n - 1)

    def ada_turn(pe, name, t):
        pe.wait_ge(*at(f"{name} rows{t}"))
        b = bank(pe, f"{name} col{t}")
        pe.transpose(b[:, 0:P], adarow[:, t % 2, :], ident[:, :]).then_inc(*PE.step(f"full {name} col{t}"))


    ada_cols = []

    def act_ada(act, name, tile0, n):
        AC.stage("ada")
        for t in range(tile0, tile0 + n):
            act.wait_ge(*at(f"full {name} row{t}"))
            b = bank_of(f"{name} row{t}")
            if len(ada_cols) >= 2:
                act.wait_ge(*at(ada_cols[-2]))
            ada_cols.append(f"full {name} col{t}")
            act.copy(adarow[:, t % 2, :], b[:, 0:P]).then_inc(*AC.step(f"free {name} row{t}", f"{name} rows{t}"))

    def dve_ada(v, name, tile0, n, outs, bias):
        DV.stage("ada")
        v.wait_ge(*at("columns"))
        for t in range(tile0, tile0 + n):
            v.wait_ge(*at(f"full {name} col{t}"))
            b = bank_of(f"{name} col{t}")
            c = b[:, 0:P].rearrange("p (j m) -> p m j", j=4)
            for m, dst in outs:
                v.tensor_tensor(dst[:, 4 * t:4 * t + 4], c[:, m, :], bias[:, 4 * t:4 * t + 4], ALU.add).then_inc(*DV.step(f"free {name} col{t}", name))

    def mark_used(pe, key):
        book.where[f"used {where[key]}"] = PE.now

    def pe_turn_in(pe, key, src, dst):
        PE.stage("turn")
        pe.wait_ge(*K.loaded("load_x"))
        for kk in range(KD // 2):
            b = bank(pe, f"{key}{kk}")
            for i in range(2):
                for c in range(NC):
                    o = (i * NC + c) * P
                    ins = pe.transpose(b[:, o:o + P], src[:, c, (2 * kk + i) * P:(2 * kk + i + 1) * P], ident[:, :])
            ins.then_inc(*PE.step(f"full {key}{kk}"))

    def act_turn_in(act, key, dst):
        AC.stage("turn")
        for kk in range(KD // 2):
            act.wait_ge(*at(f"full {key}{kk}"))
            b = bank_of(f"{key}{kk}")
            act.copy(dst[:, 2 * kk:2 * kk + 2, :], b[:, :].rearrange("p (a b) -> p a b", a=2)).then_inc(*AC.step(f"free {key}{kk}", f"{key} in"))

    def norm(key, src, n, dst, gain, shift, ready, sq):
        def pe_norm(pe):
            PE.stage("norm")
            pe.wait_ge(*at("ones"))
            b = bank(pe, key)
            pe.wait_ge(*at(key + " squares"))
            for k in range(KD):
                ins = pe.matmul(b[:, 0:n], ones[:, 0:P], sq[:, k, :], start=k == 0, stop=k == KD - 1)
            ins.then_inc(*PE.step("full " + key))

        def act_norm(act):
            AC.stage("norm")
            for step in ready:
                act.wait_ge(*at(step))
            act.activation(sq, src, ACT.Square).then_inc(*AC.step(key + " squares"))
            act.wait_ge(*at(key + " mean"))
            act.activation(rs[:, 0:n], rs[:, 0:n], ACT.Sqrt).then_inc(*AC.step(key + " root"))

        def dve_norm(v):
            DV.stage("norm")
            v.wait_ge(*at("full " + key))
            b = bank_of(key)
            v.tensor_scalar(rs[:, 0:n], b[:, 0:n], 1.0 / D, EPS, ALU.mult, ALU.add).then_inc(*DV.step("free " + key, key + " mean"))
            v.wait_ge(*at(key + " root"))
            v.reciprocal(rs[:, 0:n], rs[:, 0:n]).then_inc(*DV.step())
            v.wait_ge(*DV.last())
            for step in ready:
                v.wait_ge(*at(step))
            for k in range(KD):
                v.scalar_tensor_tensor(sq[:, k, :], src[:, k, :], gain[:, k:k + 1], rs[:, 0:n],
                                                 ALU.mult, ALU.mult).then_inc(*DV.step())
            v.wait_ge(*DV.last())
            for k in range(KD):
                if shift is None:
                    v.tensor_copy(dst[:, k, :], sq[:, k, :]).then_inc(*DV.step(key + " done"))
                else:
                    v.tensor_scalar(dst[:, k, :], sq[:, k, :], shift[:, k:k + 1], None, ALU.add).then_inc(*DV.step(key + " done"))
        return pe_norm, act_norm, dve_norm

    rs = sb("rs", N)

    def pe_linear_T(pe, key, tkey, h, n, blocks=4):
        w = tile(pe, tkey)
        per = 512 // n
        for j in range(blocks):
            if j % per == 0:
                b = bank(pe, f"{key}{j // per}")
            o = (j % per) * n
            for k in range(KD):
                ins = pe.matmul(b[:, o:o + n], w[:, k, j * P:(j + 1) * P], h[:, k, :], start=k == 0, stop=k == KD - 1)
            if j % per == per - 1 or j == blocks - 1:
                ins.then_inc(*PE.step(f"full {key}{j // per}"))
        mark_used(pe, tkey)

    def pe_linear_tok(pe, key, tkey, h, off, bias=None):
        w = tile(pe, tkey)
        for c in range(NC):
            b = bank(pe, f"{key}{c}")
            n = w.shape[2]
            for k in range(KD):
                ins = pe.matmul(b[:, 0:n], h[:, k, off + c * P:off + (c + 1) * P], w[:, k, :], start=k == 0,
                                    stop=k == KD - 1 and bias is None)
            if bias is not None:
                ins = pe.matmul(b[:, 0:n], ones[0:1, 0:P], bias, start=False, stop=True)
            ins.then_inc(*PE.step(f"full {key}{c}"))
        mark_used(pe, tkey)

    CONV = [("k", 0, c_bk, c_mlw[:, 4:], 8, N), ("k", 1, c_bk, c_mlw[:, 4:], 8, 64),
            ("q", 1, c_bq, c_mlw, 8, 64)] + [(f"hy{t}_", 1, c_bhy[:, 4 * t:], c_hyw[:, 4 * t:], 12, 64) for t in range(3)]

    def pe_project(pe):
        PE.stage("project")
        pe.wait_ge(*K.loaded("load_ml"))
        pe.wait_ge(*at("hc done"))
        pe.wait_ge(*at("hx done"))
        pe_linear_T(pe, "k", "k0", hcx, 512)
        w = tile(pe, "v0")
        for s in range(2):
            for c in range(NC):
                b = bank(pe, f"v{s}{c}")
                for k in range(KD):
                    pe.matmul(b[:, :], hcx[:, k, s * N + c * P:s * N + (c + 1) * P], w[:, k, :], start=k == 0,
                                  stop=False)
                pe.matmul(b[:, :], ones[0:1, 0:P], bvrow, start=False, stop=True).then_inc(*PE.step(f"full v{s}{c}"))
        mark_used(pe, "v0")
        b = bank(pe, "gates")
        for k in range(KD):
            ins = pe.matmul(b[0:16, :], wgate[:, k, :], hcx[:, k, :], start=k == 0, stop=k == KD - 1)
        ins.then_inc(*PE.step("full gates"))
        pe.wait_ge(*at("gates16"))
        for g in range(4):
            b = bank(pe, f"gate{g}")
            pe.matmul(b[0:4, :], ident[0:16, 4 * g:4 * g + 4], gate16, start=True, stop=True).then_inc(*PE.step(f"full gate{g}"))
        x = hcx[:, :, N:2 * N]
        pe_linear_T(pe, "q", "q0", x, N)
        pe_linear_T(pe, "hy0_", "hy0", x, N)
        pe_linear_T(pe, "hy1_", "hy1", x, N)
        pe_context(pe)
        pe_hy_turn(pe, 0)
        pe_linear_T(pe, "hy2_", "hy2", x, N)
        pe_hy_turn(pe, 1)
        pe_linear_T(pe, "o", "o0", x, N)
        pe_hy_turn(pe, 2)
        for t in range(4):
            pe_linear_T(pe, f"mergeA{t}_", f"merge1_{t}", x, N)

    def act_conv(act, i):
        key, s, bias, _, _, _ = CONV[i]
        if i >= 2:
            act.wait_ge(*at(f"conv{i - 2}"))
        for j in range(4):
            if key == "k":
                act.wait_ge(*at(f"full k{j}"))
                b, o, bk = bank_of(f"k{j}"), s * N, f"k{j}"
            else:
                bk = f"{key}{j // 2}"
                act.wait_ge(*at("full " + bk))
                b, o = bank_of(bk), (j % 2) * N
            act.activation(pre[:, i % 2, j, :], b[:, o:o + N], ACT.Identity, bias=bias[:, j:j + 1]).then_inc(*AC.step(f"pre{i}", "free " + bk))

    def dve_conv(v, i):
        _, _, _, w, pitch, L = CONV[i]
        v.wait_ge(*at(f"pre{i}"))
        if i >= 2:
            v.wait_ge(*at(f"conv read{i - 2}"))
        p = [pre[:, i % 2, j, :].rearrange("p (r l) -> p r l", l=L) for j in range(4)]
        y = [post[:, i % 2, j, :].rearrange("p (r l) -> p r l", l=L) for j in range(4)]
        for j in range(4):
            v.tensor_scalar(post[:, i % 2, j, :], pre[:, i % 2, j, :], w[:, pitch + j:pitch + j + 1], None,
                                      ALU.mult).then_inc(*DV.step())
        v.wait_ge(*DV.last())
        for j in range(4):
            v.scalar_tensor_tensor(y[j][:, :, 1:L], p[j][:, :, 0:L - 1], w[:, j:j + 1], y[j][:, :, 1:L],
                                             ALU.mult, ALU.add).then_inc(*DV.step())
        v.wait_ge(*DV.last())
        for j in range(4):
            v.scalar_tensor_tensor(y[j][:, :, 0:L - 1], p[j][:, :, 1:L],
                                             w[:, 2 * pitch + j:2 * pitch + j + 1], y[j][:, :, 0:L - 1],
                                             ALU.mult, ALU.add).then_inc(*DV.step(f"conv{i}"))

    def act_conv_out(act, i):
        act.wait_ge(*at(f"conv{i}"))
        dst = (kc, kq[:, 0], kq[:, 1])[i]
        act.activation(dst, post[:, i % 2], ACT.Silu).then_inc(*AC.step(f"conv read{i}", ("kc", "k ready", "q ready")[i]))

    def pe_hy_turn(pe, t):
        pe.wait_ge(*at(f"conv{3 + t}"))
        for jj in range(2):
            b = bank(pe, f"hyturn{t}{jj}")
            for c in range(NC):
                for j in range(2):
                    o = (c * 2 + j) * P
                    ins = pe.transpose(b[:, o:o + P], post[:, (3 + t) % 2, 2 * jj + j, c * P:(c + 1) * P], ident[:, :])
            ins.then_inc(*PE.step(f"full hyturn{t}{jj}"))
        book.where[f"conv read{3 + t}"] = PE.now

    def act_hy_turn(act, t):
        for jj in range(2):
            key = f"hyturn{t}{jj}"
            act.wait_ge(*at("full " + key))
            b = bank_of(key)
            act.copy(hyt[:, :, t * HY + jj * 256:t * HY + jj * 256 + 256],
                                 b[:, :].rearrange("p (c n) -> p c n", c=NC)).then_inc(*AC.step("free " + key, "hyena parts"))

    def act_project(act):
        AC.stage("project")
        act.wait_ge(*at("columns"))
        act.wait_ge(*at("hc done"))
        act.wait_ge(*at("hx done"))
        act.wait_ge(*K.loaded("load_ml"))
        act_conv(act, 0)
        act_conv(act, 1)
        for s in range(2):
            for c in range(NC):
                act.wait_ge(*at(f"full v{s}{c}"))
                b = bank_of(f"v{s}{c}")
                act.copy((vc, vx)[s][:, c, :, 0:P], b[:, :].rearrange("p (h e) -> p h e", h=4)).then_inc(*AC.step(f"free v{s}{c}", f"v ready{s}"))
        act.wait_ge(*at("full gates"))
        b = bank_of("gates")
        act.activation(gate16, b[0:16, :], ACT.Identity, bias=bgate).then_inc(*AC.step("free gates", "gates16"))
        for g in range(4):
            act.wait_ge(*at(f"full gate{g}"))
            b = bank_of(f"gate{g}")
            act.copy(r_gate[:, g, :], b[0:4, :]).then_inc(*AC.step(f"free gate{g}", "gate rows"))
        act_conv_out(act, 0)
        act_rows(act)
        act_conv(act, 2)
        act_conv_out(act, 1)
        act_conv(act, 3)
        act_conv_out(act, 2)
        act_conv(act, 4)
        act_context(act)
        act_hy_turn(act, 0)
        act_conv(act, 5)
        act_hy_turn(act, 1)
        for i in range(2):
            act.wait_ge(*at(f"full o{i}"))
            b = bank_of(f"o{i}")
            for j in range(2):
                act.activation(sgo[:, 2 * i + j, :], b[:, j * N:(j + 1) * N], ACT.Sigmoid,
                                           bias=c_bo[:, 2 * i + j:2 * i + j + 1]).then_inc(*AC.step(f"free o{i}", "o ready"))
        act_hy_turn(act, 2)
        act.wait_ge(*at("context done"))
        for t in range(4):
            for i in range(2):
                act.wait_ge(*at(f"full mergeA{t}_{i}"))
                b = bank_of(f"mergeA{t}_{i}")
                for j in range(2):
                    blk = 4 * t + 2 * i + j
                    act.activation(gates[:, blk % KD, blk // KD, :], b[:, j * N:(j + 1) * N], ACT.Sigmoid,
                                               bias=c_bm[:, blk:blk + 1]).then_inc(*AC.step(f"free mergeA{t}_{i}", "gates0"))

    def dve_project(v):
        DV.stage("project")
        v.wait_ge(*at("columns"))
        v.memset(vx[:, :, :, P:P + 1], 1.0).then_inc(*DV.step())
        v.memset(vc[:, :, :, P:P + 1], 1.0).then_inc(*DV.step())
        v.memset(r_s[:, 7, :], 0.0).then_inc(*DV.step("v ones"))
        dve_conv(v, 0)
        dve_conv(v, 1)
        dve_rows(v)
        dve_conv(v, 2)
        dve_conv(v, 3)
        dve_context(v)
        dve_conv(v, 4)
        dve_conv(v, 5)

    def back(ap, d):
        return ap[:, ::-1] if d else ap

    def act_rows(act):
        act.wait_ge(*at("rows 1"))
        act.activation(r_t, r_t, ACT.Exp, scale=-1.0).then_inc(*AC.step("rows 2"))
        act.wait_ge(*at("rows 3"))
        act.activation(r_t, r_t, ACT.Ln).then_inc(*AC.step("rows 4"))
        act.wait_ge(*at("rows 5"))
        act.activation(r_t[:, :, 0:N], r_t[:, :, 0:N], ACT.Exp).then_inc(*AC.step())
        act.activation(r_t[:, :, N:2 * N], r_t[:, :, N:2 * N], ACT.Exp, scale=-1.0).then_inc(*AC.step("rows 6"))

    def dve_rows(v):
        f = r_gate[:, 1::2, :]
        v.wait_ge(*at("gate rows"))
        v.scalar_tensor_tensor(r_t, f, -1.0, f, ALU.mult, ALU.max).then_inc(*DV.step("rows 1"))
        v.wait_ge(*at("rows 2"))
        v.tensor_scalar(r_t, r_t, 1.0, None, ALU.add).then_inc(*DV.step("rows 3"))
        v.wait_ge(*at("rows 4"))
        v.scalar_tensor_tensor(r_lf, f, 0.0, r_t, ALU.min, ALU.subtract).then_inc(*DV.step())
        v.wait_ge(*DV.last())
        for s in range(2):
            for d in range(2):
                v.tensor_tensor_scan(back(r_b[:, d, s * N:(s + 1) * N], d), oner,
                                               back(r_lf[:, d, s * N:(s + 1) * N], d), 0.0, ALU.mult, ALU.add).then_inc(*DV.step())
        v.wait_ge(*DV.last())
        v.tensor_tensor(r_g, r_gate[:, 0::2, :], r_b, ALU.subtract).then_inc(*DV.step())
        v.wait_ge(*DV.last())
        v.tensor_reduce(r_s[:, 0, :], r_g[:, :, 0:N], AX, ALU.max).then_inc(*DV.step())
        v.wait_ge(*DV.last())
        v.tensor_scalar(r_s[:, 0, :], r_s[:, 0, :], 0.0, None, ALU.max).then_inc(*DV.step())
        v.wait_ge(*DV.last())
        for d in range(2):
            e = 0 if d else N - 1
            v.tensor_tensor(r_s[:, 1, d:d + 1], r_s[:, 0, d:d + 1], r_b[:, d, e:e + 1], ALU.add).then_inc(*DV.step())
            v.tensor_scalar(r_t[:, d, 0:N], r_g[:, d, 0:N], r_s[:, 0, d:d + 1], None, ALU.subtract).then_inc(*DV.step())
        v.wait_ge(*DV.last())
        for d in range(2):
            v.tensor_tensor_scan(back(r_M[:, d, :], d), oner, back(r_g[:, d, N:2 * N], d),
                                           r_s[:, 1, d:d + 1], ALU.mult, ALU.max).then_inc(*DV.step())
        v.wait_ge(*DV.last())
        v.tensor_tensor(r_t[:, :, N:2 * N], r_M, r_b[:, :, N:2 * N], ALU.add).then_inc(*DV.step("rows 5"))
        v.wait_ge(*at("full tokc"))
        b = bank_of("tokc")
        v.tensor_copy(small[:, 272:328], b[:, 0:56]).then_inc(*DV.step("free tokc", "tokc"))

    oner = ones[0:4, :]

    def pe_context(pe):
        pe.wait_ge(*at("rows 6"))
        b = bank(pe, "tokc")
        for kind, r in enumerate((r_t[:, :, 0:N], r_g[:, :, N:2 * N], r_t[:, :, N:2 * N])):
            for c in range(NC):
                for d in range(2):
                    o = ((kind * 2 + c) * 2 + d) * 4
                    pe.transpose(b[:, o:o + 4], r[:, d, c * P:(c + 1) * P], ident[0:4, 0:4])
        for h in range(4):
            ins = pe.matmul(b[:, 48 + 2 * h:50 + 2 * h], selh[:, h, :], r_s[:, 1, :], start=True, stop=True)
        ins.then_inc(*PE.step("full tokc"))
        pe.wait_ge(*at("kc"))
        for c in range(NC):
            b = bank(pe, f"kturn{c}")
            for h in range(4):
                ins = pe.transpose(b[:, h * P:(h + 1) * P], kc[:, h, c * P:(c + 1) * P], ident[:, :])
            ins.then_inc(*PE.step(f"full kturn{c}"))
        pe.wait_ge(*at("kw"))
        pe.wait_ge(*at("v ready0"))
        pe.wait_ge(*at("v ones"))
        for h in range(4):
            b = bank(pe, f"state{h}")
            for d in range(2):
                for c in range(NC):
                    ins = pe.matmul(b[:, d * 130:d * 130 + 129], kw[:, c, d, h, :], vc[:, c, h, 0:129], start=c == 0,
                                        stop=c == NC - 1)
            ins.then_inc(*PE.step(f"full state{h}"))

    def act_context(act):
        for h in range(4):
            act.wait_ge(*at(f"full state{h}"))
            b = bank_of(f"state{h}")
            act.copy(cst[:, h, :, 0:129], b[:, 0:260].rearrange("p (d e) -> p d e", d=2)[:, :, 0:129]).then_inc(*AC.step(f"free state{h}", "context done"))

    def dve_context(v):
        for c in range(NC):
            v.wait_ge(*at(f"full kturn{c}"))
            b = bank_of(f"kturn{c}")
            for d in range(2):
                v.tensor_tensor(kw[:, c, d], b[:, :].rearrange("p (h e) -> p h e", h=4),
                                          spread(tokc[:, 0, c, d, :], 2, P), ALU.mult).then_inc(*DV.step(f"free kturn{c}", "kw"))

    def pe_mlstm(pe):
        PE.stage("mlstm")
        pe.wait_ge(*at("k ready"))
        pe.wait_ge(*at("q ready"))
        pe.wait_ge(*at("tokc"))
        pe.wait_ge(*at("v ready1"))
        pe.wait_ge(*at("context done"))
        for h in range(4):
            bm = bank(pe, f"Mb{h}")
            pe.matmul(bm[:, :], selh[:, h, :], r_M.rearrange("p d t -> p (d t)"), start=True, stop=True).then_inc(*PE.step(f"full Mb{h}"))
            bs = bank(pe, f"S{h}")
            for c in range(NC):
                ins = pe.matmul(bs[:, c * N:(c + 1) * N], kq[:, 0, h, c * P:(c + 1) * P], kq[:, 1, h, :], start=True,
                                    stop=True)
            ins.then_inc(*PE.step(f"full S{h}"))
            if h:
                pe_mlstm_num(pe, h - 1)
        pe_mlstm_num(pe, 3)
        pe.wait_ge(*at("mlstm normed"))
        for c in range(NC):
            b = bank(pe, f"mturn{c}")
            for h in range(4):
                ins = pe.transpose(b[:, h * P:(h + 1) * P], hh[:, c, h, :], ident[:, :])
            ins.then_inc(*PE.step(f"full mturn{c}"))

    def pe_mlstm_num(pe, h):
        pe.wait_ge(*at(f"A{h}"))
        pe.wait_ge(*at(f"qi{h}"))
        F0, F1, B0, B1 = Aw[:, 0:256], Aw[:, 256:384], Aw[:, 384:512], Aw[:, 512:768]
        for c in range(NC):
            key = f"num{h}{c}"
            b = bank(pe, key)
            parts = ([[(F0[:, 0:P], 0)], [(B0, 0), (B1[:, 0:P], 1)]], [[(F0[:, P:N], 0), (F1, 1)], [(B1[:, P:N], 1)]])[c]
            for d in range(2):
                o = b[:, d * 130:d * 130 + 129]
                for n, (a, s) in enumerate(parts[d]):
                    pe.matmul(o, a, vx[:, s, h, 0:129], start=n == 0, stop=False)
                ins = pe.matmul(o, qi[:, d, c * P:(c + 1) * P], cst[:, h, d, 0:129], start=False, stop=True)
            ins.then_inc(*PE.step("full " + key))

    def act_mlstm(act):
        AC.stage("mlstm")
        act.wait_ge(*at("tokc"))
        for h in range(4):
            act.wait_ge(*at(f"full Mb{h}"))
            b = bank_of(f"Mb{h}")
            if h:
                act.wait_ge(*at(f"qi{h - 1}"))
            act.wait_ge(*at(f"U{h}"))
            act.activation(U, U, ACT.Exp, scale=-1.0).then_inc(*AC.step(f"E{h}"))
            for d in range(2):
                act.activation(ai[:, d, :], b[:, d * N:(d + 1) * N], ACT.Exp, bias=m0c[:, h, d:d + 1],
                                           scale=-1.0).then_inc(*AC.step(f"ai{h}", f"free Mb{h}"))
        act.wait_ge(*at("mlstm mean"))
        act.activation(w4[:, 0:8], w4[:, 0:8], ACT.Sqrt).then_inc(*AC.step("mlstm root"))

    def dve_mlstm(v):
        DV.stage("mlstm")
        v.wait_ge(*at("tokc"))
        v.wait_ge(*at("conv read5"))
        for h in range(4):
            v.wait_ge(*at(f"full Mb{h}"))
            b = bank_of(f"Mb{h}")
            if h:
                v.wait_ge(*at(f"full num{h - 1}1"))
            g = tokc[:, 1]
            for (lo, hi, d, s, t0, t1) in ((0, 256, 0, 0, 0, 256), (256, 384, 0, 1, 128, 256), (384, 512, 1, 0, 0, 128),
                                           (512, 768, 1, 1, 0, 256)):
                m = mask[:, d, 0:256] if hi - lo == 256 else (mask[:, d, 0:128] if d == 0 else mask[:, d, 128:256])
                v.scalar_tensor_tensor(U[:, lo:hi], b[:, d * N + t0:d * N + t1], g[:, s, d, h:h + 1], m,
                                                 ALU.subtract, ALU.max).then_inc(*DV.step(f"U{h}"))
            v.wait_ge(*at(f"ai{h}"))
            v.scalar_tensor_tensor(qi, ai, DH ** -0.5, spread(kq[:, 1, h, :], 1, 2), ALU.mult, ALU.mult).then_inc(*DV.step(f"qi{h}"))
            v.wait_ge(*at(f"full S{h}"))
            sc = bank_of(f"S{h}")
            v.wait_ge(*at(f"E{h}"))
            for (lo, hi, s, t0, t1) in ((0, 256, 0, 0, 256), (256, 384, 1, 128, 256), (384, 512, 0, 0, 128),
                                        (512, 768, 1, 0, 256)):
                v.scalar_tensor_tensor(Aw[:, lo:hi], sc[:, s * N + t0:s * N + t1], DH ** -0.5, U[:, lo:hi],
                                                 ALU.mult, ALU.mult).then_inc(*DV.step(f"A{h}", f"free S{h}"))
            if h:
                dve_mlstm_out(v, h - 1)
        dve_mlstm_out(v, 3)
        v.wait_ge(*DV.last())
        sq = view(arena, 16804, P, 8, P)
        hf = hh.rearrange("p c h e -> p (c h) e")
        v.tensor_tensor(sq, hf, hf, ALU.mult).then_inc(*DV.step())
        v.wait_ge(*DV.last())
        v.tensor_reduce(w4[:, 0:8], sq, AX, ALU.add).then_inc(*DV.step())
        v.wait_ge(*DV.last())
        v.tensor_scalar(w4[:, 0:8], w4[:, 0:8], 1.0 / DH, EPS, ALU.mult, ALU.add).then_inc(*DV.step("mlstm mean"))
        v.wait_ge(*at("mlstm root"))
        v.reciprocal(w4[:, 0:8], w4[:, 0:8]).then_inc(*DV.step())
        v.wait_ge(*DV.last())
        v.tensor_tensor(hf, hf, spread(w4[:, 0:8], 2, P), ALU.mult).then_inc(*DV.step("mlstm normed"))
        v.wait_ge(*at("o ready"))
        for c in range(NC):
            v.wait_ge(*at(f"full mturn{c}"))
            b = bank_of(f"mturn{c}")
            for h in range(4):
                o = sgo[:, h, c * P:(c + 1) * P]
                v.scalar_tensor_tensor(o, b[:, h * P:(h + 1) * P], c_mln[:, h:h + 1], o, ALU.mult, ALU.mult).then_inc(*DV.step(f"free mturn{c}", "yb0"))

    def dve_mlstm_out(v, h):
        for c in range(NC):
            v.wait_ge(*at(f"full num{h}{c}"))
            b = bank_of(f"num{h}{c}")
            num = b[:, 0:260].rearrange("p (d e) -> p d e", d=2)
            den = w4[:, 16:18]
            v.tensor_copy(w4[:, 20:22].unsqueeze(2), num[:, :, 128:129]).then_inc(*DV.step())
            v.wait_ge(*DV.last())
            v.scalar_tensor_tensor(den, w4[:, 20:22], -1.0, w4[:, 20:22], ALU.mult, ALU.max).then_inc(*DV.step())
            v.wait_ge(*DV.last())
            v.tensor_tensor(den, den, tokc[:, 2, c, :, h], ALU.max).then_inc(*DV.step())
            v.wait_ge(*DV.last())
            v.reciprocal(den, den).then_inc(*DV.step())
            v.wait_ge(*DV.last())
            v.tensor_scalar(hh[:, c, h, :], num[:, 0, 0:P], den[:, 0:1], None, ALU.mult).then_inc(*DV.step())
            v.wait_ge(*DV.last())
            v.scalar_tensor_tensor(hh[:, c, h, :], num[:, 1, 0:P], den[:, 1:2], hh[:, c, h, :], ALU.mult,
                                             ALU.add).then_inc(*DV.step(f"free num{h}{c}"))

    def pe_hyena(pe):
        PE.stage("hyena")
        pe.wait_ge(*at("spectra"))
        for o in range(2):
            pe.wait_ge(*at("hyena parts"))
            for step in (["z1"] if o else []):
                pe.wait_ge(*at(step))
            z = (lambda c: hyt[:, c, 0:HY]) if o == 0 else (lambda c: zc[:, c, :])
            for i in range(4):
                b = bank(pe, f"dft{o}{i}")
                m = (dftc, dftc, dfts, dfts)[i]
                for c in range(NC):
                    ins = pe.matmul(b[:, :], m[:, c, (i % 2) * P:(i % 2 + 1) * P], z(c), start=c == 0, stop=c == 1)
                ins.then_inc(*PE.step(f"full dft{o}{i}"))
            pe.wait_ge(*at(f"product{o}"))
            for c in range(NC):
                b = bank(pe, f"idft{o}{c}")
                for f in range(4):
                    ins = pe.matmul(b[:, :], idft[:, f, c * P:(c + 1) * P], Yf[:, f, :], start=f == 0, stop=f == 3)
                ins.then_inc(*PE.step(f"full idft{o}{c}"))
        pe.wait_ge(*at("z2"))
        for jj in range(2):
            b = bank(pe, f"yturn{jj}")
            for j in range(2):
                for c in range(NC):
                    ins = pe.transpose(b[:, (2 * j + c) * P:(2 * j + c + 1) * P],
                                           zc[:, c, (2 * jj + j) * P:(2 * jj + j + 1) * P], ident[:, :])
            ins.then_inc(*PE.step(f"full yturn{jj}"))

    def act_hyena(act):
        AC.stage("hyena")
        act.wait_ge(*at("full S3"))
        for jj in range(2):
            act.wait_ge(*at(f"full yturn{jj}"))
            b = bank_of(f"yturn{jj}")
            act.copy(yaT[:, 2 * jj:2 * jj + 2, :], b[:, :].rearrange("p (j t) -> p j t", j=2)).then_inc(*AC.step(f"free yturn{jj}", "ya0"))

    def dve_hyena(v):
        DV.stage("hyena")
        v.wait_ge(*at("full state3"))
        v.wait_ge(*at("spectra"))
        for o in range(2):
            k = spec[:, o]
            for f in range(2):
                v.wait_ge(*at(f"full dft{o}{f}"))
                v.wait_ge(*at(f"full dft{o}{2 + f}"))
                br, bi = bank_of(f"dft{o}{f}"), bank_of(f"dft{o}{2 + f}")
                re2 = k[:, 4] if f == 0 else k[:, 1]
                if o and f == 0:
                    v.wait_ge(*at("full idft01"))
                v.tensor_tensor(Yf[:, f, :], br[:, :], k[:, f], ALU.mult).then_inc(*DV.step())
                v.tensor_tensor(t1, bi[:, :], k[:, 2 + f], ALU.mult).then_inc(*DV.step())
                v.tensor_tensor(Yf[:, 2 + f, :], br[:, :], k[:, 2 + f], ALU.mult).then_inc(*DV.step(f"free dft{o}{f}"))
                v.tensor_tensor(t2, bi[:, :], re2, ALU.mult).then_inc(*DV.step(f"free dft{o}{2 + f}"))
                v.wait_ge(*DV.last())
                v.tensor_tensor(Yf[:, f, :], Yf[:, f, :], t1, ALU.subtract).then_inc(*DV.step())
                v.tensor_tensor(Yf[:, 2 + f, :], Yf[:, 2 + f, :], t2, ALU.add).then_inc(*DV.step(f"product{o}"))
                v.wait_ge(*DV.last())
            for c in range(NC):
                v.wait_ge(*at(f"full idft{o}{c}"))
                b = bank_of(f"idft{o}{c}")
                if o and c == 0:
                    v.wait_ge(*at("full dft13"))
                v.tensor_tensor(zc[:, c, :], b[:, :], hyt[:, c, (o + 1) * HY:(o + 2) * HY], ALU.mult).then_inc(*DV.step(f"free idft{o}{c}", f"z{o + 1}"))

    merged = view(hx, KD * N, P, KD, N)

    def mixer_out(p, wa, wb, wo, yb, ga, gate_ready):
        def pe_out(pe):
            PE.stage(f"mix{p}")
            a, b_ = tile(pe, wa), tile(pe, wb)
            pe.wait_ge(*at(f"ya{p}"))
            pe.wait_ge(*at(f"yb{p}"))
            for j in range(KD):
                b = bank(pe, f"merge{p}{j}")
                for s, (w, y) in enumerate(((a, yaT if p == 0 else yT2[:, 0:4]), (b_, yb))):
                    for k in range(4):
                        ins = pe.matmul(b[:, s * N:(s + 1) * N], w[:, k, j * P:(j + 1) * P], y[:, k, :], start=k == 0,
                                            stop=k == 3)
                ins.then_inc(*PE.step(f"full merge{p}{j}"))
            mark_used(pe, wa)
            mark_used(pe, wb)
            pe.wait_ge(*at(f"merged{p}"))
            for t in range(2):
                pe_linear_T(pe, f"mixout{p}{t}", f"{wo}{t}", merged, N)

        def dve_out(v):
            DV.stage(f"mix{p}")
            v.wait_ge(*at(f"gates{p}"))
            for j in range(KD):
                v.wait_ge(*at(f"full merge{p}{j}"))
                b = bank_of(f"merge{p}{j}")
                g = gates[:, j].rearrange("p a b -> p (a b)")
                v.tensor_tensor(g, b[:, :], g, ALU.mult).then_inc(*DV.step(f"free merge{p}{j}"))
                v.wait_ge(*DV.last())
                v.tensor_tensor(merged[:, j, :], gates[:, j, 0, :], gates[:, j, 1, :], ALU.add).then_inc(*DV.step(f"merged{p}"))
            v.wait_ge(*at(gate_ready))
            for t in range(2):
                for i in range(2):
                    key = f"mixout{p}{t}{i}"
                    v.wait_ge(*at("full " + key))
                    b = bank_of(key)
                    for j in range(2):
                        blk = 4 * t + 2 * i + j
                        v.scalar_tensor_tensor(xT[:, blk, :], b[:, j * N:(j + 1) * N], ga[:, 16 + blk:17 + blk],
                                                         xT[:, blk, :], ALU.mult, ALU.add).then_inc(*DV.step("free " + key, f"x mixed{p}"))
        return pe_out, dve_out

    def dve_gain(v, key, dst, gain, scale, *ready):
        v.wait_ge(*at("columns"))
        for step in ready:
            v.wait_ge(*at(step))
        v.scalar_tensor_tensor(dst, scale, 1.0, gain, ALU.add, ALU.mult).then_inc(*DV.step(key))
        v.wait_ge(*DV.last())

    e_wr = view(arena, 0, P, KD, EXPERTS)
    e_iota, e_slot = arena[:, 128:160], arena[:, 160:161]
    e_aff = view(arena, 164, P, NC, EXPERTS)
    e_pos = view(arena, 196, P, NC, EXPERTS)
    e_st = view(arena, 228, P, 3, NC)
    e_work = arena[0:EXPERTS, 236:492]
    e_top = arena[0:EXPERTS, 492:500]
    e_sel = arena[0:EXPERTS, 500:756]
    e_pa = arena[0:EXPERTS, 756:1268]
    e_psel = view(arena, 1268, P, NC, EXPERTS * CAP)
    e_htok = view(arena, 2292, P, NC, D)
    e_xg = view(arena, 4340, P, KD, EXPERTS * CAP)
    e_xe = view(arena, 8436, P, KD, CAP)
    e_row = arena[0:EXPERTS, 8692:9204]
    e_t = arena[:, 9204:9460]
    e_G = arena[:, 9460:9716]
    e_h = arena[:, 9716:10228]
    e_hT = view(arena, 10228, P, 4, P)
    e_y = arena[:, 10740:11764]

    def act_moe_loads(act):
        act.wait_ge(*at("x mixed0"))
        act.wait_ge(*at("full yturn1"))
        act.wait_ge(*at("ya0"))
        for dst, src in ((e_wr, A["w_router"][0].rearrange("(k p) n -> p k n", p=P)), (e_iota, A["k_iota"]),
                         (e_slot, A["k_slot"])):
            act.dma_start(dst, src).then_inc(*K.load("load_moe"))

    def pe_route(pe):
        PE.stage("route")
        pe.wait_ge(*K.loaded("load_moe"))
        pe.wait_ge(*at("h ffn0 done"))
        b = bank(pe, "logits")
        for c in range(NC):
            for k in range(KD):
                ins = pe.matmul(b[:, c * 16:(c + 1) * 16], h2[:, k, c * P:(c + 1) * P], e_wr[:, k, :], start=k == 0,
                                    stop=k == KD - 1)
        ins.then_inc(*PE.step("full logits"))
        for c in range(NC):
            for i in range(2):
                b = bank(pe, f"htok{c}{i}")
                for j in range(4):
                    ins = pe.transpose(b[:, j * P:(j + 1) * P], h2[:, 4 * i + j, c * P:(c + 1) * P], ident[:, :])
                ins.then_inc(*PE.step(f"full htok{c}{i}"))
        pe.wait_ge(*at("affinity"))
        b = bank(pe, "affT")
        for c in range(NC):
            ins = pe.transpose(b[0:EXPERTS, c * P:(c + 1) * P], e_aff[:, c, :], ident[:, :])
        ins.then_inc(*PE.step("full affT"))
        pe.wait_ge(*at("slots"))
        b = bank(pe, "postok")
        for c in range(NC):
            ins = pe.transpose(b[:, c * 16:(c + 1) * 16], e_pa[:, c * P:(c + 1) * P], ident[0:16, 0:16])
        ins.then_inc(*PE.step("full postok"))
        pe.wait_ge(*at("one-hot"))
        pe.wait_ge(*at("h tokens"))
        for k in range(KD):
            b = bank(pe, f"gather{k}")
            for c in range(NC):
                ins = pe.matmul(b[:, :], e_htok[:, c, k * P:(k + 1) * P], e_psel[:, c, :], start=c == 0, stop=c == 1)
            ins.then_inc(*PE.step(f"full gather{k}"))

    def act_route(act):
        AC.stage("route")
        act.wait_ge(*at("logit max"))
        act.wait_ge(*at("full logits"))
        b = bank_of("logits")
        for c in range(NC):
            act.activation(e_aff[:, c, :], b[:, c * 16:(c + 1) * 16], ACT.Exp, bias=e_st[:, 0, c:c + 1],
                                       accum_out=e_st[:, 1, c:c + 1]).then_inc(*AC.step("free logits", "exp logits"))
        for c in range(NC):
            for i in range(2):
                act.wait_ge(*at(f"full htok{c}{i}"))
                b = bank_of(f"htok{c}{i}")
                act.copy(e_htok[:, c, 512 * i:512 * i + 512], b[:, :]).then_inc(*AC.step(f"free htok{c}{i}", "h tokens"))
        for k in range(KD):
            act.wait_ge(*at(f"full gather{k}"))
            b = bank_of(f"gather{k}")
            act.copy(e_xg[:, k, :], b[:, :]).then_inc(*AC.step(f"free gather{k}", "gathered"))

    def dve_route(v):
        DV.stage("route")
        v.wait_ge(*at("full logits"))
        b = bank_of("logits")
        v.tensor_reduce(e_st[:, 0, :], b[:, 0:32].rearrange("p (c e) -> p c e", c=NC), AX, ALU.max,
                                  negate=True).then_inc(*DV.step("logit max"))
        v.wait_ge(*at("exp logits"))
        v.reciprocal(e_st[:, 2, :], e_st[:, 1, :]).then_inc(*DV.step())
        v.wait_ge(*DV.last())
        v.tensor_tensor(e_aff, e_aff, spread(e_st[:, 2, :], 2, EXPERTS), ALU.mult).then_inc(*DV.step("affinity"))
        v.wait_ge(*at("full affT"))
        b = bank_of("affT")
        v.tensor_copy(e_pa[:, N:2 * N], b[0:EXPERTS, 0:N]).then_inc(*DV.step())
        v.tensor_copy(e_work, b[0:EXPERTS, 0:N]).then_inc(*DV.step("free affT"))
        for _ in range(CAP // 8):
            v.wait_ge(*DV.last())
            v.max(e_top, e_work).then_inc(*DV.step())
            v.wait_ge(*DV.last())
            v.match_replace(e_work, e_top, e_work, -1.0).then_inc(*DV.step())
        v.wait_ge(*DV.last())
        v.tensor_scalar(e_sel, e_work, 0.0, None, ALU.is_lt).then_inc(*DV.step())
        v.wait_ge(*DV.last())
        v.tensor_tensor_scan(e_work, oner16, e_sel, 0.0, ALU.mult, ALU.add).then_inc(*DV.step())
        v.wait_ge(*DV.last())
        v.tensor_tensor(e_work, e_work, e_sel, ALU.mult).then_inc(*DV.step())
        v.wait_ge(*DV.last())
        v.tensor_scalar(e_pa[:, 0:N], e_work, 1.0, None, ALU.subtract).then_inc(*DV.step("slots"))
        v.wait_ge(*K.loaded("load_moe"))
        v.wait_ge(*at("full postok"))
        b = bank_of("postok")
        v.tensor_copy(e_pos, b[:, 0:32].rearrange("p (c e) -> p c e", c=NC)).then_inc(*DV.step("free postok"))
        v.wait_ge(*DV.last())
        for c in range(NC):
            v.tensor_tensor(e_psel[:, c, :].rearrange("p (e s) -> p e s", s=CAP), spread(e_iota, 1, EXPERTS),
                                      spread(e_pos[:, c, :], 2, CAP), ALU.is_equal).then_inc(*DV.step("one-hot"))
        v.memset(e_y, 0.0).then_inc(*DV.step("y zero"))

    oner16 = ones[0:16, :]

    def loop(eng, Q, body):
        Q.stage("expert")
        eng.sem_inc(K.sem(Q.cur), book.per.get(Q.cur, 1))
        with eng.Fori(0, EXPERTS) as i:
            K.turn = i
            body(i)
        K.turn = None
        book.per[Q.cur] = Q.count[Q.cur]

    def pe_experts(pe):
        PE.stage("route")
        pe.wait_ge(*at("y zero"))
        for b in range(4, 8):
            key = f"moe{b}"
            pe.matmul(claim(pe, b, key)[:, :], e_y[:, 0:P], e_y[:, 0:512], start=True, stop=True,
                                   skip_group_check=True).then_inc(*PE.step("full " + key))
        for b in range(4):
            claim(pe, b, f"expert bank{b}")

        def body(i):
            def tile(t):
                n = N_PRE + t
                pe.wait_ge(tile_sem(n), i * (16 * N_EXP // RING) + 16 * (n // RING + 1))
                return n
            pe.wait_ge(*at("xe"))
            pe.wait_ge(*at("y copied", back=1))
            for s in range(2):
                for t in range(4):
                    w = place(tile(4 * s + t), P, 2, 4 * 512)
                    for kk in range(2):
                        for j in range(4):
                            ins = pe.matmul(banks[s][32 * j:32 * j + 32, :], e_xe[:, 2 * t + kk, :],
                                                w[:, kk, 512 * j:512 * j + 512], start=t + kk == 0, stop=t + kk == 4)
                    ins.then_inc(*PE.step(f"expert used{4 * s + t}", *([("a full", "b full")[s]] if t == 3 else [])))
            pe.wait_ge(*at("G", back=1))
            pe.wait_ge(*at("row"))
            pe.matmul(banks[3][:, :], ones[0:EXPERTS, 0:P], e_row, start=True, stop=True).then_inc(*PE.step("row full"))
            pe.wait_ge(*at("h ready"))
            for k in range(4):
                ins = pe.transpose(banks[2][:, k * P:(k + 1) * P], e_h[:, k * P:(k + 1) * P], ident[:, :])
            ins.then_inc(*PE.step("hT full"))
            pe.wait_ge(*at("hT copied"))
            for t in range(4):
                w = place(tile(8 + t), P, 4, D)
                for half in range(2):
                    for k in range(4):
                        ins = pe.matmul(banks[half][32 * k:32 * k + 32, :], e_hT[:, k, 32 * t:32 * t + 32],
                                            w[:, k, 512 * half:512 * half + 512], start=t == 0, stop=t == 3)
                ins.then_inc(*PE.step(f"expert used{8 + t}", *(["y full"] if t == 3 else [])))
            pe.wait_ge(*at("y copied"))
            pe.wait_ge(*at("G"))
            for j in range(KD):
                ins = pe.matmul(banks[4 + j // 2][:, (j % 2) * N:(j % 2 + 1) * N], e_y[:, j * P:(j + 1) * P], e_G,
                                    start=False, stop=True, skip_group_check=True)
            ins.then_inc(*PE.step("scattered"))
        loop(pe, PE, body)
        for b in range(4):
            book.where[f"free expert bank{b}"] = book.where.get(("y copied", "y copied", "hT copied", "G")[b], (PE.cur, 1))

    def act_experts(act):
        act.wait_ge(*at("gathered"))
        act.wait_ge(*at("y zero"))

        def body(i):
            act.wait_ge(*at("a full"))
            act.wait_ge(*at("h ready", back=1))
            act.activation(e_h, banks[0][:, :], ACT.Silu).then_inc(*AC.step("silu"))
            act.wait_ge(*at("hT full"))
            act.copy(e_hT.rearrange("p a b -> p (a b)"), banks[2][:, :]).then_inc(*AC.step("hT copied"))
            act.wait_ge(*at("y full"))
            act.wait_ge(*at("scattered", back=1))
            act.copy(e_y[:, 0:512], banks[0][:, :]).then_inc(*AC.step())
            act.copy(e_y[:, 512:1024], banks[1][:, :]).then_inc(*AC.step("y copied"))
        loop(act, AC, body)

    def dve_experts(v):
        v.wait_ge(*at("gathered"))

        def body(i):
            v.wait_ge(*at("b full", back=1))
            v.tensor_copy(e_xe, e_xg[:, :, bass.ds(i * CAP, CAP)]).then_inc(*DV.step("xe"))
            v.tensor_scalar(e_row, e_pa, ident[0:EXPERTS, bass.ds(i, 1)], None, ALU.mult).then_inc(*DV.step("row"))
            v.wait_ge(*at("row full"))
            v.wait_ge(*at("scattered", back=1))
            v.tensor_copy(e_t, banks[3][:, N:2 * N]).then_inc(*DV.step())
            v.wait_ge(*DV.last())
            v.scalar_tensor_tensor(e_G, banks[3][:, 0:N], e_slot, e_t, ALU.is_equal, ALU.mult).then_inc(*DV.step("G"))
            v.wait_ge(*at("silu"))
            v.wait_ge(*at("b full"))
            v.tensor_tensor(e_h, e_h, banks[1][:, :], ALU.mult).then_inc(*DV.step("h ready"))
        loop(v, DV, body)
        DV.stage("moeout")
        v.wait_ge(*at("scattered"))
        for j in range(KD):
            v.scalar_tensor_tensor(xT[:, j, :], banks[4 + j // 2][:, (j % 2) * N:(j % 2 + 1) * N],
                                             adaX[0][:, 40 + j:41 + j], xT[:, j, :], ALU.mult, ALU.add).then_inc(*DV.step(f"free moe{4 + j // 2}", "x moe"))

    qkv = view(arena, 0, P, NC, MERGE2)
    tabA = view(arena, 5680, P, NC, 4, HD)
    tabB = view(arena, 6192, P, NC, 4, HD)
    cs = view(arena, 6704, P, NC, 2, 32)
    gain = view(arena, 6832, P, 4, HD)
    qT = view(arena, 7088, P, 8, N)
    kp = view(arena, 9136, P, 16, N)
    y2 = view(arena, 13232, P, NC, D)
    yT2 = view(arena, 15280, P, KD, N)
    sqh = view(arena, 17328, P, NC, 28 * HD)
    ptc = view(arena, 17328, 16, 16, P)
    cw2 = view(arena, 20912, P, 2, 2, HD)
    pet = view(arena, 21168, HD, 2, 32)
    hidc = view(arena, 21232, P, 2, 32)
    kcv = view(arena, 21296, 16, 4, HD)
    kct = view(arena, 21552, P, 4, 16)
    causal = arena[:, 21616:21872]
    cmask = view(arena, 21872, P, NC, 16)
    valid = arena[:, 21904:21906]
    tabC = view(arena, 21908, 16, 2, HD)
    csc = view(arena, 22036, 16, 2, 32)
    inv = arena[:, 22100:22132]
    ang = view(arena, 22132, P, 3, 32)
    posi = arena[:, 22228:22231]
    posf = arena[:, 22232:22235]
    msq = view(arena, 22240, P, NC, 28)
    mx = view(arena, 22300, P, 3, 2)
    sums = view(arena, 22308, P, NC, 24)
    wts = view(arena, 22356, P, NC, 8)
    sC = view(arena, 22372, P, 16, 16)
    mC, suC = arena[:, 22628:22644], arena[:, 22644:22660]
    msc = arena[0:16, 22660:22664]
    tmpc = view(arena, 22664, 16, 2, HD)
    kdup = view(arena, 22792, 16, 2, 2, HD)
    gain_l = view(arena, 23048, P, 2, 4, HD)
    peraw = view(arena, 23560, 32, 2, HD)
    ffT = view(arena, 0, P, FB, N)
    sm = view(scr, 0, P, 3, 384)
    pt = view(scr, 1152, P, 3, 384)
    tmpo = scr[:, 2304:2816]
    sg = view(scr, 0, P, 2, 512)
    otok = view(arena, 0, P, NC, D)

    GROUPS = [(0, 8, 0, 0), (768, 2, 8, 1), (KW0, 2, 10, 1), (QB0, 8, 12, 2), (QB0 + 512, 8, 20, 3)]

    def act_second_loads(act):
        AC.stage("rope")
        act.wait_ge(*at("scattered"))
        act.wait_ge(*at("x moe"))

        def load(dst, src, **kw):
            act.dma_start(dst, src, **kw).then_inc(*K.load("load_second"))
        pos = A["positions_2"]
        load(posi[:, 0:2].bitcast(I32), pos[0].rearrange("(c p) -> p c", p=P), allow_slow_non_contiguous=True)
        load(posi[0:15, 2:3].bitcast(I32), pos[0, 31::16].rearrange("(n a) -> n a", a=1), allow_slow_non_contiguous=True)
        load(inv, A["k_inv"])
        load(causal, A["k_causal"])
        load(cmask, A["k_cmask"])
        load(valid, A["k_valid"])
        for l in range(LAYERS):
            for i, nm in enumerate(("nsa_q_gain_2", "nsa_k_gain_2", "moba_q_gain_2", "moba_k_gain_2")):
                load(gain_l[:, l, i, :], A[nm][l].rearrange("(a n) -> a n", a=1).broadcast_to([P, HD]))
            load(peraw[:, l, :], A["nsa_cmp_pe_2"][l])
            for i, nm in enumerate("kv"):
                load(cw2[:, l, i, :], A[f"nsa_cmp_{nm}_w2_2"][l])

    def pe_rope(pe):
        PE.stage("rope")
        pe.wait_ge(*K.loaded("load_second"))
        b = bank(pe, "pet")
        for l in range(LAYERS):
            ins = pe.transpose(b[0:HD, l * 32:(l + 1) * 32], peraw[:, l, :], ident[0:32, 0:32])
        ins.then_inc(*PE.step("full pet"))

    def act_rope(act):
        for i in range(2):
            act.wait_ge(*at(f"angle{i}"))
            act.activation(cs[:, :, i, :], ang[:, 0:2, :], ACT.Sin).then_inc(*AC.step())
            act.activation(csc[0:15, i, :], ang[0:15, 2, :], ACT.Sin).then_inc(*AC.step(f"sine{i}"))

    def dve_rope(v):
        DV.stage("rope")
        v.wait_ge(*K.loaded("load_second"))
        v.wait_ge(*at("full pet"))
        b = bank_of("pet")
        v.tensor_copy(pet, b[0:HD, 0:64].rearrange("p (l j) -> p l j", l=2)).then_inc(*DV.step("free pet", "pe ready"))
        v.memset(kp, 0.0).then_inc(*DV.step())
        v.memset(kct, 0.0).then_inc(*DV.step())
        v.memset(kcv, 0.0).then_inc(*DV.step())
        v.memset(posf, 0.0).then_inc(*DV.step())
        v.wait_ge(*DV.last())
        v.tensor_copy(posf[:, 0:2], posi[:, 0:2].bitcast(I32)).then_inc(*DV.step())
        v.tensor_copy(posf[0:15, 2:3], posi[0:15, 2:3].bitcast(I32)).then_inc(*DV.step())
        v.wait_ge(*DV.last())
        a0 = sqh[:, 0, 0:96].rearrange("p (a b) -> p a b", a=3)
        kk = sqh[:, 1, 0:96].rearrange("p (a b) -> p a b", a=3)
        for c in range(3):
            v.tensor_scalar(a0[:, c, :], inv, posf[:, c:c + 1], None, ALU.mult).then_inc(*DV.step())
        for i in range(2):
            if i:
                v.wait_ge(*at("sine0"))
            v.wait_ge(*DV.last())
            dve_reduce(v, ang, a0, kk, quarter=i == 0)
            book.where[f"angle{i}"] = DV.now
        v.wait_ge(*at("sine1"))

    def pe_in(pe, l):
        PE.stage("second")
        pe.wait_ge(*at(f"h mix{l + 1} done"))
        for t in range(6):
            pe_linear_tok(pe, f"in{l}_{t}", f"in{l}_{t}", h2, 0)

    IN_COLS = [(0, 512), (512, 1024), (1024, 1304), (1304, 1816), (1816, 2328), (2328, 2840)]

    def act_in(act, l):
        AC.stage("second")
        act.wait_ge(*at("x moe" if l == 0 else "ffn read0"))
        for t, (lo, hi) in enumerate(IN_COLS):
            for c in range(NC):
                key = f"in{l}_{t}{c}"
                act.wait_ge(*at("full " + key))
                b = bank_of(key)
                act.copy(qkv[:, c, lo:hi], b[:, 0:hi - lo]).then_inc(*AC.step("free " + key, f"in{l} {t}"))
        act.wait_ge(*AC.last())
        for c in range(NC):
            for col, H, lo, _ in GROUPS:
                act.activation(sqh[:, c, lo * HD:(lo + H) * HD], qkv[:, c, col:col + H * HD], ACT.Square).then_inc(*AC.step(f"squares{l}"))
        for c in range(NC):
            act.activation(qkv[:, c, KV0 + 768:KV0 + 792], qkv[:, c, KV0 + 768:KV0 + 792], ACT.Sigmoid).then_inc(*AC.step(f"head gates{l}"))
        act.wait_ge(*at(f"head mean{l}"))
        act.activation(msq, msq, ACT.Sqrt).then_inc(*AC.step(f"head root{l}"))

    def dve_in(v, l):
        DV.stage("second")
        v.wait_ge(*at("sine1"))
        g4 = gain_l[:, l].rearrange("p g (s e) -> p g s e", s=2)
        for c in range(NC):
            a4 = tabA[:, c].rearrange("p g (s e) -> p (g s) e", s=2)
            b4 = tabB[:, c].rearrange("p g (s e) -> p g s e", s=2)
            v.tensor_tensor(a4, gain_l[:, l].rearrange("p g (s e) -> p (g s) e", s=2),
                                      spread(cs[:, c, 0, :], 1, 8), ALU.mult).then_inc(*DV.step())
            v.scalar_tensor_tensor(b4[:, :, 0, :], g4[:, :, 1, :], -1.0, spread(cs[:, c, 1, :], 1, 4),
                                             ALU.mult, ALU.mult).then_inc(*DV.step())
            v.tensor_tensor(b4[:, :, 1, :], g4[:, :, 0, :], spread(cs[:, c, 1, :], 1, 4), ALU.mult).then_inc(*DV.step())
        v.wait_ge(*at(f"squares{l}"))
        v.tensor_reduce(msq, sqh.rearrange("p c (h e) -> p c h e", e=HD), AX, ALU.add).then_inc(*DV.step())
        v.wait_ge(*DV.last())
        v.tensor_scalar(msq, msq, 1.0 / HD, EPS, ALU.mult, ALU.add).then_inc(*DV.step(f"head mean{l}"))
        v.wait_ge(*at(f"head root{l}"))
        v.reciprocal(msq, msq).then_inc(*DV.step())
        v.wait_ge(*DV.last())
        for c in range(NC):
            for col, H, lo, g in GROUPS:
                x = qkv[:, c, col:col + H * HD].rearrange("p (h e) -> p h e", e=HD)
                v.tensor_tensor(x, x, spread(msq[:, c, lo:lo + H], 2, HD), ALU.mult).then_inc(*DV.step())
        v.wait_ge(*DV.last())
        for c in range(NC):
            for col, H, lo, g in GROUPS:
                x = qkv[:, c, col:col + H * HD].rearrange("p (h e) -> p h e", e=HD)
                t = sqh[:, c, lo * HD:(lo + H) * HD].rearrange("p (h e) -> p h e", e=HD)
                v.tensor_tensor(t[:, :, 0:32], x[:, :, 32:64], spread(tabB[:, c, g, 0:32], 1, H), ALU.mult).then_inc(*DV.step())
                v.tensor_tensor(t[:, :, 32:64], x[:, :, 0:32], spread(tabB[:, c, g, 32:64], 1, H), ALU.mult).then_inc(*DV.step())
        v.wait_ge(*DV.last())
        for c in range(NC):
            for col, H, lo, g in GROUPS:
                x = qkv[:, c, col:col + H * HD].rearrange("p (h e) -> p h e", e=HD)
                v.tensor_tensor(x, x, spread(tabA[:, c, g, :], 1, H), ALU.mult).then_inc(*DV.step())
        v.wait_ge(*DV.last())
        for c in range(NC):
            for col, H, lo, g in GROUPS:
                x = qkv[:, c, col:col + H * HD]
                v.tensor_tensor(x, x, sqh[:, c, lo * HD:(lo + H) * HD], ALU.add).then_inc(*DV.step(f"roped{l}"))

    def pe_compress(pe, l):
        PE.stage("compress")
        pe.wait_ge(*at(f"in{l} 1"))
        pe.wait_ge(*at("pe ready"))
        for s in range(2):
            key = f"cturn{l}{s}"
            b = bank(pe, key)
            for g in range(2):
                for c in range(NC):
                    col = KV0 + s * 128 + g * HD
                    ins = pe.transpose(b[0:HD, (g * 2 + c) * P:(g * 2 + c + 1) * P], qkv[:, c, col:col + HD], ident[:, :])
            ins.then_inc(*PE.step("full " + key))
        for s in range(2):
            w = tile(pe, f"cmp{'kv'[s]}{l}_0")
            pe.wait_ge(*at(f"cmp x{l}{s}"))
            key = f"chid{l}{s}"
            b = bank(pe, key)
            for j in range(32):
                x = cmpx[:, 2 * s + j // 16].rearrange("p g (n j) -> p g n j", j=16)
                x = x[:, :, j // 16:j // 16 + 15, j % 16]
                ins = pe.matmul(b[:, 0:30], w[:, j, :], x, start=j == 0, stop=j == 31)
            ins.then_inc(*PE.step("full " + key))
            mark_used(pe, f"cmp{'kv'[s]}{l}_0")
        pe.wait_ge(*at(f"gelu{l}"))
        b = bank(pe, f"cout{l}")
        for s in range(2):
            for g in range(2):
                o = (2 * s + g) * HD
                ins = pe.matmul(b[0:15, o:o + HD], hidc[:, s, 15 * g:15 * g + 15], cw2[:, l, s, :], start=True, stop=True)
        ins.then_inc(*PE.step(f"full cout{l}"))
        pe.wait_ge(*at(f"kdup{l}"))
        b = bank(pe, f"kct{l}")
        for g in range(2):
            ins = pe.transpose(b[:, g * 16:g * 16 + 15], kdup[0:15, g].rearrange("p a b -> p (a b)"), ident[0:15, 0:15])
        ins.then_inc(*PE.step(f"full kct{l}"))

    def act_compress(act, l):
        AC.stage("compress")
        for s in range(2):
            act.wait_ge(*at(f"full chid{l}{s}"))
            b = bank_of(f"chid{l}{s}")
            act.activation(hidc[:, s, 0:30], b[:, 0:30], ACT.Gelu_apprx_tanh).then_inc(*AC.step(f"free chid{l}{s}", f"gelu{l}"))
        act.wait_ge(*at(f"cmp mean{l}"))
        act.activation(msc[0:15, 0:2], msc[0:15, 0:2], ACT.Sqrt).then_inc(*AC.step(f"cmp root{l}"))

    def dve_compress(v, l):
        DV.stage("compress")
        v.wait_ge(*at("pe ready"))
        for s in range(2):
            v.wait_ge(*at(f"full cturn{l}{s}"))
            b = bank_of(f"cturn{l}{s}")
            for half in range(2):
                v.tensor_tensor(cmpx[:, 2 * s + half].rearrange("p g (n j) -> p (g n) j", j=16),
                                          b[0:HD, :].rearrange("p (n j) -> p n j", j=16),
                                          spread(pet[:, l, half * 16:half * 16 + 16], 1, 32), ALU.add).then_inc(*DV.step(f"free cturn{l}{s}", f"cmp x{l}{s}"))
        v.wait_ge(*at(f"full cout{l}"))
        b = bank_of(f"cout{l}")
        v.tensor_copy(kcv[0:15], b[0:15, 0:256].rearrange("p (a b) -> p a b", a=4)).then_inc(*DV.step(f"free cout{l}"))
        v.wait_ge(*DV.last())
        k2 = kcv[0:15, 0:2, :]
        v.tensor_tensor(tmpc[0:15], k2, k2, ALU.mult).then_inc(*DV.step())
        v.wait_ge(*DV.last())
        v.tensor_reduce(msc[0:15, 0:2], tmpc[0:15], AX, ALU.add).then_inc(*DV.step())
        v.wait_ge(*DV.last())
        v.tensor_scalar(msc[0:15, 0:2], msc[0:15, 0:2], 1.0 / HD, EPS, ALU.mult, ALU.add).then_inc(*DV.step(f"cmp mean{l}"))
        g = gain_l[0:15, l, 1, :].rearrange("p (s e) -> p s e", s=2)
        ta = tabC[0:15, 0, :].rearrange("p (s e) -> p s e", s=2)
        tb = tabC[0:15, 1, :].rearrange("p (s e) -> p s e", s=2)
        v.tensor_tensor(ta, g, spread(csc[0:15, 0, :], 1, 2), ALU.mult).then_inc(*DV.step())
        v.scalar_tensor_tensor(tb[:, 0, :], g[:, 1, :], -1.0, csc[0:15, 1, :], ALU.mult, ALU.mult).then_inc(*DV.step())
        v.tensor_tensor(tb[:, 1, :], g[:, 0, :], csc[0:15, 1, :], ALU.mult).then_inc(*DV.step())
        v.wait_ge(*at(f"cmp root{l}"))
        v.reciprocal(msc[0:15, 0:2], msc[0:15, 0:2]).then_inc(*DV.step())
        v.wait_ge(*DV.last())
        v.tensor_tensor(k2, k2, spread(msc[0:15, 0:2], 2, HD), ALU.mult).then_inc(*DV.step())
        v.wait_ge(*DV.last())
        v.tensor_tensor(tmpc[0:15, :, 0:32], k2[:, :, 32:64], spread(tabC[0:15, 1, 0:32], 1, 2), ALU.mult).then_inc(*DV.step())
        v.tensor_tensor(tmpc[0:15, :, 32:64], k2[:, :, 0:32], spread(tabC[0:15, 1, 32:64], 1, 2), ALU.mult).then_inc(*DV.step())
        v.wait_ge(*DV.last())
        v.tensor_tensor(k2, k2, spread(tabC[0:15, 0, :], 1, 2), ALU.mult).then_inc(*DV.step())
        v.wait_ge(*DV.last())
        for i in range(2):
            v.tensor_tensor(kdup[0:15, :, i, :], k2, tmpc[0:15], ALU.add).then_inc(*DV.step(f"kdup{l}"))
        v.wait_ge(*at(f"full kct{l}"))
        b = bank_of(f"kct{l}")
        bb = b[:, 0:32].rearrange("p (g n) -> p g n", g=2)[:, :, 0:15]
        for par in range(2):
            lo, hi = 64 * par, 64 * par + 64
            v.tensor_copy(kct[lo:hi, par::2, 0:15], bb[lo:hi]).then_inc(*DV.step(f"free kct{l}", f"kct ready{l}"))

    def pe_heads(pe, l):
        PE.stage("heads")
        pe.wait_ge(*at(f"roped{l}"))
        for q in range(4):
            for c in range(NC):
                if q < 2:
                    srcs = [qkv[:, c, (0, QB0)[q] + i * P:(0, QB0)[q] + (i + 1) * P] for i in range(4)]
                elif q == 2:
                    srcs = [qkv[:, c, QB0 + 512 + i * P:QB0 + 512 + (i + 1) * P] for i in range(4)]
                else:
                    srcs = [dup[:, c, i, :] for i in range(4)]
                key = f"heads{l}{q}{c}"
                b = bank(pe, key)
                for i, s in enumerate(srcs):
                    ins = pe.transpose(b[:, i * P:(i + 1) * P], s, ident[:, :])
                ins.then_inc(*PE.step("full " + key))

    dup = view(hx, KD * N, P, NC, 4, P)

    def act_heads(act, l):
        AC.stage("heads")
        for q in range(2):
            for c in range(NC):
                key = f"heads{l}{q}{c}"
                act.wait_ge(*at("full " + key))
                b = bank_of(key)
                act.copy(qT[:, 4 * q:4 * q + 4, c * P:(c + 1) * P], b[:, :].rearrange("p (i t) -> p i t", i=4)).then_inc(*AC.step("free " + key, f"qT{l}"))

    def dve_heads(v, l):
        DV.stage("heads")
        for c in range(NC):
            for bi, col in enumerate((768, KW0)):
                for i in range(2):
                    v.tensor_copy(dup[:, c, 2 * bi:2 * bi + 2, i * HD:(i + 1) * HD],
                                            qkv[:, c, col:col + P].rearrange("p (g e) -> p g e", g=2)).then_inc(*DV.step(f"roped{l}"))
        for q in range(2, 4):
            for c in range(NC):
                key = f"heads{l}{q}{c}"
                v.wait_ge(*at("full " + key))
                b = bank_of(key)
                bb = b[:, :].rearrange("p (i t) -> p i t", i=4)
                for par in range(2):
                    lo, hi = 64 * par, 64 * par + 64
                    s0 = par if q == 2 else 8 + par
                    v.tensor_copy(kp[lo:hi, s0:s0 + 7:2, c * P:(c + 1) * P], bb[lo:hi]).then_inc(*DV.step("free " + key, f"kp{l}"))

    UNITS = [(b, h) for b in range(3) for h in range(8)]

    def unit(n):
        b, h = UNITS[n]
        pair = h // 2 + (4 if b == 2 else 0)
        slot_ = h if b == 2 else 8 + 4 * b + (h // 4) * 2 + h % 2
        vcol = (896, 1152, 2328)[b] + (h if b == 2 else h // 4) * HD
        return b, h, pair, slot_, vcol

    pool4 = {"w": 0}

    def bank4(pe, key):
        b = pool4["w"] % 4
        pool4["w"] += 1
        book.bank[key] = b
        return claim(pe, b, key)

    def obank(pe, key, b, c):
        n = 4 + 2 * (b % 2) + c
        book.bank[key] = n
        return claim(pe, n, key)

    def pe_attend(pe, l):
        PE.stage("attend")
        pe.wait_ge(*at(f"qT{l}"))
        pe.wait_ge(*at(f"kct ready{l}"))
        pe.wait_ge(*at(f"kp{l}"))
        key = f"cs{l}"
        b = bank4(pe, key)
        for h in range(8):
            for c in range(NC):
                o = (h * 2 + c) * 16
                ins = pe.matmul(b[:, o:o + 16], qT[:, h // 2, c * P:(c + 1) * P], kct[:, (h // 4) * 2 + h % 2, :],
                                    start=True, stop=True)
        ins.then_inc(*PE.step("full " + key))

        o_bank = []

        def scores(n):
            br, h, pair, sl, _ = unit(n)
            key = f"s{l}_{n}"
            b = bank4(pe, key)
            pe.matmul(b[:, 0:P], qT[:, pair, 0:P], kp[:, sl, 0:P], start=True, stop=True)
            pe.matmul(b[:, P:P + N], qT[:, pair, P:N], kp[:, sl, :], start=True, stop=True).then_inc(*PE.step("full " + key))

        def turned(n):
            key = f"pt{l}_{n}"
            b = bank4(pe, key)
            pe.wait_ge(*at(f"P{l}_{n}"))
            for i in range(3):
                ins = pe.transpose(b[:, i * P:(i + 1) * P], sm[:, n % 3, i * P:(i + 1) * P], ident[:, :])
            ins.then_inc(*PE.step("full " + key))

        def values(n):
            br, h, _, _, vcol = unit(n)
            if h == 0:
                o_bank[:] = [obank(pe, f"o{l}_{br}{c}", br + 1, c) for c in range(NC)]
            pe.wait_ge(*at(f"PT{l}_{n}"))
            o = slice(h * HD, h * HD + HD)
            p_ = pt[:, n % 3]
            ins = pe.matmul(o_bank[0][:, o], p_[:, 0:P], qkv[:, 0, vcol:vcol + HD], start=True, stop=True)
            if h == 7:
                ins.then_inc(*PE.step(f"full o{l}_{br}0"))
            pe.matmul(o_bank[1][:, o], p_[:, P:2 * P], qkv[:, 0, vcol:vcol + HD], start=True, stop=False)
            ins = pe.matmul(o_bank[1][:, o], p_[:, 2 * P:3 * P], qkv[:, 1, vcol:vcol + HD], start=False, stop=True)
            if h == 7:
                ins.then_inc(*PE.step(f"full o{l}_{br}1"))
                book.where[f"V{l}_{n}"] = PE.now
            else:
                ins.then_inc(*PE.step(f"V{l}_{n}"))

        scores(0)
        pe.wait_ge(*at(f"PC{l}"))
        for i in range(4):
            key = f"ct{l}{i}"
            b = bank4(pe, key)
            for j in range(4):
                ins = pe.transpose(b[0:16, j * P:(j + 1) * P], sC[:, 4 * i + j, :], ident[:, :])
            ins.then_inc(*PE.step("full " + key))
        scores(1)
        turned(0)
        pe.wait_ge(*at(f"PTC{l}"))
        ob = [obank(pe, f"oc{l}{c}", 0, c) for c in range(NC)]
        for c in range(NC):
            for h in range(8):
                ins = pe.matmul(ob[c][:, h * HD:(h + 1) * HD], ptc[:, 2 * h + c, :], kcv[:, 2 + h // 4, :], start=True,
                                    stop=True)
            ins.then_inc(*PE.step(f"full oc{l}{c}"))
        for n in range(2, 24):
            scores(n)
            turned(n - 1)
            values(n - 2)
        turned(23)
        values(22)
        values(23)
        pe.wait_ge(*at(f"attended{l}"))
        for kk in range(4):
            key = f"yt{l}{kk}"
            b = bank4(pe, key)
            for i in range(2):
                for c in range(NC):
                    j = 2 * kk + i
                    ins = pe.transpose(b[:, (2 * i + c) * P:(2 * i + c + 1) * P], y2[:, c, j * P:(j + 1) * P], ident[:, :])
            ins.then_inc(*PE.step("full " + key))

    def act_attend(act, l):
        AC.stage("attend")

        def probs(n):
            act.wait_ge(*at(f"sm{l}_{n}"))
            for c, (lo, hi) in enumerate(((0, P), (P, 3 * P))):
                act.activation(sm[:, n % 3, lo:hi], sm[:, n % 3, lo:hi], ACT.Exp, bias=mx[:, n % 3, c:c + 1],
                                           scale=HD ** -0.5, accum_out=sums[:, c, n:n + 1]).then_inc(*AC.step(f"P{l}_{n}"))

        def copies(n):
            key = f"pt{l}_{n}"
            act.wait_ge(*at("full " + key))
            b = bank_of(key)
            if n >= 3:
                act.wait_ge(*at(f"V{l}_{n - 3}"))
            act.copy(pt[:, n % 3, :], b[:, 0:384]).then_inc(*AC.step("free " + key, f"PT{l}_{n}"))

        act.wait_ge(*at(f"smC{l}"))
        act.activation(sC, sC, ACT.Exp, scale=HD ** -0.5).then_inc(*AC.step(f"PC{l}"))
        probs(0)
        for i in range(4):
            key = f"ct{l}{i}"
            act.wait_ge(*at("full " + key))
            b = bank_of(key)
            act.copy(ptc[:, 4 * i:4 * i + 4, :], b[0:16, :].rearrange("p (a b) -> p a b", a=4)).then_inc(*AC.step("free " + key, f"PTC{l}"))
        for n in range(1, 24):
            probs(n)
            copies(n - 1)
        copies(23)
        for kk in range(4):
            key = f"yt{l}{kk}"
            act.wait_ge(*at("full " + key))
            b = bank_of(key)
            act.copy(yT2[:, 2 * kk:2 * kk + 2, :], b[:, :].rearrange("p (a t) -> p a t", a=2)).then_inc(*AC.step("free " + key, f"ya{l + 1}", f"yb{l + 1}"))

    def dve_attend(v, l):
        DV.stage("attend")
        v.wait_ge(*at(f"full cs{l}"))
        b = bank_of(f"cs{l}")
        v.tensor_tensor(sC.rearrange("p (h c) n -> p h (c n)", c=2),
                                  b[:, 0:256].rearrange("p (h m) -> p h m", h=8),
                                  spread(cmask.rearrange("p c n -> p (c n)"), 1, 8), ALU.add).then_inc(*DV.step(f"free cs{l}"))
        v.wait_ge(*DV.last())
        v.tensor_reduce(mC, sC, AX, ALU.max).then_inc(*DV.step())
        v.wait_ge(*DV.last())
        v.tensor_tensor(sC, sC, spread(mC, 2, 16), ALU.subtract).then_inc(*DV.step(f"smC{l}"))

        def softmax_in(n):
            key = f"s{l}_{n}"
            v.wait_ge(*at("full " + key))
            b = bank_of(key)
            if n >= 3:
                v.wait_ge(*at(f"full pt{l}_{n - 3}"))
            for c, (lo, hi) in enumerate(((0, P), (P, 3 * P))):
                v.tensor_tensor_reduce(sm[:, n % 3, lo:hi], b[:, lo:hi],
                                                 causal[:, P:N] if c == 0 else causal[:, :], 1.0, -3e38, ALU.add, ALU.max,
                                                 mxr[:, n % 3, c:c + 1]).then_inc(*DV.step("free " + key))
            v.wait_ge(*DV.last())
            v.tensor_scalar(mx[:, n % 3, :], mxr[:, n % 3, :], -HD ** -0.5, None, ALU.mult).then_inc(*DV.step(f"sm{l}_{n}"))

        def outputs(br):
            v.wait_ge(*at(f"P{l}_{8 * br + 7}"))
            for c in range(NC):
                w = wts[:, c, :]
                v.reciprocal(w, sums[:, c, 8 * br:8 * br + 8]).then_inc(*DV.step())
                v.wait_ge(*DV.last())
                if br < 2:
                    g = qkv[:, c, GATES2:GATES2 + 24].rearrange("p (h b) -> p h b", b=3)[:, :, br + 1]
                    v.tensor_tensor(w, w, g, ALU.mult).then_inc(*DV.step())
                    v.wait_ge(*DV.last())
                v.wait_ge(*at(f"full o{l}_{br}{c}"))
                b = bank_of(f"o{l}_{br}{c}")
                ob = b[:, :].rearrange("p (h e) -> p h e", h=8)
                if br == 2:
                    v.tensor_tensor(y2[:, c, 512:1024].rearrange("p (h e) -> p h e", h=8), ob, spread(w, 2, HD),
                                              ALU.mult).then_inc(*DV.step(f"free o{l}_{br}{c}", f"attended{l}"))
                else:
                    v.tensor_tensor(tmpo.rearrange("p (h e) -> p h e", h=8), ob, spread(w, 2, HD), ALU.mult).then_inc(*DV.step(f"free o{l}_{br}{c}"))
                    v.wait_ge(*DV.last())
                    v.tensor_tensor(y2[:, c, 0:512], y2[:, c, 0:512], tmpo, ALU.add).then_inc(*DV.step())

        softmax_in(0)
        v.wait_ge(*at(f"PC{l}"))
        v.tensor_reduce(suC, sC, AX, ALU.add).then_inc(*DV.step())
        v.wait_ge(*DV.last())
        v.reciprocal(suC, suC).then_inc(*DV.step())
        softmax_in(1)
        v.wait_ge(*at(f"head gates{l}"))
        for c in range(NC):
            w = wts[:, c, :]
            g = qkv[:, c, GATES2:GATES2 + 24].rearrange("p (h b) -> p h b", b=3)[:, :, 0]
            v.scalar_tensor_tensor(w, suC.rearrange("p (h c) -> p h c", c=2)[:, :, c], valid[:, c:c + 1], g,
                                             ALU.mult, ALU.mult).then_inc(*DV.step())
            v.wait_ge(*DV.last())
            v.wait_ge(*at(f"full oc{l}{c}"))
            b = bank_of(f"oc{l}{c}")
            v.tensor_tensor(y2[:, c, 0:512].rearrange("p (h e) -> p h e", h=8),
                                      b[:, :].rearrange("p (h e) -> p h e", h=8), spread(w, 2, HD), ALU.mult).then_inc(*DV.step(f"free oc{l}{c}"))
        for n in range(2, 24):
            softmax_in(n)
            if n in (10, 18):
                outputs(n // 8 - 1)
        outputs(2)

    mxr = view(arena, 23690, P, 3, 2)

    def pe_gates2(pe, l):
        PE.stage("gates")
        for t in range(4):
            pe_linear_T(pe, f"gt2{l}{t}", f"merge2_{l}{t}", h2, N)

    def act_gates2(act, l):
        AC.stage("gates")
        if l == 0:
            act.wait_ge(*at("x mixed0"))
        else:
            act.wait_ge(*at("x mixed1"))
        for t in range(4):
            for i in range(2):
                key = f"gt2{l}{t}{i}"
                act.wait_ge(*at("full " + key))
                b = bank_of(key)
                blk = 4 * t + 2 * i
                act.activation(gates[:, blk % KD:blk % KD + 2, blk // KD, :],
                                           b[:, :].rearrange("p (j t) -> p j t", j=2), ACT.Sigmoid).then_inc(*AC.step("free " + key, f"gates{l + 1}"))

    def pe_ffn(pe, l):
        PE.stage("ffn")
        pe.wait_ge(*at(f"h ffn{l + 1} done"))
        for i in range(6):
            nb = 4 if i < 5 else 2
            pe_linear_T(pe, f"g{l}{i}_", f"gt{l}_{i}_0", h2, N, nb)
            pe_linear_T(pe, f"u{l}{i}_", f"up{l}_{i}_0", h2, N, nb)
        acc = [bank(pe, f"down{l}{i}") for i in range(4)]
        pe.wait_ge(*at(f"hidden{l}"))
        for t in range(6):
            w = tile(pe, f"down{l}_{t}")
            nk = 4 if t < 5 else 2
            for j in range(KD):
                for k in range(nk):
                    f = 4 * t + k
                    ins = pe.matmul(acc[j // 2][:, (j % 2) * N:(j % 2 + 1) * N], w[:, k, j * P:(j + 1) * P],
                                        ffT[:, f, :], start=f == 0 and j % 2 == 0, stop=f == FB - 1, skip_group_check=True)
                if t == 5 and j % 2:
                    ins.then_inc(*PE.step(f"full down{l}{j // 2}"))
            if t < 5:
                ins.then_inc(*PE.step())
            mark_used(pe, f"down{l}_{t}")
        book.where[f"ffn read{l}"] = PE.now

    def act_ffn(act, l):
        AC.stage("ffn")
        act.wait_ge(*at(f"h ffn{l + 1} done"))
        n = 0
        for i in range(6):
            for j in range(2 if i < 5 else 1):
                key = f"g{l}{i}_{j}"
                act.wait_ge(*at("full " + key))
                b = bank_of(key)
                if n >= 2:
                    act.wait_ge(*at(f"hid{l}_{n - 2}"))
                act.activation(sg[:, n % 2, :], b[:, :], ACT.Silu).then_inc(*AC.step("free " + key, f"sg{l}_{n}"))
                n += 1

    def dve_ffn(v, l):
        DV.stage("ffn")
        n = 0
        for i in range(6):
            for j in range(2 if i < 5 else 1):
                key = f"u{l}{i}_{j}"
                v.wait_ge(*at("full " + key))
                b = bank_of(key)
                v.wait_ge(*at(f"sg{l}_{n}"))
                f = 4 * i + 2 * j
                v.tensor_tensor(ffT[:, f:f + 2, :].rearrange("p a b -> p (a b)"), b[:, :], sg[:, n % 2, :],
                                          ALU.mult).then_inc(*DV.step("free " + key, f"hid{l}_{n}", f"hidden{l}"))
                n += 1
        for j in range(KD):
            v.wait_ge(*at(f"full down{l}{j // 2}"))
            b = bank_of(f"down{l}{j // 2}")
            v.scalar_tensor_tensor(xT[:, j, :], b[:, (j % 2) * N:(j % 2 + 1) * N],
                                             adaX[l + 1][:, 40 + j:41 + j], xT[:, j, :], ALU.mult, ALU.add).then_inc(*DV.step(f"free down{l}{j // 2}", f"x layer{l}"))

    def pe_result(pe):
        PE.stage("result")
        pe.wait_ge(*at("x layer1"))
        for c in range(NC):
            for i in range(2):
                key = f"res{c}{i}"
                b = bank(pe, key)
                for j in range(4):
                    ins = pe.transpose(b[:, j * P:(j + 1) * P], xT[:, 4 * i + j, c * P:(c + 1) * P], ident[:, :])
                ins.then_inc(*PE.step("full " + key))

    def act_result(act):
        AC.stage("result")
        act.wait_ge(*at("ffn read1"))
        for c in range(NC):
            for i in range(2):
                key = f"res{c}{i}"
                act.wait_ge(*at("full " + key))
                b = bank_of(key)
                act.copy(otok[:, c, 512 * i:512 * i + 512], b[:, :]).then_inc(*AC.step("free " + key, f"result{c}{i}"))

    scrc, scrx = view(scr, 0, P, KD, N), view(scr, 2048, P, KD, N)
    n_ctx = norm("hc", ctxT, N, hcx[:, :, 0:N], gsC, adaC[:, 0:8], ("turnc in", "spectra", "columns", "gain c"), scrc)
    n_x = norm("hx", xT, N, hcx[:, :, N:2 * N], gs, adaX[0][:, 0:8], ("turnx in", "spectra", "columns", "gain mix0"), scrx)
    n_ffn0 = norm("h ffn0", xT, N, h2, gs, adaX[0][:, 24:32], ("x mixed0", "gain ffn0"), scrx)
    n_fin = norm("fin", xT, N, xT, c_fin, None, ("x moe",), scrx)
    n_mix = [norm(f"h mix{l + 1}", xT, N, h2, gs, adaX[l + 1][:, 0:8], (("fin done", "x layer0")[l], f"gain mix{l + 1}"),
                  scrx) for l in range(LAYERS)]
    n_ffn = [norm(f"h ffn{l + 1}", xT, N, h2, gs, adaX[l + 1][:, 24:32], (f"x mixed{l + 1}", f"gain ffn{l + 1}"), scrx)
             for l in range(LAYERS)]
    m_out = [mixer_out(0, "branch_hy0", "branch_ml0", "out1_", sgo, adaX[0], "adaX0b")]
    m_out += [mixer_out(l + 1, f"upa{l}_0", f"upb{l}_0", f"out2_{l}", yT2[:, 4:8], adaX[l + 1], f"ada2{l}")
              for l in range(LAYERS)]

    both = [(0, adaX[0]), (1, adaC)]
    plan = [
        (act_loads, "act"), (pe_filter, "pe"), (act_filter, "act"), (dve_filter, "dve"),
        (pe_tables, "pe"), (act_tables, "act"), (dve_tables, "dve"),
        (lambda q: pe_turn_in(q, "turnx", xin, xT), "pe"), (lambda q: act_turn_in(q, "turnx", xT), "act"),
        (lambda q: pe_turn_in(q, "turnc", cin, ctxT), "pe"), (lambda q: act_turn_in(q, "turnc", ctxT), "act"),
        (lambda q: pe_ada(q, "adaX0a", "ada_a", 0, 4), "pe"), (lambda q: act_ada(q, "adaX0a", 0, 4), "act"),
        (lambda q: dve_ada(q, "adaX0a", 0, 4, both, c_bada), "dve"),
        (lambda q: dve_gain(q, "gain c", gsC, c_mix[:, 0:8], adaC[:, 8:16], "adaX0a"), "dve"),
        (lambda q: dve_gain(q, "gain mix0", gs, c_mix[:, 0:8], adaX[0][:, 8:16], "adaX0a"), "dve"),
        (n_ctx[0], "pe"), (n_x[0], "pe"), (n_ctx[1], "act"), (n_x[1], "act"), (n_ctx[2], "dve"), (n_x[2], "dve"),
        (pe_project, "pe"), (act_project, "act"), (dve_project, "dve"),
        (pe_mlstm, "pe"), (act_mlstm, "act"), (dve_mlstm, "dve"),
        (pe_hyena, "pe"), (act_hyena, "act"), (dve_hyena, "dve"),
        (lambda q: pe_ada(q, "adaX0b", "ada_b", 4, 8), "pe"), (lambda q: act_ada(q, "adaX0b", 4, 8), "act"),
        (lambda q: dve_ada(q, "adaX0b", 4, 8, both[:1], c_bada), "dve"),
        (m_out[0][0], "pe"), (m_out[0][1], "dve"),
        (act_moe_loads, "act"),
        (lambda q: dve_gain(q, "gain ffn0", gs, c_ffn[:, 0:8], adaX[0][:, 32:40], "adaX0b"), "dve"),
        (n_ffn0[0], "pe"), (n_ffn0[1], "act"), (n_ffn0[2], "dve"),
        (pe_route, "pe"), (act_route, "act"), (dve_route, "dve"),
    ]
    for l in range(LAYERS):
        bias = C2[:, 48 * l:48 * l + 48]
        plan += [(lambda q, l=l: pe_ada(q, f"ada2{l}", f"ada2_{l}", 0, 12), "pe"),
                 (lambda q, l=l: act_ada(q, f"ada2{l}", 0, 12), "act"),
                 (lambda q, l=l, bias=bias: dve_ada(q, f"ada2{l}", 0, 12, [(2, adaX[l + 1])], bias), "dve")]
    plan += [
             (pe_experts, "pe"), (act_experts, "act"), (dve_experts, "dve"),
             (act_second_loads, "act"), (pe_rope, "pe"), (act_rope, "act"), (dve_rope, "dve"),
             (n_fin[0], "pe"), (n_fin[1], "act"), (n_fin[2], "dve")]
    for l in range(LAYERS):
        plan += [
            (lambda q, l=l: dve_gain(q, f"gain mix{l + 1}", gs, c_mix2[:, 8 * l:8 * l + 8], adaX[l + 1][:, 8:16],
                                     f"ada2{l}"), "dve"),
            (n_mix[l][0], "pe"), (n_mix[l][1], "act"), (n_mix[l][2], "dve"),
            (lambda q, l=l: pe_in(q, l), "pe"), (lambda q, l=l: act_in(q, l), "act"),
            (lambda q, l=l: pe_compress(q, l), "pe"), (lambda q, l=l: pe_gates2(q, l), "pe"),
            (lambda q, l=l: act_compress(q, l), "act"), (lambda q, l=l: act_gates2(q, l), "act"),
            (lambda q, l=l: dve_in(q, l), "dve"), (lambda q, l=l: dve_compress(q, l), "dve"),
            (lambda q, l=l: pe_heads(q, l), "pe"), (lambda q, l=l: act_heads(q, l), "act"),
            (lambda q, l=l: dve_heads(q, l), "dve"),
            (lambda q, l=l: pe_attend(q, l), "pe"), (lambda q, l=l: act_attend(q, l), "act"),
            (lambda q, l=l: dve_attend(q, l), "dve"),
            (m_out[l + 1][0], "pe"), (m_out[l + 1][1], "dve"),
            (lambda q, l=l: dve_gain(q, f"gain ffn{l + 1}", gs, c_ffn2[:, 8 * l:8 * l + 8], adaX[l + 1][:, 32:40]), "dve"),
            (n_ffn[l][0], "pe"), (n_ffn[l][1], "act"), (n_ffn[l][2], "dve"),
            (lambda q, l=l: pe_ffn(q, l), "pe"), (lambda q, l=l: act_ffn(q, l), "act"),
            (lambda q, l=l: dve_ffn(q, l), "dve")]
    plan += [(pe_result, "pe"), (act_result, "act")]

    def stages(eng, Q):
        for part, engine in plan:
            if engine == Q.engine:
                part(eng)

    @block.tensor
    def _(eng):
        stages(eng, PE)

    @block.scalar
    def _(eng):
        stages(eng, AC)

    @block.vector
    def _(eng):
        stages(eng, DV)

    @block.sync
    def _(sp):
        SP.stage("sync")

        def load(sem, dst, src):
            sp.dma_start(dst, src).then_inc(*K.load(sem))

        def one(n, item):
            _, (src, parts, a, b) = item
            if n >= RING:
                old = n - RING
                if N_PRE <= old < POST0:
                    sp.wait_ge(*at(f"expert used{(old - N_PRE) % N_EXP}"))
                else:
                    sp.wait_ge(*at(f"used {old}"))
            sp.dma_start(place(n, parts, a, b), src).then_inc(tile_sem(n), 16)

        for n in range(2):
            one(n, stream[n])
        load("load_x", xin, A["x"][0].rearrange("(c p) n -> p c n", p=P))
        load("load_x", cin, A["ctx"][0].rearrange("(c p) n -> p c n", p=P))
        load("load_ml", bvrow, A["b_in"][0:1, ML0 + 1024:ML0 + 1536])
        for n in range(2, N_PRE):
            one(n, stream[n])

        def expert_tile(i, t):
            n = N_PRE + t
            if t < 8:
                w = A["w_exp1" if t < 4 else "w_exp3"][0][i]
                src = w[256 * (t % 4):256 * (t % 4) + 256, :].rearrange("(k p) n -> p k n", p=P)
                dst = place(n, P, 2, 4 * 512)
            else:
                src = A["w_exp2"][0][i][512 * (t - 8):512 * (t - 8) + 512, :].rearrange("(k p) n -> p k n", p=P)
                dst = place(n, P, 4, D)
            sp.dma_start(dst, src).then_inc(tile_sem(n), 16)

        for t in range(RING):
            sp.wait_ge(*at(f"used {N_PRE + t - RING}"))
            expert_tile(0, t)
        with sp.Fori(0, EXPERTS - 1) as i:
            K.turn = i
            for t in range(RING, N_EXP):
                sp.wait_ge(*at(f"expert used{t - RING}"))
                expert_tile(i, t)
            for t in range(RING):
                sp.wait_ge(*at(f"expert used{N_EXP - RING + t}"))
                expert_tile(i + 1, t)
        K.turn = None
        for t in range(RING, N_EXP):
            sp.wait_ge(*at(f"expert used{t - RING}"))
            expert_tile(EXPERTS - 1, t)
        for i, item in enumerate(after_experts):
            one(POST0 + i, item)
        for c in range(NC):
            for i in range(2):
                sp.wait_ge(*at(f"result{c}{i}"))
                sp.dma_start(out[0, c * P:(c + 1) * P, 512 * i:512 * i + 512],
                             otok[:, c, 512 * i:512 * i + 512]).then_inc(*K.load("stored"))
        sp.wait_ge(*K.loaded("stored"))

    book.loads = K.loads


def constants():
    f32 = lambda a: np.ascontiguousarray(a, dtype=np.float32)
    L = N
    t = np.linspace(0.0, 1.0, L)
    bands = np.linspace(1e-4, 15, 16)
    an = (2.0 * np.pi / L) * np.arange(L)[:, None] * bands[None, :]
    z = np.concatenate([t[:, None], np.cos(an), np.sin(an)], axis=1)
    lo, hi = np.log(1e-2) / 1.5, np.log(1e-2) / 0.3
    dec = np.exp(-t[:, None] * np.abs(np.linspace(lo, hi, HY))[None, :])
    dec2 = dec.copy()
    dec2[0] = 0.0
    w = 2 * np.pi * np.outer(np.arange(L), np.arange(L)) / (2 * L)
    cos, msin = np.cos(w), -np.sin(w)
    nyq = np.cos(np.pi * np.arange(L))
    msin_u = msin.copy()
    msin_u[:, 0] = nyq
    msin_k, cos_k = msin[:, 0:128].copy(), cos[:, 0:128].copy()
    msin_k[:, 0] = 0.0
    cos_k[:, 0] = nyq
    inv_r, inv_i = 2 * np.cos(w).T / (2 * L), -2 * np.sin(w).T / (2 * L)
    inv_r[0] /= 2
    inv_i[0] = nyq / (2 * L)
    chunks = lambda a: a.reshape(2, P, *a.shape[1:]).swapaxes(0, 1)
    s, tt = np.arange(P)[:, None], np.arange(P)[None, :]
    fwd, bwd = np.where(s <= tt, 0.0, BIG), np.where(s >= tt, 0.0, BIG)
    zero = np.zeros((P, P))
    mask = np.stack([np.concatenate([fwd, zero], 1), np.concatenate([zero, bwd], 1)], 1)
    selh = np.zeros((4, 4, P))
    for h in range(4):
        selh[h, h] = 1.0
    causal = np.concatenate([zero, np.where(tt <= s, 0.0, NEG)], 1)
    ends = 16 * np.arange(16) + 31
    tok = np.arange(N)
    cm = np.where((ends[None, :] <= tok[:, None]) & (np.arange(16) < NCMP)[None, :], 0.0, NEG)
    inv = 1.0 / (10000.0 ** (np.arange(0, HD, 2, dtype=np.float32) / np.float32(HD)))
    return {
        "k_zT": f32(z.T), "k_decay": f32(chunks(np.stack([dec, dec2], 1))), "k_dftc": f32(chunks(cos)),
        "k_dfts": f32(chunks(msin_u)), "k_dftn": f32(chunks(np.stack([msin_k, cos_k], 1))),
        "k_idft": f32(np.concatenate([inv_r, inv_i], 0).reshape(4, P, N).swapaxes(0, 1)),
        "k_ident": f32(np.eye(P)), "k_mask": f32(mask), "k_selh": f32(selh), "k_causal": f32(causal),
        "k_cmask": f32(chunks(cm)), "k_valid": f32(chunks((tok >= 31).astype(float))),
        "k_inv": f32(np.broadcast_to(inv, (P, 32))), "k_iota": f32(np.broadcast_to(np.arange(CAP), (P, CAP))),
        "k_slot": f32((np.arange(P) % CAP)[:, None]),
    }


def kernel(**inputs):
    import concourse.bacc as bacc
    from concourse.bass_utils import run_bass_kernel_spmd

    arrays = {f"in_{k}": np.ascontiguousarray(v) for k, v in inputs.items()}
    arrays.update({f"in_{k}": v for k, v in constants().items()})

    book = Book()
    for turn in range(2):
        nc = bacc.Bacc("TRN2", target_bir_lowering=False, num_devices=1, dynamic_dma_scratch_size=1024)
        A = {k[3:]: nc.dram_tensor(k, v.shape, mybir.dt.from_np(v.dtype), kind="ExternalInput").ap()
             for k, v in arrays.items()}
        out = nc.dram_tensor("out_0", (1, N, D), F32, kind="ExternalOutput").ap()
        build(nc, A, out, book)
        book.known = True
    r = run_bass_kernel_spmd(nc, [arrays], core_ids=[0])
    return r.results[0]["out_0"]
```

```python
from contextlib import ExitStack

import numpy as np

import concourse.bass as bass
from concourse import mybir

F32 = mybir.dt.float32
I32 = mybir.dt.int32
ALU = mybir.AluOpType
ACT = mybir.ActivationFunctionType
AX = mybir.AxisListType.X

P = 128
N = 256
NC = N // P
D = 1024
KD = D // P
EPS = 1e-6
HY = 512
HEADS, DH = 4, 128
ML0, GATE0, MERGE0, IN1 = 1536, 3584, 3600, 5648
EXPERTS, CAP, FF1 = 16, 32, 2048
LAYERS = 2
HD = 64
KV0, KW0, QB0, GATES2, MERGE2, IN2 = 512, 1024, 1304, 1280, 2840, 4888
NCMP = N // 16 - 1
FF2 = 2816
FB = FF2 // P
NEG = -1e30
BIG = 1e30
RING, TILE = 4, 4096


class Book:

    def __init__(self):
        self.where, self.per, self.bank, self.loads, self.known = {}, {}, {}, {}, False


class Steps:

    def __init__(self, engine, k):
        self.engine, self.k, self.count, self.cur, self.now = engine, k, {}, None, None

    def stage(self, stage):
        self.cur = f"{stage}_{self.engine}"
        self.count.setdefault(self.cur, 0)

    def step(self, *names):
        self.count[self.cur] += 1
        self.now = (self.cur, self.count[self.cur])
        for n in names:
            self.k.book.where[n] = self.now
        return self.k.sem(self.cur), 1

    def last(self):
        return self.k.value(*self.now)


class Kernel:
    def __init__(self, nc, ctx, book):
        self.nc, self.ctx, self.book, self.sems, self.turn = nc, ctx, book, {}, None
        self.loads = {}

    def sem(self, name):
        if name not in self.sems:
            self.sems[name] = self.ctx.enter_context(self.nc.semaphore(name))
        return self.sems[name]

    def load(self, name):
        self.loads[name] = self.loads.get(name, 0) + 16
        return self.sem(name), 16

    def loaded(self, name):
        return self.sem(name), self.book.loads.get(name, 16)

    def at(self, name, back=0):
        if not self.book.known:
            return self.value(*next(iter(self.book.where.values())), back)
        return self.value(*self.book.where[name], back)

    def value(self, sem, count, back=0):
        if not sem.startswith("expert_"):
            return self.sem(sem), count
        per = self.book.per.get(sem, 1)
        if self.turn is None:
            return self.sem(sem), EXPERTS * per + count
        return self.sem(sem), self.turn * per + (count + (1 - back) * per)


def view(t, off, parts, *dims):
    n = int(np.prod(dims))
    v = t[0:parts, off:off + n]
    if len(dims) == 2:
        return v.rearrange("p (a b) -> p a b", a=dims[0])
    if len(dims) == 3:
        return v.rearrange("p (a b c) -> p a b c", a=dims[0], b=dims[1])
    if len(dims) == 4:
        return v.rearrange("p (a b c d) -> p a b c d", a=dims[0], b=dims[1], c=dims[2])
    return v


def spread(ap, axis, n):
    u = ap.unsqueeze(axis)
    shape = list(u.shape)
    shape[axis] = n
    return u.broadcast_to(shape)


def build(nc, A, out, book):
    ctx = ExitStack()
    with ctx:
        program(nc, ctx, A, out, book)


def program(nc, ctx, A, out, book):
    K = Kernel(nc, ctx, book)
    at = K.at
    PE, AC, DV, SP = (Steps(n, K) for n in ("pe", "act", "dve", "sp"))

    def sb(name, n, parts=P):
        return ctx.enter_context(nc.sbuf_tensor(name, [parts, n], F32))

    ring = sb("ring", RING * TILE)
    xT = view(sb("xT", KD * N), 0, P, KD, N)
    hx = sb("hx", KD * 2 * N)
    scr = sb("scr", KD * 2 * N)
    mg = sb("mg", KD * 2 * N)
    arena = sb("arena", 24504)
    ident, ones = sb("ident", P), sb("ones", N)
    cols = sb("cols", 320)
    ada = sb("ada", 3 * 48 + 16)
    small = sb("small", 460)
    banks = [ctx.enter_context(nc.psum_tensor(f"bank{i}", [P, 512], F32)) for i in range(8)]

    hcx = view(hx, 0, P, KD, 2 * N)
    h2 = view(hx, 0, P, KD, N)
    cmpx = view(hx, KD * N, HD, 4, 2, N)
    gates = view(mg, 0, P, KD, 2, N)
    C0, C1, C2 = cols[:, 0:104], cols[:, 104:212], cols[:, 212:308]
    c_bhy, c_bq, c_bk, c_bo, c_bm, c_hyw, c_mlw = (C0[:, i:] for i in (0, 12, 16, 24, 28, 44, 80))
    c_mix, c_ffn, c_mln, c_fin, c_mix2, c_ffn2, c_bada = (C1[:, i:] for i in (0, 8, 16, 20, 28, 44, 60))
    adaX = [ada[:, 48 * i:48 * i + 48] for i in range(3)]
    adaC = ada[:, 144:160]
    gs = small[:, 0:8]
    gsC = small[:, 8:16]
    cT = view(small, 16, P, KD, 32)
    tokc = view(small, 272, P, 3, 2, 2, 4)
    m0c = view(small, 320, P, 4, 2)
    w4 = small[:, 328:460]

    dftc = view(arena, 0, P, 2, 256)
    dfts = view(arena, 512, P, 2, 256)
    idft = view(arena, 1024, P, 4, 256)
    spec = view(arena, 2048, P, 2, 5, HY)
    hyt = view(arena, 7168, P, NC, 3 * HY)
    kq = view(arena, 10240, P, 2, 4, N)
    vx = view(arena, 12288, P, NC, 4, 130)
    cst = view(arena, 13328, P, 4, 2, 130)
    sgo = view(arena, 14368, P, 4, N)
    mask = view(arena, 15392, P, 2, N)
    selh = view(arena, 15904, 4, 4, P)
    wgate = view(arena, 16416, P, KD, 16)
    bgate = arena[0:16, 16544:16545]
    adarow = view(arena, 16548, P, 2, P)
    pre = view(arena, 16804, P, 2, 4, N)
    post = view(arena, 18852, P, 2, 4, N)
    bvrow = arena[0:1, 23992:24504]
    ctxT = view(arena, 16804, P, KD, N)
    cin = view(arena, 18852, P, NC, D)
    xin = view(arena, 20900, P, NC, D)
    r_g = view(arena, 20900, 4, 2, 2 * N)
    r_t = view(arena, 21924, 4, 2, 2 * N)
    r_M = view(arena, 22948, 4, 2, N)
    r_s = view(arena, 23460, 4, 8, 2)
    gate16 = arena[0:16, 23480:23992]
    r_gate = view(scr, 0, 4, 4, 2 * N)
    r_lf = view(scr, 2048, 4, 2, 2 * N)
    r_b = view(scr, 3072, 4, 2, 2 * N)
    kc = view(mg, 0, P, 4, N)
    vc = view(mg, 1024, P, NC, 4, 130)
    kw = view(scr, 0, P, NC, 2, 4, P)
    U = arena[:, 16804:17572]
    Aw = arena[:, 17572:18340]
    ai = view(arena, 18852, P, 2, N)
    qi = view(arena, 19364, P, 2, N)
    hh = view(arena, 19876, P, NC, 4, P)
    Yf = view(scr, 0, P, 4, HY)
    zc = view(scr, 2048, P, NC, HY)
    t1, t2 = scr[:, 3072:3584], scr[:, 3584:4096]
    yaT = view(arena, 10240, P, 4, N)
    dftn = view(arena, 10240, P, 2, 2, 128)
    decay = view(arena, 10752, P, 2, 2, HY)
    zT = arena[0:33, 12800:13056]
    fw1, fw2 = arena[0:33, 13056:13120], arena[0:64, 13120:13184]
    fb = arena[0:64, 13184:13186]
    hid = view(arena, 13200, 64, 4, N)
    fw3 = view(scr, 0, 64, 4, HY)
    hfil = view(mg, 0, P, 2, 4, HY)
    hsd = [[view(arena, off, P, 2, HY) for off in offs] for offs in ((7168, 8192), (9216, 22948))]
    skips = arena[0:1, 14368:15392]
    tab = view(scr, 2048, P, 4, P)

    stream = []

    def tiles(key, aps):
        stream.extend((f"{key}{i}", ap) for i, ap in enumerate(aps))

    def wide(w, lo, hi):
        return [(w[:, c:min(c + 512, hi)].rearrange("(k p) n -> p k n", p=P), P, KD, min(512, hi - c))
                for c in range(lo, hi, 512)]

    def deep(w, lo, hi):
        return [(w[r:min(r + 512, hi), :].rearrange("(k p) n -> p k n", p=P), P, (min(r + 512, hi) - r) // P, D)
                for r in range(lo, hi, 512)]

    w_in, w_ada = A["w_in"][0], A["w_ada"][0]
    later = list(wide(w_ada, 2048, 6144))
    for l in range(LAYERS):
        later += wide(A["w_ada_2"][l], 0, 6144)

    def tiles_and_ada(key, aps):
        tiles(key, aps)
        n = sum(k.startswith("later") for k, _ in stream)
        stream.extend((f"later{i}", later[i]) for i in range(n, n + 2))

    tiles("ada_a", wide(w_ada, 0, 2048))
    tiles("k", wide(w_in, ML0 + 512, ML0 + 1024))
    tiles("v", wide(w_in, ML0 + 1024, ML0 + 1536))
    tiles_and_ada("q", wide(w_in, ML0, ML0 + 512))
    for t in range(3):
        tiles_and_ada(f"hy{t}", wide(w_in, 512 * t, 512 * t + 512))
    tiles_and_ada("o", wide(w_in, ML0 + 1536, ML0 + 2048))
    for t in range(4):
        tiles_and_ada(f"merge1_{t}", wide(w_in, MERGE0 + 512 * t, MERGE0 + 512 * t + 512))
    for t in range(4 + 3):
        tiles_and_ada("", [])
    tiles("branch_hy", deep(A["w_branch_hy"][0], 0, 512))
    tiles("branch_ml", deep(A["w_branch_ml"][0], 0, 512))
    tiles("out1_", wide(A["w_out"][0], 0, D))
    N_PRE = len(stream)
    N_EXP = 12
    after_experts = []

    def tiles2(key, aps):
        after_experts.extend((f"{key}{i}", ap) for i, ap in enumerate(aps))

    for l in range(LAYERS):
        w2 = A["w_in_2"][l]
        tiles2(f"in{l}_", wide(w2, 0, KW0) + [(w2[:, KW0:QB0].rearrange("(k p) n -> p k n", p=P), P, KD, QB0 - KW0)]
               + wide(w2, QB0, MERGE2))
        merge = wide(w2, MERGE2, IN2)
        for t in range(4):
            if t == 2:
                for n in "kv":
                    w = A[f"nsa_cmp_{n}_w1_2"][l].rearrange("(j d) h -> d j h", d=HD)
                    tiles2(f"cmp{n}{l}_", [(w, HD, 32, P)])
            tiles2(f"merge2_{l}{t}", merge[t:t + 1])
        tiles2(f"upa{l}_", deep(A["w_up_nsa_2"][l], 0, 512))
        tiles2(f"upb{l}_", deep(A["w_up_moba_2"][l], 0, 512))
        tiles2(f"out2_{l}", wide(A["w_out_2"][l], 0, D))
        wf = A["w_ffn_in_2"][l]
        gt, up = wide(wf, 0, FF2), wide(wf, FF2, 2 * FF2)
        for i in range(len(gt)):
            tiles2(f"gt{l}_{i}_", gt[i:i + 1])
            tiles2(f"up{l}_{i}_", up[i:i + 1])
        tiles2(f"down{l}_", deep(A["w_ffn_out_2"][l], 0, FF2))

    POST0 = N_PRE + EXPERTS * N_EXP
    where = {key: i for i, (key, _) in enumerate(stream)}
    where.update({key: POST0 + i for i, (key, _) in enumerate(after_experts)})

    def slot(n):
        return n % RING

    def tile_sem(n):
        return K.sem(f"tile_slot{slot(n)}")

    def place(n, parts, a, b):
        return view(ring, slot(n) * TILE, parts, a, b)

    def tile(pe, key):
        n = where[key]
        _, parts, a, b = (stream[n] if n < N_PRE else after_experts[n - POST0])[1]
        pe.wait_ge(tile_sem(n), 16 * (n // RING + 1))
        return place(n, parts, a, b)

    block = ctx.enter_context(nc.Block())

    owner = {}

    def claim(pe, b, key):
        if b in owner:
            pe.wait_ge(*at("free " + owner[b]))
        owner[b] = key
        return banks[b]

    turn = {"w": 0}

    def bank(pe, key):
        b = turn["w"] % 6
        turn["w"] += 1
        book.bank[key] = b
        return claim(pe, b, key)

    def bank_of(key):
        return banks[book.bank.get(key, 0)]

    def act_loads(act):
        def load(sem, dst, src):
            act.dma_start(dst, src).then_inc(*K.load(sem))

        def rowload(j, r, src, n):
            load("load_tables", tab[r:r + n, j, :], src.rearrange("(r p) -> r p", p=P))

        load("load_filter", zT, A["k_zT"])
        load("load_filter", fw1, A["hy_f_w1"][0])
        load("load_filter", fw2, A["hy_f_w2"][0])
        load("load_filter", fb[:, 0:1], A["hy_f_b1"][0].rearrange("(p a) -> p a", a=1))
        load("load_filter", fb[:, 1:2], A["hy_f_b2"][0].rearrange("(p a) -> p a", a=1))
        load("load_filter", ident[:, :], A["k_ident"])
        load("load_filter", fw3, A["hy_f_w3"][0].rearrange("k (a n) -> k a n", a=4))
        rowload(3, 0, A["c"][0], 8)
        rowload(3, 8, A["c_ctx"], 8)
        rowload(3, 16, A["c_2"][0], 8)
        b_in = A["b_in"][0]
        rowload(0, 0, b_in[0:3584], 28)
        rowload(0, 28, b_in[MERGE0:IN1], 16)
        load("load_tables", tab[44:80, 0, :], A["hy_conv"][0].rearrange("j (b p) -> (j b) p", p=P))
        load("load_tables", tab[80:104, 0, :], A["ml_conv"][0].rearrange("j (b p) -> (j b) p", p=P))
        rowload(1, 0, A["norm_mix_g"][0], 8)
        rowload(1, 8, A["norm_ffn_g"][0], 8)
        rowload(1, 16, A["ml_norm_g"][0], 4)
        rowload(1, 20, A["final_norm_g"], 8)
        load("load_tables", tab[28:44, 1, :], A["norm_mix_2"].rearrange("l (r p) -> (l r) p", p=P))
        load("load_tables", tab[44:60, 1, :], A["norm_ffn_2"].rearrange("l (r p) -> (l r) p", p=P))
        rowload(1, 60, A["b_ada"][0], 48)
        load("load_tables", tab[0:96, 2, :], A["b_ada_2"].rearrange("l (r p) -> (l r) p", p=P))
        load("load_dft", decay, A["k_decay"])
        load("load_dft", skips, A["hy_skip"].rearrange("a o n -> a (o n)"))
        load("load_dft", dftc, A["k_dftc"])
        load("load_dft", dfts, A["k_dfts"])
        load("load_dft", dftn, A["k_dftn"])
        load("load_dft", idft, A["k_idft"])
        load("load_ml", mask, A["k_mask"])
        load("load_ml", selh, A["k_selh"])
        load("load_ml", wgate, A["w_in"][0][:, GATE0:MERGE0].rearrange("(k p) n -> p k n", p=P))
        load("load_ml", bgate, b_in[GATE0:MERGE0].rearrange("(p a) -> p a", a=1))

    def dve_reduce(v, r, x, k, quarter=False):
        TURN = 2 * np.pi
        c1 = 6.28125
        c2 = float(np.float32(round((TURN - c1) * 2 ** 20) / 2 ** 20))
        c3 = TURN - c1 - c2
        v.tensor_scalar(k, x, 1 / TURN, 0.25 if quarter else 0.0, ALU.mult, ALU.add).then_inc(*DV.step())
        v.wait_ge(*DV.last())
        v.tensor_scalar(k, k, 12582912.0, 12582912.0, ALU.add, ALU.subtract).then_inc(*DV.step())
        src = x
        for c in (c1, c2, c3):
            v.wait_ge(*DV.last())
            v.scalar_tensor_tensor(r, k, -c, src, ALU.mult, ALU.add).then_inc(*DV.step())
            src = r
        if quarter:
            v.wait_ge(*DV.last())
            v.tensor_scalar(r, r, np.pi / 2, None, ALU.add).then_inc(*DV.step())
        v.wait_ge(*DV.last())
        return v.tensor_scalar(r, r, 3.1415925, -3.1415925, ALU.min, ALU.max).then_inc(*DV.step())

    def pe_filter(pe, i):
        PE.stage("filter")
        pe.wait_ge(*K.loaded("load_filter"))
        if i:
            pe.wait_ge(*at("filter sin0"))
        b = bank(pe, f"filter{i}")
        pe.matmul(b[0:64, 0:N], (fw1, fw2)[i], (zT, hid[:, 1, :])[i], start=True, stop=True).then_inc(
            *PE.step(f"full filter{i}"))

    def pe_filter_taps(pe):
        PE.stage("filter")
        pe.wait_ge(*at("filter sin1"))
        for c in range(NC):
            for a in range(4):
                key = f"filter h{c}{a}"
                b = bank(pe, key)
                pe.matmul(b[:, :], hid[:, 3, c * P:(c + 1) * P], fw3[:, a, :], start=True, stop=True).then_inc(
                    *PE.step("full " + key))

    def pe_spectra(pe):
        PE.stage("filter")
        for o in range(2):
            for i, (m, sd) in enumerate(((lambda c: dftc[:, c, 0:128], 0), (lambda c: dftc[:, c, 128:256], 0),
                                         (lambda c: dftn[:, c, 0, :], 1), (lambda c: dfts[:, c, 128:256], 1),
                                         (lambda c: dftn[:, c, 1, :], 0))):
                if o == 0 and i == 0:
                    pe.wait_ge(*at("filter sums"))
                key = f"spec{o}{i}"
                b = bank(pe, key)
                for c in range(NC):
                    ins = pe.matmul(b[:, :], m(c), hsd[c][o][:, sd, :], start=c == 0, stop=c == NC - 1)
                ins.then_inc(*PE.step("full " + key))

    def act_filter(act, i):
        AC.stage("filter")
        act.wait_ge(*at(f"filter reduced{i}"))
        act.activation(hid[:, 2 * i + 1, :], hid[:, 2 * i, :], ACT.Sin).then_inc(*AC.step(f"filter sin{i}"))

    def act_spectra(act):
        AC.stage("filter")
        for o in range(2):
            for i in range(5):
                key = f"spec{o}{i}"
                act.wait_ge(*at("full " + key))
                b = bank_of(key)
                act.copy(spec[:, o, i, :], b[:, :]).then_inc(*AC.step("free " + key, "spectra"))

    def dve_filter(v, i):
        DV.stage("filter")
        v.wait_ge(*K.loaded("load_filter"))
        v.wait_ge(*at(f"full filter{i}"))
        b = bank_of(f"filter{i}")
        x = hid[:, 2 * i, :]
        v.tensor_scalar(x, b[0:64, 0:N], fb[:, i:i + 1], None, ALU.add).then_inc(*DV.step(f"free filter{i}"))
        v.wait_ge(*DV.last())
        dve_reduce(v, x, x, hfil[0:64, 0, 0, 0:N])
        book.where[f"filter reduced{i}"] = DV.now

    def dve_filter_taps(v):
        DV.stage("filter")
        v.wait_ge(*K.loaded("load_dft"))
        for c in range(NC):
            for a in range(4):
                key = f"filter h{c}{a}"
                v.wait_ge(*at("full " + key))
                b = bank_of(key)
                v.tensor_tensor(hfil[:, c, a, :], b[:, :], decay[:, c, a % 2, :], ALU.mult).then_inc(*DV.step("free " + key))
        v.wait_ge(*DV.last())
        for c in range(NC):
            for o in range(2):
                v.tensor_tensor(hsd[c][o][:, 0, :], hfil[:, c, 2 * o, :], hfil[:, c, 2 * o + 1, :], ALU.add).then_inc(*DV.step())
                v.tensor_tensor(hsd[c][o][:, 1, :], hfil[:, c, 2 * o, :], hfil[:, c, 2 * o + 1, :],
                                          ALU.subtract).then_inc(*DV.step())
        v.wait_ge(*DV.last())
        for o in range(2):
            v.tensor_tensor(hsd[0][o][0:1, 0, :], hsd[0][o][0:1, 0, :], skips[:, o * HY:(o + 1) * HY],
                                      ALU.add).then_inc(*DV.step("filter sums"))

    def pe_tables(pe):
        PE.stage("tables")
        pe.wait_ge(*K.loaded("load_tables"))
        pe.wait_ge(*at("silu c"))
        b = bank(pe, "tables")
        for j, n in enumerate((104, 108, 96)):
            pe.transpose(b[:, (0, 104, 212)[j]:(0, 104, 212)[j] + n], tab[0:n, j, :], ident[0:n, 0:n])
        pe.transpose(b[:, 320:344], tab[0:24, 3, :], ident[0:24, 0:24]).then_inc(*PE.step("full tables"))

    def act_tables(act):
        AC.stage("tables")
        act.wait_ge(*K.loaded("load_tables"))
        act.activation(tab[0:24, 3, :], tab[0:24, 3, :], ACT.Silu).then_inc(*AC.step("silu c"))

    def dve_tables(v):
        DV.stage("tables")
        v.wait_ge(*at("full tables"))
        b = bank_of("tables")
        v.wait_ge(*DV.last())
        v.tensor_copy(cT[:, :, 0:3], b[:, 320:344].rearrange("p (m k) -> p k m", m=3)).then_inc(*DV.step("c columns"))
        v.tensor_copy(cols[:, 0:308], b[:, 0:308]).then_inc(*DV.step("free tables", "columns"))

    def pe_ada(pe, name, key, tile0, n):
        PE.stage("ada")
        pe.wait_ge(*at("c columns"))
        for t in range(n):
            w = tile(pe, f"{key}{t}")
            b = bank(pe, f"{name} row{tile0 + t}")
            for k in range(KD):
                for j in range(4):
                    ins = pe.matmul(b[32 * j:32 * j + 32, 0:P], cT[:, k, :], w[:, k, j * P:(j + 1) * P],
                                        start=k == 0, stop=k == KD - 1)
            ins.then_inc(*PE.step(f"full {name} row{tile0 + t}"))
            mark_used(pe, f"{key}{t}")
            if t:
                ada_turn(pe, name, tile0 + t - 1)
        ada_turn(pe, name, tile0 + n - 1)

    def ada_turn(pe, name, t):
        pe.wait_ge(*at(f"{name} rows{t}"))
        b = bank(pe, f"{name} col{t}")
        pe.transpose(b[:, 0:P], adarow[:, t % 2, :], ident[:, :]).then_inc(*PE.step(f"full {name} col{t}"))


    ada_cols = []

    def act_ada(act, name, tile0, n):
        AC.stage("ada")
        for t in range(tile0, tile0 + n):
            act.wait_ge(*at(f"full {name} row{t}"))
            b = bank_of(f"{name} row{t}")
            if len(ada_cols) >= 2:
                act.wait_ge(*at(ada_cols[-2]))
            ada_cols.append(f"full {name} col{t}")
            act.copy(adarow[:, t % 2, :], b[:, 0:P]).then_inc(*AC.step(f"free {name} row{t}", f"{name} rows{t}"))

    def dve_ada(v, name, tile0, n, outs, bias):
        DV.stage("ada")
        v.wait_ge(*at("columns"))
        for t in range(tile0, tile0 + n):
            v.wait_ge(*at(f"full {name} col{t}"))
            b = bank_of(f"{name} col{t}")
            c = b[:, 0:P].rearrange("p (j m) -> p m j", j=4)
            for m, dst in outs:
                v.tensor_tensor(dst[:, 4 * t:4 * t + 4], c[:, m, :], bias[:, 4 * t:4 * t + 4], ALU.add).then_inc(*DV.step(f"free {name} col{t}", name))

    both = [(0, adaX[0]), (1, adaC)]
    adarow4 = arena[:, 23992:24504]
    LATER = ([("adaX0b", 16 + 16 * g, both[:1], c_bada) for g in range(2)]
             + [(f"ada2{l}", 16 * g, [(2, adaX[l + 1])], C2[:, 48 * l:48 * l + 48]) for l in range(LAYERS) for g in range(3)])
    next_later = [0]

    def pe_later(pe):
        stage = PE.cur
        PE.stage("ada")
        for i in range(next_later[0], next_later[0] + 2):
            g = i // 4
            if i % 4 == 0:
                if g:
                    pe_later_turn(pe, g - 1)
                claim(pe, 6, f"later rows{g}")
            w = tile(pe, f"later{i}")
            for k in range(KD):
                for j in range(4):
                    ins = pe.matmul(banks[6][32 * j:32 * j + 32, (i % 4) * P:(i % 4 + 1) * P], cT[:, k, :],
                                    w[:, k, j * P:(j + 1) * P], start=k == 0, stop=k == KD - 1)
            ins.then_inc(*PE.step(f"full later rows{g}"))
            mark_used(pe, f"later{i}")
        next_later[0] += 2
        PE.cur = stage

    def pe_later_turn(pe, g):
        pe.wait_ge(*at(f"later copied{g}"))
        b = claim(pe, 7, f"later cols{g}")
        for i in range(4):
            ins = pe.transpose(b[:, i * P:(i + 1) * P], adarow4[:, i * P:(i + 1) * P], ident[:, :])
        ins.then_inc(*PE.step(f"full later cols{g}"))

    def act_later(act, g):
        act.wait_ge(*at("full v11"))
        if g:
            act.wait_ge(*at(f"full later cols{g - 1}"))
        act.wait_ge(*at(f"full later rows{g}"))
        act.copy(adarow4, banks[6][:, :]).then_inc(*AC.step(f"free later rows{g}", f"later copied{g}"))

    def dve_later(v, g):
        name, first, outs, bias = LATER[g]
        v.wait_ge(*at(f"full later cols{g}"))
        c = banks[7][:, :].rearrange("p (q m) -> p m q", m=32)
        for m, dst in outs:
            v.tensor_tensor(dst[:, first:first + 16], c[:, m, :], bias[:, first:first + 16], ALU.add).then_inc(
                *DV.step(f"free later cols{g}", name))

    def mark_used(pe, key):
        book.where[f"used {where[key]}"] = PE.now

    def pe_turn_in(pe, key, src, dst):
        PE.stage("turn")
        pe.wait_ge(*K.loaded("load_x"))
        for kk in range(KD // 2):
            b = bank(pe, f"{key}{kk}")
            for i in range(2):
                for c in range(NC):
                    o = (i * NC + c) * P
                    ins = pe.transpose(b[:, o:o + P], src[:, c, (2 * kk + i) * P:(2 * kk + i + 1) * P], ident[:, :])
            ins.then_inc(*PE.step(f"full {key}{kk}"))

    def act_turn_in(act, key, dst):
        AC.stage("turn")
        for kk in range(KD // 2):
            act.wait_ge(*at(f"full {key}{kk}"))
            b = bank_of(f"{key}{kk}")
            act.copy(dst[:, 2 * kk:2 * kk + 2, :], b[:, :].rearrange("p (a b) -> p a b", a=2)).then_inc(*AC.step(f"free {key}{kk}", f"{key} in{kk}"))

    def norm(key, src, n, dst, gain, shift, ready, given, sq, rs=None):
        rs = rs_ if rs is None else rs

        def pe_norm(pe):
            PE.stage("norm")
            pe.wait_ge(*at("ones"))
            b = bank(pe, key)
            for k in range(KD):
                pe.wait_ge(*at(f"{key} square{k}"))
                ins = pe.matmul(b[:, 0:n], ones[:, 0:P], sq[:, k, :], start=k == 0, stop=k == KD - 1)
            ins.then_inc(*PE.step(f"full {key}"))

        def act_squares(act):
            AC.stage("norm")
            for k in range(KD):
                act.wait_ge(*at(ready(k)))
                act.activation(sq[:, k, :], src[:, k, :], ACT.Square).then_inc(*AC.step(f"{key} square{k}"))

        def act_root(act):
            AC.stage("norm")
            act.wait_ge(*at(f"{key} mean"))
            act.activation(rs[:, 0:n], rs[:, 0:n], ACT.Sqrt).then_inc(*AC.step(f"{key} root"))

        def act_shift(act):
            AC.stage("norm")
            for k in range(KD):
                act.wait_ge(*at(f"{key} scaled{k}"))
                act.activation(dst[:, k, :], sq[:, k, :], ACT.Identity, bias=shift[:, k:k + 1]).then_inc(
                    *AC.step(f"{key} done{k}", f"{key} done"))

        def act_norm(act):
            act_squares(act)
            act_root(act)
            if shift is not None:
                act_shift(act)

        def dve_mean(v):
            DV.stage("norm")
            v.wait_ge(*at(f"full {key}"))
            b = bank_of(key)
            v.tensor_scalar(rs[:, 0:n], b[:, 0:n], 1.0 / D, EPS, ALU.mult, ALU.add).then_inc(
                *DV.step(f"free {key}", f"{key} mean"))

        def dve_scale(v):
            DV.stage("norm")
            v.wait_ge(*at(f"{key} root"))
            v.reciprocal(rs[:, 0:n], rs[:, 0:n]).then_inc(*DV.step())
            v.wait_ge(*DV.last())
            for step in given:
                v.wait_ge(*at(step))
            out_ = dst if shift is None else sq
            for k in range(KD):
                v.scalar_tensor_tensor(out_[:, k, :], src[:, k, :], gain[:, k:k + 1], rs[:, 0:n], ALU.mult,
                                       ALU.mult).then_inc(*DV.step(f"{key} scaled{k}"))

        def dve_norm(v):
            dve_mean(v)
            dve_scale(v)
        return pe_norm, act_norm, dve_norm, act_squares, act_root, act_shift, dve_mean, dve_scale

    rs_ = sb("rs", N)

    def pe_linear_T(pe, key, tkey, h, n, blocks=4, fresh=None):
        w = tile(pe, tkey)
        per = 512 // n
        for j in range(blocks):
            if j % per == 0:
                b = bank(pe, f"{key}{j // per}")
            o = (j % per) * n
            for k in range(KD):
                if fresh and j == 0:
                    pe.wait_ge(*at(f"{fresh} done{k}"))
                ins = pe.matmul(b[:, o:o + n], w[:, k, j * P:(j + 1) * P], h[:, k, :], start=k == 0, stop=k == KD - 1)
            if j % per == per - 1 or j == blocks - 1:
                ins.then_inc(*PE.step(f"full {key}{j // per}"))
        mark_used(pe, tkey)

    def pe_linear_tok(pe, key, tkey, h, fresh=None):
        w = tile(pe, tkey)
        for c in range(NC):
            b = bank(pe, f"{key}{c}")
            n = w.shape[2]
            for k in range(KD):
                if fresh and c == 0:
                    pe.wait_ge(*at(f"{fresh} done{k}"))
                ins = pe.matmul(b[:, 0:n], h[:, k, c * P:(c + 1) * P], w[:, k, :], start=k == 0, stop=k == KD - 1)
            ins.then_inc(*PE.step(f"full {key}{c}"))
        mark_used(pe, tkey)

    CONV = [("k", 0, c_bk, c_mlw[:, 4:], 8, N), ("k", 1, c_bk, c_mlw[:, 4:], 8, 64),
            ("q", 1, c_bq, c_mlw, 8, 64)] + [(f"hy{t}_", 1, c_bhy[:, 4 * t:], c_hyw[:, 4 * t:], 12, 64) for t in range(3)]

    def pe_project(pe):
        PE.stage("project")
        pe.wait_ge(*K.loaded("load_ml"))
        pe.wait_ge(*at("hc done"))
        pe.wait_ge(*at("hx done"))
        pe_linear_T(pe, "k", "k0", hcx, 512)
        w = tile(pe, "v0")
        for s in range(2):
            for c in range(NC):
                b = bank(pe, f"v{s}{c}")
                for k in range(KD):
                    pe.matmul(b[:, :], hcx[:, k, s * N + c * P:s * N + (c + 1) * P], w[:, k, :], start=k == 0,
                                  stop=False)
                pe.matmul(b[:, :], ones[0:1, 0:P], bvrow, start=False, stop=True).then_inc(*PE.step(f"full v{s}{c}"))
        mark_used(pe, "v0")
        b = bank(pe, "gates")
        for k in range(KD):
            ins = pe.matmul(b[0:16, :], wgate[:, k, :], hcx[:, k, :], start=k == 0, stop=k == KD - 1)
        ins.then_inc(*PE.step("full gates"))
        pe.wait_ge(*at("gates16"))
        for g in range(4):
            b = bank(pe, f"gate{g}")
            pe.matmul(b[0:4, :], ident[0:16, 4 * g:4 * g + 4], gate16, start=True, stop=True).then_inc(*PE.step(f"full gate{g}"))
        x = hcx[:, :, N:2 * N]
        pe_linear_T(pe, "q", "q0", x, N)
        pe_later(pe)
        pe_linear_T(pe, "hy0_", "hy00", x, N)
        pe_later(pe)
        pe_linear_T(pe, "hy1_", "hy10", x, N)
        pe_later(pe)
        pe_context(pe)
        pe_hy_turn(pe, 0)
        pe_linear_T(pe, "hy2_", "hy20", x, N)
        pe_later(pe)
        pe_hy_turn(pe, 1)
        pe_linear_T(pe, "o", "o0", x, N)
        pe_later(pe)
        pe_hy_turn(pe, 2)
        for t in range(4):
            pe_linear_T(pe, f"mergeA{t}_", f"merge1_{t}0", x, N)
            pe_later(pe)

    def act_conv(act, i):
        key, s, bias, _, _, _ = CONV[i]
        if i >= 2:
            act.wait_ge(*at(f"conv{i - 2}"))
        for j in range(4):
            if key == "k":
                act.wait_ge(*at(f"full k{j}"))
                b, o, bk = bank_of(f"k{j}"), s * N, f"k{j}"
            else:
                bk = f"{key}{j // 2}"
                act.wait_ge(*at("full " + bk))
                b, o = bank_of(bk), (j % 2) * N
            act.activation(pre[:, i % 2, j, :], b[:, o:o + N], ACT.Identity, bias=bias[:, j:j + 1]).then_inc(*AC.step(f"pre{i}", "free " + bk))

    def dve_conv(v, i):
        _, _, _, w, pitch, L = CONV[i]
        v.wait_ge(*at(f"pre{i}"))
        if i >= 2:
            v.wait_ge(*at(f"conv read{i - 2}"))
        p = [pre[:, i % 2, j, :].rearrange("p (r l) -> p r l", l=L) for j in range(4)]
        y = [post[:, i % 2, j, :].rearrange("p (r l) -> p r l", l=L) for j in range(4)]
        for j in range(4):
            v.tensor_scalar(post[:, i % 2, j, :], pre[:, i % 2, j, :], w[:, pitch + j:pitch + j + 1], None,
                                      ALU.mult).then_inc(*DV.step())
        v.wait_ge(*DV.last())
        for j in range(4):
            v.scalar_tensor_tensor(y[j][:, :, 1:L], p[j][:, :, 0:L - 1], w[:, j:j + 1], y[j][:, :, 1:L],
                                             ALU.mult, ALU.add).then_inc(*DV.step())
        v.wait_ge(*DV.last())
        for j in range(4):
            v.scalar_tensor_tensor(y[j][:, :, 0:L - 1], p[j][:, :, 1:L],
                                             w[:, 2 * pitch + j:2 * pitch + j + 1], y[j][:, :, 0:L - 1],
                                             ALU.mult, ALU.add).then_inc(*DV.step(f"conv{i}"))

    def act_conv_out(act, i):
        act.wait_ge(*at(f"conv{i}"))
        dst = (kc, kq[:, 0], kq[:, 1])[i]
        act.activation(dst, post[:, i % 2], ACT.Silu).then_inc(*AC.step(f"conv read{i}", ("kc", "k ready", "q ready")[i]))

    def pe_hy_turn(pe, t):
        pe.wait_ge(*at(f"conv{3 + t}"))
        for jj in range(2):
            b = bank(pe, f"hyturn{t}{jj}")
            for c in range(NC):
                for j in range(2):
                    o = (c * 2 + j) * P
                    ins = pe.transpose(b[:, o:o + P], post[:, (3 + t) % 2, 2 * jj + j, c * P:(c + 1) * P], ident[:, :])
            ins.then_inc(*PE.step(f"full hyturn{t}{jj}"))
        book.where[f"conv read{3 + t}"] = PE.now

    def act_hy_turn(act, t):
        for jj in range(2):
            key = f"hyturn{t}{jj}"
            act.wait_ge(*at("full " + key))
            b = bank_of(key)
            act.copy(hyt[:, :, t * HY + jj * 256:t * HY + jj * 256 + 256],
                                 b[:, :].rearrange("p (c n) -> p c n", c=NC)).then_inc(*AC.step("free " + key, "hyena parts"))

    def act_project(act):
        AC.stage("project")
        act.wait_ge(*at("columns"))
        act.wait_ge(*at("hc done"))
        act.wait_ge(*at("hx done"))
        act.wait_ge(*K.loaded("load_ml"))
        act_conv(act, 0)
        act_conv(act, 1)
        for s in range(2):
            for c in range(NC):
                act.wait_ge(*at(f"full v{s}{c}"))
                b = bank_of(f"v{s}{c}")
                act.copy((vc, vx)[s][:, c, :, 0:P], b[:, :].rearrange("p (h e) -> p h e", h=4)).then_inc(*AC.step(f"free v{s}{c}", f"v ready{s}"))
        act.wait_ge(*at("full gates"))
        b = bank_of("gates")
        act.activation(gate16, b[0:16, :], ACT.Identity, bias=bgate).then_inc(*AC.step("free gates", "gates16"))
        for g in range(4):
            act.wait_ge(*at(f"full gate{g}"))
            b = bank_of(f"gate{g}")
            act.copy(r_gate[:, g, :], b[0:4, :]).then_inc(*AC.step(f"free gate{g}", "gate rows"))
        act_conv_out(act, 0)
        act_rows(act)
        act_conv(act, 2)
        act_conv_out(act, 1)
        act_conv(act, 3)
        act_later(act, 0)
        act_conv_out(act, 2)
        act_conv(act, 4)
        act_context(act)
        act_hy_turn(act, 0)
        act_conv(act, 5)
        act_later(act, 1)
        act_hy_turn(act, 1)
        for i in range(2):
            act.wait_ge(*at(f"full o{i}"))
            b = bank_of(f"o{i}")
            for j in range(2):
                act.activation(sgo[:, 2 * i + j, :], b[:, j * N:(j + 1) * N], ACT.Sigmoid,
                                           bias=c_bo[:, 2 * i + j:2 * i + j + 1]).then_inc(*AC.step(f"free o{i}", "o ready"))
        act_hy_turn(act, 2)
        act.wait_ge(*at("context done"))
        for t in range(4):
            for i in range(2):
                act.wait_ge(*at(f"full mergeA{t}_{i}"))
                b = bank_of(f"mergeA{t}_{i}")
                for j in range(2):
                    blk = 4 * t + 2 * i + j
                    act.activation(gates[:, blk % KD, blk // KD, :], b[:, j * N:(j + 1) * N], ACT.Sigmoid,
                                               bias=c_bm[:, blk:blk + 1]).then_inc(*AC.step(f"free mergeA{t}_{i}", "gates0"))
            if t % 2 == 0:
                act_later(act, 2 + t // 2)

    def dve_project(v):
        DV.stage("project")
        v.wait_ge(*at("columns"))
        v.wait_ge(*at("full spec14"))
        v.memset(vx[:, :, :, P:P + 1], 1.0).then_inc(*DV.step())
        v.memset(vc[:, :, :, P:P + 1], 1.0).then_inc(*DV.step())
        v.memset(r_s[:, 7, :], 0.0).then_inc(*DV.step("v ones"))
        dve_conv(v, 0)
        dve_conv(v, 1)
        dve_rows(v)
        dve_conv(v, 2)
        dve_conv(v, 3)
        dve_context(v)
        dve_conv(v, 4)
        dve_later(v, 0)
        dve_conv(v, 5)
        for g in range(1, 4):
            dve_later(v, g)

    def back(ap, d):
        return ap[:, ::-1] if d else ap

    def act_rows(act):
        act.wait_ge(*at("rows 1"))
        act.activation(r_t, r_t, ACT.Exp, scale=-1.0).then_inc(*AC.step("rows 2"))
        act.wait_ge(*at("rows 3"))
        act.activation(r_t, r_t, ACT.Ln).then_inc(*AC.step("rows 4"))
        act.wait_ge(*at("rows 5"))
        act.activation(r_t[:, :, 0:N], r_t[:, :, 0:N], ACT.Exp).then_inc(*AC.step())
        act.activation(r_t[:, :, N:2 * N], r_t[:, :, N:2 * N], ACT.Exp, scale=-1.0).then_inc(*AC.step("rows 6"))

    def dve_rows(v):
        f = r_gate[:, 1::2, :]
        v.wait_ge(*at("gate rows"))
        v.scalar_tensor_tensor(r_t, f, -1.0, f, ALU.mult, ALU.max).then_inc(*DV.step("rows 1"))
        v.wait_ge(*at("rows 2"))
        v.tensor_scalar(r_t, r_t, 1.0, None, ALU.add).then_inc(*DV.step("rows 3"))
        v.wait_ge(*at("rows 4"))
        v.scalar_tensor_tensor(r_lf, f, 0.0, r_t, ALU.min, ALU.subtract).then_inc(*DV.step())
        v.wait_ge(*DV.last())
        for s in range(2):
            for d in range(2):
                v.tensor_tensor_scan(back(r_b[:, d, s * N:(s + 1) * N], d), oner,
                                               back(r_lf[:, d, s * N:(s + 1) * N], d), 0.0, ALU.mult, ALU.add).then_inc(*DV.step())
        v.wait_ge(*DV.last())
        v.tensor_tensor(r_g, r_gate[:, 0::2, :], r_b, ALU.subtract).then_inc(*DV.step())
        v.wait_ge(*DV.last())
        v.tensor_reduce(r_s[:, 0, :], r_g[:, :, 0:N], AX, ALU.max).then_inc(*DV.step())
        v.wait_ge(*DV.last())
        v.tensor_scalar(r_s[:, 0, :], r_s[:, 0, :], 0.0, None, ALU.max).then_inc(*DV.step())
        v.wait_ge(*DV.last())
        for d in range(2):
            e = 0 if d else N - 1
            v.tensor_tensor(r_s[:, 1, d:d + 1], r_s[:, 0, d:d + 1], r_b[:, d, e:e + 1], ALU.add).then_inc(*DV.step())
            v.tensor_scalar(r_t[:, d, 0:N], r_g[:, d, 0:N], r_s[:, 0, d:d + 1], None, ALU.subtract).then_inc(*DV.step())
        v.wait_ge(*DV.last())
        for d in range(2):
            v.tensor_tensor_scan(back(r_M[:, d, :], d), oner, back(r_g[:, d, N:2 * N], d),
                                           r_s[:, 1, d:d + 1], ALU.mult, ALU.max).then_inc(*DV.step())
        v.wait_ge(*DV.last())
        v.tensor_tensor(r_t[:, :, N:2 * N], r_M, r_b[:, :, N:2 * N], ALU.add).then_inc(*DV.step("rows 5"))
        v.wait_ge(*at("full tokc"))
        b = bank_of("tokc")
        v.tensor_copy(small[:, 272:328], b[:, 0:56]).then_inc(*DV.step("free tokc", "tokc"))

    oner = ones[0:4, :]

    def pe_context(pe):
        pe.wait_ge(*at("rows 6"))
        b = bank(pe, "tokc")
        for kind, r in enumerate((r_t[:, :, 0:N], r_g[:, :, N:2 * N], r_t[:, :, N:2 * N])):
            for c in range(NC):
                for d in range(2):
                    o = ((kind * 2 + c) * 2 + d) * 4
                    pe.transpose(b[:, o:o + 4], r[:, d, c * P:(c + 1) * P], ident[0:4, 0:4])
        for h in range(4):
            ins = pe.matmul(b[:, 48 + 2 * h:50 + 2 * h], selh[:, h, :], r_s[:, 1, :], start=True, stop=True)
        ins.then_inc(*PE.step("full tokc"))
        pe.wait_ge(*at("kc"))
        for c in range(NC):
            b = bank(pe, f"kturn{c}")
            for h in range(4):
                ins = pe.transpose(b[:, h * P:(h + 1) * P], kc[:, h, c * P:(c + 1) * P], ident[:, :])
            ins.then_inc(*PE.step(f"full kturn{c}"))
        pe.wait_ge(*at("kw"))
        pe.wait_ge(*at("v ready0"))
        pe.wait_ge(*at("v ones"))
        for h in range(4):
            b = bank(pe, f"state{h}")
            for d in range(2):
                for c in range(NC):
                    ins = pe.matmul(b[:, d * 130:d * 130 + 129], kw[:, c, d, h, :], vc[:, c, h, 0:129], start=c == 0,
                                        stop=c == NC - 1)
            ins.then_inc(*PE.step(f"full state{h}"))

    def act_context(act):
        for h in range(4):
            act.wait_ge(*at(f"full state{h}"))
            b = bank_of(f"state{h}")
            act.copy(cst[:, h, :, 0:129], b[:, 0:260].rearrange("p (d e) -> p d e", d=2)[:, :, 0:129]).then_inc(*AC.step(f"free state{h}", "context done"))

    def dve_context(v):
        for c in range(NC):
            v.wait_ge(*at(f"full kturn{c}"))
            b = bank_of(f"kturn{c}")
            for d in range(2):
                v.tensor_tensor(kw[:, c, d], b[:, :].rearrange("p (h e) -> p h e", h=4),
                                          spread(tokc[:, 0, c, d, :], 2, P), ALU.mult).then_inc(*DV.step(f"free kturn{c}", "kw"))

    def pe_mlstm(pe):
        PE.stage("mlstm")
        pe.wait_ge(*at("k ready"))
        pe.wait_ge(*at("q ready"))
        pe.wait_ge(*at("tokc"))
        pe.wait_ge(*at("v ready1"))
        pe.wait_ge(*at("context done"))
        for h in range(4):
            bm = bank(pe, f"Mb{h}")
            pe.matmul(bm[:, :], selh[:, h, :], r_M.rearrange("p d t -> p (d t)"), start=True, stop=True).then_inc(*PE.step(f"full Mb{h}"))
            bs = bank(pe, f"S{h}")
            for c in range(NC):
                ins = pe.matmul(bs[:, c * N:(c + 1) * N], kq[:, 0, h, c * P:(c + 1) * P], kq[:, 1, h, :], start=True,
                                    stop=True)
            ins.then_inc(*PE.step(f"full S{h}"))
            pe_later(pe)
            if h:
                pe_mlstm_num(pe, h - 1)
        pe_mlstm_num(pe, 3)

    def pe_mlstm_turn(pe):
        pe.wait_ge(*at("mlstm normed"))
        for c in range(NC):
            b = bank(pe, f"mturn{c}")
            for h in range(4):
                ins = pe.transpose(b[:, h * P:(h + 1) * P], hh[:, c, h, :], ident[:, :])
            ins.then_inc(*PE.step(f"full mturn{c}"))

    def pe_mlstm_num(pe, h):
        pe.wait_ge(*at(f"A{h}"))
        pe.wait_ge(*at(f"qi{h}"))
        F0, F1, B0, B1 = Aw[:, 0:256], Aw[:, 256:384], Aw[:, 384:512], Aw[:, 512:768]
        for c in range(NC):
            key = f"num{h}{c}"
            b = bank(pe, key)
            parts = ([[(F0[:, 0:P], 0)], [(B0, 0), (B1[:, 0:P], 1)]], [[(F0[:, P:N], 0), (F1, 1)], [(B1[:, P:N], 1)]])[c]
            for d in range(2):
                o = b[:, d * 130:d * 130 + 129]
                for n, (a, s) in enumerate(parts[d]):
                    pe.matmul(o, a, vx[:, s, h, 0:129], start=n == 0, stop=False)
                ins = pe.matmul(o, qi[:, d, c * P:(c + 1) * P], cst[:, h, d, 0:129], start=False, stop=True)
            ins.then_inc(*PE.step("full " + key))

    def act_mlstm(act):
        AC.stage("mlstm")
        act.wait_ge(*at("tokc"))
        for h in range(4):
            act.wait_ge(*at(f"full Mb{h}"))
            b = bank_of(f"Mb{h}")
            if h:
                act.wait_ge(*at(f"qi{h - 1}"))
            act.wait_ge(*at(f"U{h}"))
            act.activation(U, U, ACT.Exp, scale=-1.0).then_inc(*AC.step(f"E{h}"))
            for d in range(2):
                act.activation(ai[:, d, :], b[:, d * N:(d + 1) * N], ACT.Exp, bias=m0c[:, h, d:d + 1],
                                           scale=-1.0).then_inc(*AC.step(f"ai{h}", f"free Mb{h}"))
            if h % 2 == 0:
                act_later(act, 4 + h // 2)
        act.wait_ge(*at("mlstm mean"))
        act.activation(w4[:, 0:8], w4[:, 0:8], ACT.Sqrt).then_inc(*AC.step("mlstm root"))

    def dve_mlstm(v):
        DV.stage("mlstm")
        v.wait_ge(*at("tokc"))
        v.wait_ge(*at("conv read5"))
        for h in range(4):
            v.wait_ge(*at(f"full Mb{h}"))
            b = bank_of(f"Mb{h}")
            if h:
                v.wait_ge(*at(f"full num{h - 1}1"))
            g = tokc[:, 1]
            for (lo, hi, d, s, t0, t1) in ((0, 256, 0, 0, 0, 256), (256, 384, 0, 1, 128, 256), (384, 512, 1, 0, 0, 128),
                                           (512, 768, 1, 1, 0, 256)):
                m = mask[:, d, 0:256] if hi - lo == 256 else (mask[:, d, 0:128] if d == 0 else mask[:, d, 128:256])
                v.scalar_tensor_tensor(U[:, lo:hi], b[:, d * N + t0:d * N + t1], g[:, s, d, h:h + 1], m,
                                                 ALU.subtract, ALU.max).then_inc(*DV.step(f"U{h}"))
            v.wait_ge(*at(f"ai{h}"))
            v.scalar_tensor_tensor(qi, ai, DH ** -0.5, spread(kq[:, 1, h, :], 1, 2), ALU.mult, ALU.mult).then_inc(*DV.step(f"qi{h}"))
            v.wait_ge(*at(f"full S{h}"))
            sc = bank_of(f"S{h}")
            v.wait_ge(*at(f"E{h}"))
            for (lo, hi, s, t0, t1) in ((0, 256, 0, 0, 256), (256, 384, 1, 128, 256), (384, 512, 0, 0, 128),
                                        (512, 768, 1, 0, 256)):
                v.scalar_tensor_tensor(Aw[:, lo:hi], sc[:, s * N + t0:s * N + t1], DH ** -0.5, U[:, lo:hi],
                                                 ALU.mult, ALU.mult).then_inc(*DV.step(f"A{h}", f"free S{h}"))
            if h:
                dve_mlstm_out(v, h - 1)
            if h % 2:
                dve_later(v, 4 + h // 2)
        dve_mlstm_out(v, 3)
        v.wait_ge(*DV.last())
        sq = view(arena, 16804, P, 8, P)
        hf = hh.rearrange("p c h e -> p (c h) e")
        v.tensor_tensor(sq, hf, hf, ALU.mult).then_inc(*DV.step())
        v.wait_ge(*DV.last())
        v.tensor_reduce(w4[:, 0:8], sq, AX, ALU.add).then_inc(*DV.step())
        v.wait_ge(*DV.last())
        v.tensor_scalar(w4[:, 0:8], w4[:, 0:8], 1.0 / DH, EPS, ALU.mult, ALU.add).then_inc(*DV.step("mlstm mean"))
        v.wait_ge(*at("mlstm root"))
        v.reciprocal(w4[:, 0:8], w4[:, 0:8]).then_inc(*DV.step())
        v.wait_ge(*DV.last())
        v.tensor_tensor(hf, hf, spread(w4[:, 0:8], 2, P), ALU.mult).then_inc(*DV.step("mlstm normed"))
        v.wait_ge(*at("o ready"))
        for c in range(NC):
            v.wait_ge(*at(f"full mturn{c}"))
            b = bank_of(f"mturn{c}")
            for h in range(4):
                o = sgo[:, h, c * P:(c + 1) * P]
                v.scalar_tensor_tensor(o, b[:, h * P:(h + 1) * P], c_mln[:, h:h + 1], o, ALU.mult, ALU.mult).then_inc(*DV.step(f"free mturn{c}", "yb0"))

    def dve_mlstm_out(v, h):
        for c in range(NC):
            v.wait_ge(*at(f"full num{h}{c}"))
            b = bank_of(f"num{h}{c}")
            num = b[:, 0:260].rearrange("p (d e) -> p d e", d=2)
            den = w4[:, 16:18]
            v.tensor_copy(w4[:, 20:22].unsqueeze(2), num[:, :, 128:129]).then_inc(*DV.step())
            v.wait_ge(*DV.last())
            v.scalar_tensor_tensor(den, w4[:, 20:22], -1.0, w4[:, 20:22], ALU.mult, ALU.max).then_inc(*DV.step())
            v.wait_ge(*DV.last())
            v.tensor_tensor(den, den, tokc[:, 2, c, :, h], ALU.max).then_inc(*DV.step())
            v.wait_ge(*DV.last())
            v.reciprocal(den, den).then_inc(*DV.step())
            v.wait_ge(*DV.last())
            v.tensor_scalar(hh[:, c, h, :], num[:, 0, 0:P], den[:, 0:1], None, ALU.mult).then_inc(*DV.step())
            v.wait_ge(*DV.last())
            v.scalar_tensor_tensor(hh[:, c, h, :], num[:, 1, 0:P], den[:, 1:2], hh[:, c, h, :], ALU.mult,
                                             ALU.add).then_inc(*DV.step(f"free num{h}{c}"))

    def pe_hyena(pe):
        for o in range(2):
            pe.wait_ge(*at("hyena parts"))
            for step in (["z1"] if o else []):
                pe.wait_ge(*at(step))
            z = (lambda c: hyt[:, c, 0:HY]) if o == 0 else (lambda c: zc[:, c, :])
            for i in range(4):
                b = bank(pe, f"dft{o}{i}")
                m = (dftc, dftc, dfts, dfts)[i]
                for c in range(NC):
                    ins = pe.matmul(b[:, :], m[:, c, (i % 2) * P:(i % 2 + 1) * P], z(c), start=c == 0, stop=c == 1)
                ins.then_inc(*PE.step(f"full dft{o}{i}"))
            if o == 0:
                pe_mlstm_turn(pe)
            PE.stage("hyena")
            pe_later(pe)
            pe.wait_ge(*at(f"product{o}"))
            for c in range(NC):
                b = bank(pe, f"idft{o}{c}")
                for f in range(4):
                    ins = pe.matmul(b[:, :], idft[:, f, c * P:(c + 1) * P], Yf[:, f, :], start=f == 0, stop=f == 3)
                ins.then_inc(*PE.step(f"full idft{o}{c}"))
            if o == 0:
                pe_later(pe)
        pe_later_turn(pe, 7)
        pe_rope(pe)
        PE.stage("hyena")
        pe.wait_ge(*at("z2"))
        for jj in range(2):
            b = bank(pe, f"yturn{jj}")
            for j in range(2):
                for c in range(NC):
                    ins = pe.transpose(b[:, (2 * j + c) * P:(2 * j + c + 1) * P],
                                           zc[:, c, (2 * jj + j) * P:(2 * jj + j + 1) * P], ident[:, :])
            ins.then_inc(*PE.step(f"full yturn{jj}"))

    def act_hyena(act):
        AC.stage("hyena")
        act_later(act, 6)
        act_later(act, 7)
        act.wait_ge(*at("full S3"))
        for jj in range(2):
            act.wait_ge(*at(f"full yturn{jj}"))
            b = bank_of(f"yturn{jj}")
            act.copy(yaT[:, 2 * jj:2 * jj + 2, :], b[:, :].rearrange("p (j t) -> p j t", j=2)).then_inc(*AC.step(f"free yturn{jj}", "ya0"))

    def dve_hyena(v):
        DV.stage("hyena")
        v.wait_ge(*at("full state3"))
        v.wait_ge(*at("spectra"))
        for o in range(2):
            k = spec[:, o]
            for f in range(2):
                v.wait_ge(*at(f"full dft{o}{f}"))
                v.wait_ge(*at(f"full dft{o}{2 + f}"))
                br, bi = bank_of(f"dft{o}{f}"), bank_of(f"dft{o}{2 + f}")
                re2 = k[:, 4] if f == 0 else k[:, 1]
                if o and f == 0:
                    v.wait_ge(*at("full idft01"))
                v.tensor_tensor(Yf[:, f, :], br[:, :], k[:, f], ALU.mult).then_inc(*DV.step())
                v.tensor_tensor(t1, bi[:, :], k[:, 2 + f], ALU.mult).then_inc(*DV.step())
                v.tensor_tensor(Yf[:, 2 + f, :], br[:, :], k[:, 2 + f], ALU.mult).then_inc(*DV.step(f"free dft{o}{f}"))
                v.tensor_tensor(t2, bi[:, :], re2, ALU.mult).then_inc(*DV.step(f"free dft{o}{2 + f}"))
                v.wait_ge(*DV.last())
                v.tensor_tensor(Yf[:, f, :], Yf[:, f, :], t1, ALU.subtract).then_inc(*DV.step())
                v.tensor_tensor(Yf[:, 2 + f, :], Yf[:, 2 + f, :], t2, ALU.add).then_inc(*DV.step(f"product{o}"))
                v.wait_ge(*DV.last())
            for c in range(NC):
                v.wait_ge(*at(f"full idft{o}{c}"))
                b = bank_of(f"idft{o}{c}")
                if o and c == 0:
                    v.wait_ge(*at("full dft13"))
                v.tensor_tensor(zc[:, c, :], b[:, :], hyt[:, c, (o + 1) * HY:(o + 2) * HY], ALU.mult).then_inc(*DV.step(f"free idft{o}{c}", f"z{o + 1}"))
            dve_later(v, 6 + o)

    merged = view(hx, KD * N, P, KD, N)

    def mixer_out(p, wa, wb, wo, yb, ga, gate_ready):
        def pe_out(pe):
            PE.stage(f"mix{p}")
            a, b_ = tile(pe, wa), tile(pe, wb)
            pe.wait_ge(*at(f"ya{p}"))
            pe.wait_ge(*at(f"yb{p}"))
            for j in range(KD):
                b = bank(pe, f"merge{p}{j}")
                for s, (w, y) in enumerate(((a, yaT if p == 0 else yT2[:, 0:4]), (b_, yb))):
                    for k in range(4):
                        ins = pe.matmul(b[:, s * N:(s + 1) * N], w[:, k, j * P:(j + 1) * P], y[:, k, :], start=k == 0,
                                            stop=k == 3)
                ins.then_inc(*PE.step(f"full merge{p}{j}"))
            mark_used(pe, wa)
            mark_used(pe, wb)
            for t in range(2):
                pe_linear_T(pe, f"mixout{p}{t}", f"{wo}{t}", merged, N, 4, None if t else f"merged{p}")

        def dve_out(v):
            DV.stage(f"mix{p}")
            v.wait_ge(*at(f"gates{p}"))
            for j in range(KD):
                v.wait_ge(*at(f"full merge{p}{j}"))
                b = bank_of(f"merge{p}{j}")
                g = gates[:, j].rearrange("p a b -> p (a b)")
                v.tensor_tensor(g, b[:, :], g, ALU.mult).then_inc(*DV.step(f"free merge{p}{j}"))
                v.wait_ge(*DV.last())
                v.tensor_tensor(merged[:, j, :], gates[:, j, 0, :], gates[:, j, 1, :], ALU.add).then_inc(*DV.step(f"merged{p} done{j}"))
            v.wait_ge(*at(gate_ready))
            for t in range(2):
                for i in range(2):
                    key = f"mixout{p}{t}{i}"
                    v.wait_ge(*at("full " + key))
                    b = bank_of(key)
                    for j in range(2):
                        blk = 4 * t + 2 * i + j
                        v.scalar_tensor_tensor(xT[:, blk, :], b[:, j * N:(j + 1) * N], ga[:, 16 + blk:17 + blk],
                                                         xT[:, blk, :], ALU.mult, ALU.add).then_inc(*DV.step("free " + key, f"x mixed{p}", f"x mixed{p} {blk}"))
        return pe_out, dve_out

    def dve_gain(v, key, dst, gain, scale, *ready):
        v.wait_ge(*at("columns"))
        for step in ready:
            v.wait_ge(*at(step))
        v.scalar_tensor_tensor(dst, scale, 1.0, gain, ALU.add, ALU.mult).then_inc(*DV.step(key))
        v.wait_ge(*DV.last())

    e_wr = view(arena, 0, P, KD, EXPERTS)
    e_iota, e_slot = arena[:, 128:160], arena[:, 160:161]
    e_aff = view(arena, 164, P, NC, EXPERTS)
    e_pos = view(arena, 196, P, NC, EXPERTS)
    e_st = view(arena, 228, P, 3, NC)
    e_work = arena[0:EXPERTS, 236:492]
    e_top = arena[0:EXPERTS, 492:500]
    e_sel = arena[0:EXPERTS, 500:756]
    e_pa = arena[0:EXPERTS, 756:1268]
    e_psel = view(arena, 1268, P, NC, EXPERTS * CAP)
    e_htok = view(arena, 2292, P, NC, D)
    e_xg = view(arena, 4340, P, KD, EXPERTS * CAP)
    e_xe = view(arena, 8436, P, KD, CAP)
    e_row = arena[0:EXPERTS, 8692:9204]
    e_t = arena[:, 9204:9460]
    e_G = arena[:, 9460:9716]
    e_h = arena[:, 9716:10228]
    e_hT = view(arena, 10228, P, 4, P)
    e_y = arena[:, 10740:11764]

    def act_moe_loads(act):
        act.wait_ge(*at("x mixed0"))
        act.wait_ge(*at("full yturn1"))
        act.wait_ge(*at("ya0"))
        for dst, src in ((e_wr, A["w_router"][0].rearrange("(k p) n -> p k n", p=P)), (e_iota, A["k_iota"]),
                         (e_slot, A["k_slot"])):
            act.dma_start(dst, src).then_inc(*K.load("load_moe"))

    def pe_route(pe):
        PE.stage("route")
        pe.wait_ge(*K.loaded("load_moe"))
        pe.wait_ge(*at("h ffn0 done"))
        b = bank(pe, "logits")
        for c in range(NC):
            for k in range(KD):
                ins = pe.matmul(b[:, c * 16:(c + 1) * 16], h2[:, k, c * P:(c + 1) * P], e_wr[:, k, :], start=k == 0,
                                    stop=k == KD - 1)
        ins.then_inc(*PE.step("full logits"))
        for c in range(NC):
            for i in range(2):
                b = bank(pe, f"htok{c}{i}")
                for j in range(4):
                    ins = pe.transpose(b[:, j * P:(j + 1) * P], h2[:, 4 * i + j, c * P:(c + 1) * P], ident[:, :])
                ins.then_inc(*PE.step(f"full htok{c}{i}"))
        pe.wait_ge(*at("affinity"))
        b = bank(pe, "affT")
        for c in range(NC):
            ins = pe.transpose(b[0:EXPERTS, c * P:(c + 1) * P], e_aff[:, c, :], ident[:, :])
        ins.then_inc(*PE.step("full affT"))
        pe.wait_ge(*at("slots"))
        b = bank(pe, "postok")
        for c in range(NC):
            ins = pe.transpose(b[:, c * 16:(c + 1) * 16], e_pa[:, c * P:(c + 1) * P], ident[0:16, 0:16])
        ins.then_inc(*PE.step("full postok"))
        pe.wait_ge(*at("one-hot"))
        pe.wait_ge(*at("h tokens"))
        for k in range(KD):
            b = bank(pe, f"gather{k}")
            for c in range(NC):
                ins = pe.matmul(b[:, :], e_htok[:, c, k * P:(k + 1) * P], e_psel[:, c, :], start=c == 0, stop=c == 1)
            ins.then_inc(*PE.step(f"full gather{k}"))

    def act_route(act):
        AC.stage("route")
        act.wait_ge(*at("logit max"))
        act.wait_ge(*at("full logits"))
        b = bank_of("logits")
        for c in range(NC):
            act.activation(e_aff[:, c, :], b[:, c * 16:(c + 1) * 16], ACT.Exp, bias=e_st[:, 0, c:c + 1],
                                       accum_out=e_st[:, 1, c:c + 1]).then_inc(*AC.step("free logits", "exp logits"))
        for c in range(NC):
            for i in range(2):
                act.wait_ge(*at(f"full htok{c}{i}"))
                b = bank_of(f"htok{c}{i}")
                act.copy(e_htok[:, c, 512 * i:512 * i + 512], b[:, :]).then_inc(*AC.step(f"free htok{c}{i}", "h tokens"))
        for k in range(KD):
            act.wait_ge(*at(f"full gather{k}"))
            b = bank_of(f"gather{k}")
            act.copy(e_xg[:, k, :], b[:, :]).then_inc(*AC.step(f"free gather{k}", "gathered"))

    def dve_route(v):
        DV.stage("route")
        v.wait_ge(*at("full logits"))
        b = bank_of("logits")
        v.tensor_reduce(e_st[:, 0, :], b[:, 0:32].rearrange("p (c e) -> p c e", c=NC), AX, ALU.max,
                                  negate=True).then_inc(*DV.step("logit max"))
        v.wait_ge(*at("exp logits"))
        v.reciprocal(e_st[:, 2, :], e_st[:, 1, :]).then_inc(*DV.step())
        v.wait_ge(*DV.last())
        v.tensor_tensor(e_aff, e_aff, spread(e_st[:, 2, :], 2, EXPERTS), ALU.mult).then_inc(*DV.step("affinity"))
        v.wait_ge(*at("full affT"))
        b = bank_of("affT")
        v.tensor_copy(e_pa[:, N:2 * N], b[0:EXPERTS, 0:N]).then_inc(*DV.step())
        v.tensor_copy(e_work, b[0:EXPERTS, 0:N]).then_inc(*DV.step("free affT"))
        for _ in range(CAP // 8):
            v.wait_ge(*DV.last())
            v.max(e_top, e_work).then_inc(*DV.step())
            v.wait_ge(*DV.last())
            v.match_replace(e_work, e_top, e_work, -1.0).then_inc(*DV.step())
        v.wait_ge(*DV.last())
        v.tensor_scalar(e_sel, e_work, 0.0, None, ALU.is_lt).then_inc(*DV.step())
        v.wait_ge(*DV.last())
        v.tensor_tensor_scan(e_work, oner16, e_sel, 0.0, ALU.mult, ALU.add).then_inc(*DV.step())
        v.wait_ge(*DV.last())
        v.tensor_tensor(e_work, e_work, e_sel, ALU.mult).then_inc(*DV.step())
        v.wait_ge(*DV.last())
        v.tensor_scalar(e_pa[:, 0:N], e_work, 1.0, None, ALU.subtract).then_inc(*DV.step("slots"))
        v.wait_ge(*K.loaded("load_moe"))
        v.wait_ge(*at("full postok"))
        b = bank_of("postok")
        v.tensor_copy(e_pos, b[:, 0:32].rearrange("p (c e) -> p c e", c=NC)).then_inc(*DV.step("free postok"))
        v.wait_ge(*DV.last())
        for c in range(NC):
            v.tensor_tensor(e_psel[:, c, :].rearrange("p (e s) -> p e s", s=CAP), spread(e_iota, 1, EXPERTS),
                                      spread(e_pos[:, c, :], 2, CAP), ALU.is_equal).then_inc(*DV.step("one-hot"))
        v.memset(e_y, 0.0).then_inc(*DV.step("y zero"))

    oner16 = ones[0:16, :]

    def loop(eng, Q, body):
        Q.stage("expert")
        eng.sem_inc(K.sem(Q.cur), book.per.get(Q.cur, 1))
        with eng.Fori(0, EXPERTS) as i:
            K.turn = i
            body(i)
        K.turn = None
        book.per[Q.cur] = Q.count[Q.cur]

    def pe_experts(pe):
        PE.stage("route")
        pe.wait_ge(*at("y zero"))
        for b in range(4, 8):
            key = f"moe{b}"
            pe.matmul(claim(pe, b, key)[:, :], e_y[:, 0:P], e_y[:, 0:512], start=True, stop=True,
                                   skip_group_check=True).then_inc(*PE.step("full " + key))
        for b in range(4):
            claim(pe, b, f"expert bank{b}")

        def body(i):
            def tile(t):
                n = N_PRE + t
                pe.wait_ge(tile_sem(n), i * (16 * N_EXP // RING) + 16 * (n // RING + 1))
                return n
            pe.wait_ge(*at("xe"))
            pe.wait_ge(*at("y copied", back=1))
            for s in range(2):
                for t in range(4):
                    w = place(tile(4 * s + t), P, 2, 4 * 512)
                    for kk in range(2):
                        for j in range(4):
                            ins = pe.matmul(banks[s][32 * j:32 * j + 32, :], e_xe[:, 2 * t + kk, :],
                                                w[:, kk, 512 * j:512 * j + 512], start=t + kk == 0, stop=t + kk == 4)
                    ins.then_inc(*PE.step(f"expert used{4 * s + t}", *([("a full", "b full")[s]] if t == 3 else [])))
            pe.wait_ge(*at("G", back=1))
            pe.wait_ge(*at("row"))
            pe.matmul(banks[3][:, :], ones[0:EXPERTS, 0:P], e_row, start=True, stop=True).then_inc(*PE.step("row full"))
            pe.wait_ge(*at("h ready"))
            for k in range(4):
                ins = pe.transpose(banks[2][:, k * P:(k + 1) * P], e_h[:, k * P:(k + 1) * P], ident[:, :])
            ins.then_inc(*PE.step("hT full"))
            pe.wait_ge(*at("hT copied"))
            for t in range(4):
                w = place(tile(8 + t), P, 4, D)
                for half in range(2):
                    for k in range(4):
                        ins = pe.matmul(banks[half][32 * k:32 * k + 32, :], e_hT[:, k, 32 * t:32 * t + 32],
                                            w[:, k, 512 * half:512 * half + 512], start=t == 0, stop=t == 3)
                ins.then_inc(*PE.step(f"expert used{8 + t}", *(["y full"] if t == 3 else [])))
            pe.wait_ge(*at("y copied"))
            pe.wait_ge(*at("G"))
            for j in range(KD):
                ins = pe.matmul(banks[4 + j // 2][:, (j % 2) * N:(j % 2 + 1) * N], e_y[:, j * P:(j + 1) * P], e_G,
                                    start=False, stop=True, skip_group_check=True)
            ins.then_inc(*PE.step("scattered"))
        loop(pe, PE, body)
        for b in range(4):
            book.where[f"free expert bank{b}"] = book.where.get(("y copied", "y copied", "hT copied", "G")[b], (PE.cur, 1))

    def act_experts(act):
        act.wait_ge(*at("gathered"))
        act.wait_ge(*at("y zero"))

        def body(i):
            act.wait_ge(*at("a full"))
            act.wait_ge(*at("h ready", back=1))
            act.activation(e_h, banks[0][:, :], ACT.Silu).then_inc(*AC.step("silu"))
            act.wait_ge(*at("hT full"))
            act.copy(e_hT.rearrange("p a b -> p (a b)"), banks[2][:, :]).then_inc(*AC.step("hT copied"))
            act.wait_ge(*at("y full"))
            act.wait_ge(*at("scattered", back=1))
            act.copy(e_y[:, 0:512], banks[0][:, :]).then_inc(*AC.step())
            act.copy(e_y[:, 512:1024], banks[1][:, :]).then_inc(*AC.step("y copied"))
        loop(act, AC, body)

    def dve_experts(v):
        v.wait_ge(*at("gathered"))

        def body(i):
            v.wait_ge(*at("b full", back=1))
            v.tensor_copy(e_xe, e_xg[:, :, bass.ds(i * CAP, CAP)]).then_inc(*DV.step("xe"))
            v.tensor_scalar(e_row, e_pa, ident[0:EXPERTS, bass.ds(i, 1)], None, ALU.mult).then_inc(*DV.step("row"))
            v.wait_ge(*at("row full"))
            v.wait_ge(*at("scattered", back=1))
            v.tensor_copy(e_t, banks[3][:, N:2 * N]).then_inc(*DV.step())
            v.wait_ge(*DV.last())
            v.scalar_tensor_tensor(e_G, banks[3][:, 0:N], e_slot, e_t, ALU.is_equal, ALU.mult).then_inc(*DV.step("G"))
            v.wait_ge(*at("silu"))
            v.wait_ge(*at("b full"))
            v.tensor_tensor(e_h, e_h, banks[1][:, :], ALU.mult).then_inc(*DV.step("h ready"))
        loop(v, DV, body)
        DV.stage("moeout")
        v.wait_ge(*at("scattered"))
        for j in range(KD):
            v.scalar_tensor_tensor(xT[:, j, :], banks[4 + j // 2][:, (j % 2) * N:(j % 2 + 1) * N],
                                             adaX[0][:, 40 + j:41 + j], xT[:, j, :], ALU.mult, ALU.add).then_inc(*DV.step(f"free moe{4 + j // 2}", "x moe", f"x moe {j}"))

    qkv = view(arena, 0, P, NC, MERGE2)
    tabA = view(arena, 5680, P, NC, 4, HD)
    tabB = view(arena, 6192, P, NC, 4, HD)
    cs = view(arena, 23700, P, NC, 2, 32)
    qT = view(arena, 7088, P, 8, N)
    kp = view(arena, 9136, P, 16, N)
    y2 = view(arena, 13232, P, NC, D)
    yT2 = view(arena, 15280, P, KD, N)
    sqh = view(arena, 17328, P, NC, 28 * HD)
    ptc = view(arena, 17328, 16, 16, P)
    cw2 = view(arena, 20912, P, 2, 2, HD)
    pet = view(arena, 21168, HD, 2, 32)
    hidc = view(arena, 21232, P, 2, 32)
    kcv = view(arena, 21296, 16, 4, HD)
    kct = view(arena, 21552, P, 4, 16)
    causal = arena[:, 21616:21872]
    cmask = view(arena, 21872, P, NC, 16)
    valid = arena[:, 21904:21906]
    tabC = view(arena, 21908, 16, 2, HD)
    csc = view(arena, 22036, 16, 2, 32)
    inv = arena[:, 22100:22132]
    ang = view(arena, 22132, P, 3, 32)
    posi = arena[:, 22228:22231]
    posf = arena[:, 22232:22235]
    msq = view(arena, 22240, P, NC, 28)
    mx = view(arena, 22300, P, 3, 2)
    sums = view(arena, 22308, P, NC, 24)
    wts = view(arena, 22356, P, NC, 8)
    sC = view(arena, 22372, P, 16, 16)
    mC, suC = arena[:, 22628:22644], arena[:, 22644:22660]
    msc = arena[0:16, 22660:22664]
    tmpc = view(arena, 22664, 16, 2, HD)
    kdup = view(arena, 22792, 16, 2, 2, HD)
    gain_l = view(arena, 23048, P, 2, 4, HD)
    peraw = view(arena, 23560, 32, 2, HD)
    ffT = view(arena, 0, P, FB, N)
    sm = view(scr, 0, P, 3, 384)
    pt = view(scr, 1152, P, 3, 384)
    tmpo = scr[:, 2304:2816]
    sg = view(scr, 0, P, 2, 512)
    otok = view(arena, 0, P, NC, D)

    GROUPS = [(0, 8, 0, 0), (768, 2, 8, 1), (KW0, 2, 10, 1), (QB0, 8, 12, 2), (QB0 + 512, 8, 20, 3)]

    def act_second_loads(act):
        AC.stage("rope")
        act.wait_ge(*at("full mturn1"))
        act.wait_ge(*at("mlstm normed"))

        def load(dst, src, **kw):
            act.dma_start(dst, src, **kw).then_inc(*K.load("load_second"))
        pos = A["positions_2"]
        load(posi[:, 0:2].bitcast(I32), pos[0].rearrange("(c p) -> p c", p=P), allow_slow_non_contiguous=True)
        load(posi[0:15, 2:3].bitcast(I32), pos[0, 31::16].rearrange("(n a) -> n a", a=1), allow_slow_non_contiguous=True)
        load(inv, A["k_inv"])
        load(causal, A["k_causal"])
        load(cmask, A["k_cmask"])
        load(valid, A["k_valid"])
        for l in range(LAYERS):
            for i, nm in enumerate(("nsa_q_gain_2", "nsa_k_gain_2", "moba_q_gain_2", "moba_k_gain_2")):
                load(gain_l[:, l, i, :], A[nm][l].rearrange("(a n) -> a n", a=1).broadcast_to([P, HD]))
            load(peraw[:, l, :], A["nsa_cmp_pe_2"][l])
            for i, nm in enumerate("kv"):
                load(cw2[:, l, i, :], A[f"nsa_cmp_{nm}_w2_2"][l])

    def pe_rope(pe):
        PE.stage("rope")
        pe.wait_ge(*K.loaded("load_second"))
        b = bank(pe, "pet")
        for l in range(LAYERS):
            ins = pe.transpose(b[0:HD, l * 32:(l + 1) * 32], peraw[:, l, :], ident[0:32, 0:32])
        ins.then_inc(*PE.step("full pet"))

    def act_rope(act):
        AC.stage("rope")
        for i in range(2):
            act.wait_ge(*at(f"angle{i}"))
            act.activation(cs[:, :, i, :], ang[:, 0:2, :], ACT.Sin).then_inc(*AC.step())
            act.activation(csc[0:15, i, :], ang[0:15, 2, :], ACT.Sin).then_inc(*AC.step(f"sine{i}"))

    def dve_rope(v):
        DV.stage("rope")
        v.wait_ge(*K.loaded("load_second"))
        v.wait_ge(*at("full pet"))
        b = bank_of("pet")
        v.tensor_copy(pet, b[0:HD, 0:64].rearrange("p (l j) -> p l j", l=2)).then_inc(*DV.step("free pet", "pe ready"))
        v.memset(kct, 0.0).then_inc(*DV.step())
        v.memset(kcv, 0.0).then_inc(*DV.step())
        v.memset(posf, 0.0).then_inc(*DV.step())
        v.wait_ge(*DV.last())
        v.tensor_copy(posf[:, 0:2], posi[:, 0:2].bitcast(I32)).then_inc(*DV.step())
        v.tensor_copy(posf[0:15, 2:3], posi[0:15, 2:3].bitcast(I32)).then_inc(*DV.step())
        v.wait_ge(*DV.last())
        a0 = sqh[:, 0, 0:96].rearrange("p (a b) -> p a b", a=3)
        kk = sqh[:, 1, 0:96].rearrange("p (a b) -> p a b", a=3)
        for c in range(3):
            v.tensor_scalar(a0[:, c, :], inv, posf[:, c:c + 1], None, ALU.mult).then_inc(*DV.step())
        for i in range(2):
            if i:
                v.wait_ge(*at("sine0"))
            v.wait_ge(*DV.last())
            dve_reduce(v, ang, a0, kk, quarter=i == 0)
            book.where[f"angle{i}"] = DV.now
        v.wait_ge(*at("sine1"))

    def pe_in(pe, l):
        PE.stage("second")
        for t in range(6):
            pe_linear_tok(pe, f"in{l}_{t}", f"in{l}_{t}", h2, None if t else f"h mix{l + 1}")

    IN_COLS = [(0, 512), (512, 1024), (1024, 1304), (1304, 1816), (1816, 2328), (2328, 2840)]

    def act_in(act, l):
        AC.stage("second")
        act.wait_ge(*at("x moe" if l == 0 else "ffn read0"))
        for t, (lo, hi) in enumerate(IN_COLS):
            for c in range(NC):
                key = f"in{l}_{t}{c}"
                act.wait_ge(*at("full " + key))
                b = bank_of(key)
                act.copy(qkv[:, c, lo:hi], b[:, 0:hi - lo]).then_inc(*AC.step("free " + key, f"in{l} {t}"))
        act.wait_ge(*AC.last())
        for c in range(NC):
            for col, H, lo, _ in GROUPS:
                act.activation(sqh[:, c, lo * HD:(lo + H) * HD], qkv[:, c, col:col + H * HD], ACT.Square).then_inc(*AC.step(f"squares{l}"))
        for c in range(NC):
            act.activation(qkv[:, c, KV0 + 768:KV0 + 792], qkv[:, c, KV0 + 768:KV0 + 792], ACT.Sigmoid).then_inc(*AC.step(f"head gates{l}"))
        act.wait_ge(*at(f"head mean{l}"))
        act.activation(msq, msq, ACT.Sqrt).then_inc(*AC.step(f"head root{l}"))

    def dve_in(v, l):
        DV.stage("second")
        v.wait_ge(*at("sine1"))
        g4 = gain_l[:, l].rearrange("p g (s e) -> p g s e", s=2)
        for c in range(NC):
            a4 = tabA[:, c].rearrange("p g (s e) -> p (g s) e", s=2)
            b4 = tabB[:, c].rearrange("p g (s e) -> p g s e", s=2)
            v.tensor_tensor(a4, gain_l[:, l].rearrange("p g (s e) -> p (g s) e", s=2),
                                      spread(cs[:, c, 0, :], 1, 8), ALU.mult).then_inc(*DV.step())
            v.scalar_tensor_tensor(b4[:, :, 0, :], g4[:, :, 1, :], -1.0, spread(cs[:, c, 1, :], 1, 4),
                                             ALU.mult, ALU.mult).then_inc(*DV.step())
            v.tensor_tensor(b4[:, :, 1, :], g4[:, :, 0, :], spread(cs[:, c, 1, :], 1, 4), ALU.mult).then_inc(*DV.step())
        v.wait_ge(*at(f"squares{l}"))
        v.tensor_reduce(msq, sqh.rearrange("p c (h e) -> p c h e", e=HD), AX, ALU.add).then_inc(*DV.step())
        v.wait_ge(*DV.last())
        v.tensor_scalar(msq, msq, 1.0 / HD, EPS, ALU.mult, ALU.add).then_inc(*DV.step(f"head mean{l}"))
        v.wait_ge(*at(f"head root{l}"))
        v.reciprocal(msq, msq).then_inc(*DV.step())
        v.wait_ge(*DV.last())
        for c in range(NC):
            for col, H, lo, g in GROUPS:
                x = qkv[:, c, col:col + H * HD].rearrange("p (h e) -> p h e", e=HD)
                v.tensor_tensor(x, x, spread(msq[:, c, lo:lo + H], 2, HD), ALU.mult).then_inc(*DV.step())
        v.wait_ge(*DV.last())
        for c in range(NC):
            for col, H, lo, g in GROUPS:
                x = qkv[:, c, col:col + H * HD].rearrange("p (h e) -> p h e", e=HD)
                t = sqh[:, c, lo * HD:(lo + H) * HD].rearrange("p (h e) -> p h e", e=HD)
                v.tensor_tensor(t[:, :, 0:32], x[:, :, 32:64], spread(tabB[:, c, g, 0:32], 1, H), ALU.mult).then_inc(*DV.step())
                v.tensor_tensor(t[:, :, 32:64], x[:, :, 0:32], spread(tabB[:, c, g, 32:64], 1, H), ALU.mult).then_inc(*DV.step())
        v.wait_ge(*DV.last())
        for c in range(NC):
            for col, H, lo, g in GROUPS:
                x = qkv[:, c, col:col + H * HD].rearrange("p (h e) -> p h e", e=HD)
                v.tensor_tensor(x, x, spread(tabA[:, c, g, :], 1, H), ALU.mult).then_inc(*DV.step())
        v.wait_ge(*DV.last())
        for c in range(NC):
            for col, H, lo, g in GROUPS:
                x = qkv[:, c, col:col + H * HD]
                v.tensor_tensor(x, x, sqh[:, c, lo * HD:(lo + H) * HD], ALU.add).then_inc(*DV.step(f"roped{l}"))

    def pe_compress(pe, l):
        PE.stage("compress")
        pe.wait_ge(*at(f"in{l} 1"))
        pe.wait_ge(*at("pe ready"))
        for s in range(2):
            key = f"cturn{l}{s}"
            b = bank(pe, key)
            for g in range(2):
                for c in range(NC):
                    col = KV0 + s * 128 + g * HD
                    ins = pe.transpose(b[0:HD, (g * 2 + c) * P:(g * 2 + c + 1) * P], qkv[:, c, col:col + HD], ident[:, :])
            ins.then_inc(*PE.step("full " + key))
        pe_gates2(pe, l, 0)
        pe_gates2(pe, l, 1)
        for s in range(2):
            w = tile(pe, f"cmp{'kv'[s]}{l}_0")
            pe.wait_ge(*at(f"cmp x{l}{s}"))
            key = f"chid{l}{s}"
            b = bank(pe, key)
            for j in range(32):
                x = cmpx[:, 2 * s + j // 16].rearrange("p g (n j) -> p g n j", j=16)
                x = x[:, :, j // 16:j // 16 + 15, j % 16]
                ins = pe.matmul(b[:, 0:30], w[:, j, :], x, start=j == 0, stop=j == 31)
            ins.then_inc(*PE.step("full " + key))
            mark_used(pe, f"cmp{'kv'[s]}{l}_0")
        pe_gates2(pe, l, 2)
        pe.wait_ge(*at(f"gelu{l}"))
        b = bank(pe, f"cout{l}")
        for s in range(2):
            for g in range(2):
                o = (2 * s + g) * HD
                ins = pe.matmul(b[0:15, o:o + HD], hidc[:, s, 15 * g:15 * g + 15], cw2[:, l, s, :], start=True, stop=True)
        ins.then_inc(*PE.step(f"full cout{l}"))
        pe_gates2(pe, l, 3)
        pe.wait_ge(*at(f"kdup{l}"))
        b = bank(pe, f"kct{l}")
        for g in range(2):
            ins = pe.transpose(b[:, g * 16:g * 16 + 15], kdup[0:15, g].rearrange("p a b -> p (a b)"), ident[0:15, 0:15])
        ins.then_inc(*PE.step(f"full kct{l}"))

    def act_compress(act, l):
        AC.stage("compress")
        act_gates2(act, l, 0, 1)
        for s in range(2):
            act.wait_ge(*at(f"full chid{l}{s}"))
            b = bank_of(f"chid{l}{s}")
            act.activation(hidc[:, s, 0:30], b[:, 0:30], ACT.Gelu_apprx_tanh).then_inc(*AC.step(f"free chid{l}{s}", f"gelu{l}"))
        act_gates2(act, l, 2)
        act.wait_ge(*at(f"cmp mean{l}"))
        act.activation(msc[0:15, 0:2], msc[0:15, 0:2], ACT.Sqrt).then_inc(*AC.step(f"cmp root{l}"))
        act_gates2(act, l, 3)

    def dve_dup(v, l):
        v.wait_ge(*DV.last())
        v.wait_ge(*at(f"full chid{l}1"))
        for c in range(NC):
            for bi, col in enumerate((768, KW0)):
                for i in range(2):
                    v.tensor_copy(dup[:, c, 2 * bi:2 * bi + 2, i * HD:(i + 1) * HD],
                                            qkv[:, c, col:col + P].rearrange("p (g e) -> p g e", g=2)).then_inc(*DV.step(f"roped{l}"))

    def dve_blocks(v, l):
        DV.stage("compress")
        v.wait_ge(*at("pe ready"))
        for s in range(2):
            v.wait_ge(*at(f"full cturn{l}{s}"))
            b = bank_of(f"cturn{l}{s}")
            for half in range(2):
                v.tensor_tensor(cmpx[:, 2 * s + half].rearrange("p g (n j) -> p (g n) j", j=16),
                                          b[0:HD, :].rearrange("p (n j) -> p n j", j=16),
                                          spread(pet[:, l, half * 16:half * 16 + 16], 1, 32), ALU.add).then_inc(*DV.step(f"free cturn{l}{s}", f"cmp x{l}{s}"))

    def dve_compress(v, l):
        DV.stage("compress")
        v.wait_ge(*at(f"full cout{l}"))
        b = bank_of(f"cout{l}")
        v.tensor_copy(kcv[0:15], b[0:15, 0:256].rearrange("p (a b) -> p a b", a=4)).then_inc(*DV.step(f"free cout{l}"))
        v.wait_ge(*DV.last())
        k2 = kcv[0:15, 0:2, :]
        v.tensor_tensor(tmpc[0:15], k2, k2, ALU.mult).then_inc(*DV.step())
        v.wait_ge(*DV.last())
        v.tensor_reduce(msc[0:15, 0:2], tmpc[0:15], AX, ALU.add).then_inc(*DV.step())
        v.wait_ge(*DV.last())
        v.tensor_scalar(msc[0:15, 0:2], msc[0:15, 0:2], 1.0 / HD, EPS, ALU.mult, ALU.add).then_inc(*DV.step(f"cmp mean{l}"))
        g = gain_l[0:15, l, 1, :].rearrange("p (s e) -> p s e", s=2)
        ta = tabC[0:15, 0, :].rearrange("p (s e) -> p s e", s=2)
        tb = tabC[0:15, 1, :].rearrange("p (s e) -> p s e", s=2)
        v.tensor_tensor(ta, g, spread(csc[0:15, 0, :], 1, 2), ALU.mult).then_inc(*DV.step())
        v.scalar_tensor_tensor(tb[:, 0, :], g[:, 1, :], -1.0, csc[0:15, 1, :], ALU.mult, ALU.mult).then_inc(*DV.step())
        v.tensor_tensor(tb[:, 1, :], g[:, 0, :], csc[0:15, 1, :], ALU.mult).then_inc(*DV.step())
        v.wait_ge(*at(f"cmp root{l}"))
        v.reciprocal(msc[0:15, 0:2], msc[0:15, 0:2]).then_inc(*DV.step())
        v.wait_ge(*DV.last())
        v.tensor_tensor(k2, k2, spread(msc[0:15, 0:2], 2, HD), ALU.mult).then_inc(*DV.step())
        v.wait_ge(*DV.last())
        v.tensor_tensor(tmpc[0:15, :, 0:32], k2[:, :, 32:64], spread(tabC[0:15, 1, 0:32], 1, 2), ALU.mult).then_inc(*DV.step())
        v.tensor_tensor(tmpc[0:15, :, 32:64], k2[:, :, 0:32], spread(tabC[0:15, 1, 32:64], 1, 2), ALU.mult).then_inc(*DV.step())
        v.wait_ge(*DV.last())
        v.tensor_tensor(k2, k2, spread(tabC[0:15, 0, :], 1, 2), ALU.mult).then_inc(*DV.step())
        v.wait_ge(*DV.last())
        for i in range(2):
            v.tensor_tensor(kdup[0:15, :, i, :], k2, tmpc[0:15], ALU.add).then_inc(*DV.step(f"kdup{l}"))
        v.wait_ge(*at(f"full kct{l}"))
        b = bank_of(f"kct{l}")
        bb = b[:, 0:32].rearrange("p (g n) -> p g n", g=2)[:, :, 0:15]
        for par in range(2):
            lo, hi = 64 * par, 64 * par + 64
            v.tensor_copy(kct[lo:hi, par::2, 0:15], bb[lo:hi]).then_inc(*DV.step(f"free kct{l}", f"kct ready{l}"))

    def pe_heads(pe, l):
        PE.stage("heads")
        pe.wait_ge(*at(f"roped{l}"))
        for q in range(4):
            for c in range(NC):
                if q < 2:
                    srcs = [qkv[:, c, (0, QB0)[q] + i * P:(0, QB0)[q] + (i + 1) * P] for i in range(4)]
                elif q == 2:
                    srcs = [qkv[:, c, QB0 + 512 + i * P:QB0 + 512 + (i + 1) * P] for i in range(4)]
                else:
                    srcs = [dup[:, c, i, :] for i in range(4)]
                key = f"heads{l}{q}{c}"
                b = bank(pe, key)
                for i, s in enumerate(srcs):
                    ins = pe.transpose(b[:, i * P:(i + 1) * P], s, ident[:, :])
                ins.then_inc(*PE.step("full " + key))

    dup = view(hx, KD * N, P, NC, 4, P)

    def act_heads(act, l):
        AC.stage("heads")
        for q in range(2):
            for c in range(NC):
                key = f"heads{l}{q}{c}"
                act.wait_ge(*at("full " + key))
                b = bank_of(key)
                act.copy(qT[:, 4 * q:4 * q + 4, c * P:(c + 1) * P], b[:, :].rearrange("p (i t) -> p i t", i=4)).then_inc(*AC.step("free " + key, f"qT{l}"))

    def dve_heads(v, l):
        DV.stage("heads")
        for q in range(2, 4):
            for c in range(NC):
                key = f"heads{l}{q}{c}"
                v.wait_ge(*at("full " + key))
                b = bank_of(key)
                bb = b[:, :].rearrange("p (i t) -> p i t", i=4)
                for par in range(2):
                    lo, hi = 64 * par, 64 * par + 64
                    s0 = par if q == 2 else 8 + par
                    v.tensor_copy(kp[lo:hi, s0:s0 + 7:2, c * P:(c + 1) * P], bb[lo:hi]).then_inc(*DV.step("free " + key, f"kp{l}"))

    UNITS = [(b, h) for b in range(3) for h in range(8)]

    def unit(n):
        b, h = UNITS[n]
        pair = h // 2 + (4 if b == 2 else 0)
        slot_ = h if b == 2 else 8 + 4 * b + (h // 4) * 2 + h % 2
        vcol = (896, 1152, 2328)[b] + (h if b == 2 else h // 4) * HD
        return b, h, pair, slot_, vcol

    pool4 = {"w": 0}

    def bank4(pe, key):
        b = pool4["w"] % 4
        pool4["w"] += 1
        book.bank[key] = b
        return claim(pe, b, key)

    def obank(pe, key, b, c):
        n = 4 + 2 * (b % 2) + c
        book.bank[key] = n
        return claim(pe, n, key)

    def pe_attend(pe, l):
        PE.stage("attend")
        pe.wait_ge(*at(f"qT{l}"))
        pe.wait_ge(*at(f"kct ready{l}"))
        pe.wait_ge(*at(f"kp{l}"))
        key = f"cs{l}"
        b = bank4(pe, key)
        for h in range(8):
            for c in range(NC):
                o = (h * 2 + c) * 16
                ins = pe.matmul(b[:, o:o + 16], qT[:, h // 2, c * P:(c + 1) * P], kct[:, (h // 4) * 2 + h % 2, :],
                                    start=True, stop=True)
        ins.then_inc(*PE.step("full " + key))

        o_bank = []

        def scores(n):
            br, h, pair, sl, _ = unit(n)
            key = f"s{l}_{n}"
            b = bank4(pe, key)
            pe.matmul(b[:, 0:P], qT[:, pair, 0:P], kp[:, sl, 0:P], start=True, stop=True)
            pe.matmul(b[:, P:P + N], qT[:, pair, P:N], kp[:, sl, :], start=True, stop=True).then_inc(*PE.step("full " + key))

        def turned(n):
            key = f"pt{l}_{n}"
            b = bank4(pe, key)
            pe.wait_ge(*at(f"P{l}_{n}"))
            for i in range(3):
                ins = pe.transpose(b[:, i * P:(i + 1) * P], sm[:, n % 3, i * P:(i + 1) * P], ident[:, :])
            ins.then_inc(*PE.step("full " + key))

        def values(n):
            br, h, _, _, vcol = unit(n)
            if h == 0:
                o_bank[:] = [obank(pe, f"o{l}_{br}{c}", br + 1, c) for c in range(NC)]
            pe.wait_ge(*at(f"PT{l}_{n}"))
            o = slice(h * HD, h * HD + HD)
            p_ = pt[:, n % 3]
            ins = pe.matmul(o_bank[0][:, o], p_[:, 0:P], qkv[:, 0, vcol:vcol + HD], start=True, stop=True)
            if h == 7:
                ins.then_inc(*PE.step(f"full o{l}_{br}0"))
            pe.matmul(o_bank[1][:, o], p_[:, P:2 * P], qkv[:, 0, vcol:vcol + HD], start=True, stop=False)
            ins = pe.matmul(o_bank[1][:, o], p_[:, 2 * P:3 * P], qkv[:, 1, vcol:vcol + HD], start=False, stop=True)
            if h == 7:
                ins.then_inc(*PE.step(f"full o{l}_{br}1"))
                book.where[f"V{l}_{n}"] = PE.now
            else:
                ins.then_inc(*PE.step(f"V{l}_{n}"))

        scores(0)
        pe.wait_ge(*at(f"PC{l}"))
        for i in range(4):
            key = f"ct{l}{i}"
            b = bank4(pe, key)
            for j in range(4):
                ins = pe.transpose(b[0:16, j * P:(j + 1) * P], sC[:, 4 * i + j, :], ident[:, :])
            ins.then_inc(*PE.step("full " + key))
        scores(1)
        turned(0)
        pe.wait_ge(*at(f"PTC{l}"))
        ob = [obank(pe, f"oc{l}{c}", 0, c) for c in range(NC)]
        for c in range(NC):
            for h in range(8):
                ins = pe.matmul(ob[c][:, h * HD:(h + 1) * HD], ptc[:, 2 * h + c, :], kcv[:, 2 + h // 4, :], start=True,
                                    stop=True)
            ins.then_inc(*PE.step(f"full oc{l}{c}"))
        for n in range(2, 24):
            scores(n)
            turned(n - 1)
            values(n - 2)
        turned(23)
        values(22)
        values(23)
        pe.wait_ge(*at(f"attended{l}"))
        for kk in range(4):
            key = f"yt{l}{kk}"
            b = bank4(pe, key)
            for i in range(2):
                for c in range(NC):
                    j = 2 * kk + i
                    ins = pe.transpose(b[:, (2 * i + c) * P:(2 * i + c + 1) * P], y2[:, c, j * P:(j + 1) * P], ident[:, :])
            ins.then_inc(*PE.step("full " + key))

    def act_attend(act, l):
        AC.stage("attend")

        def probs(n):
            act.wait_ge(*at(f"sm{l}_{n}"))
            for c, (lo, hi) in enumerate(((0, P), (P, 3 * P))):
                act.activation(sm[:, n % 3, lo:hi], sm[:, n % 3, lo:hi], ACT.Exp, bias=mx[:, n % 3, c:c + 1],
                                           scale=HD ** -0.5, accum_out=sums[:, c, n:n + 1]).then_inc(*AC.step(f"P{l}_{n}"))

        def copies(n):
            key = f"pt{l}_{n}"
            act.wait_ge(*at("full " + key))
            b = bank_of(key)
            if n >= 3:
                act.wait_ge(*at(f"V{l}_{n - 3}"))
            act.copy(pt[:, n % 3, :], b[:, 0:384]).then_inc(*AC.step("free " + key, f"PT{l}_{n}"))

        act.wait_ge(*at(f"smC{l}"))
        act.activation(sC, sC, ACT.Exp, scale=HD ** -0.5).then_inc(*AC.step(f"PC{l}"))
        probs(0)
        for i in range(4):
            key = f"ct{l}{i}"
            act.wait_ge(*at("full " + key))
            b = bank_of(key)
            act.copy(ptc[:, 4 * i:4 * i + 4, :], b[0:16, :].rearrange("p (a b) -> p a b", a=4)).then_inc(*AC.step("free " + key, f"PTC{l}"))
        for n in range(1, 24):
            probs(n)
            copies(n - 1)
        copies(23)
        for kk in range(4):
            key = f"yt{l}{kk}"
            act.wait_ge(*at("full " + key))
            b = bank_of(key)
            act.copy(yT2[:, 2 * kk:2 * kk + 2, :], b[:, :].rearrange("p (a t) -> p a t", a=2)).then_inc(*AC.step("free " + key, f"ya{l + 1}", f"yb{l + 1}"))

    def dve_attend(v, l):
        DV.stage("attend")
        v.wait_ge(*at(f"full cs{l}"))
        b = bank_of(f"cs{l}")
        v.tensor_tensor(sC.rearrange("p (h c) n -> p h (c n)", c=2),
                                  b[:, 0:256].rearrange("p (h m) -> p h m", h=8),
                                  spread(cmask.rearrange("p c n -> p (c n)"), 1, 8), ALU.add).then_inc(*DV.step(f"free cs{l}"))
        v.wait_ge(*DV.last())
        v.tensor_reduce(mC, sC, AX, ALU.max).then_inc(*DV.step())
        v.wait_ge(*DV.last())
        v.tensor_tensor(sC, sC, spread(mC, 2, 16), ALU.subtract).then_inc(*DV.step(f"smC{l}"))

        def softmax_in(n):
            key = f"s{l}_{n}"
            v.wait_ge(*at("full " + key))
            b = bank_of(key)
            if n >= 3:
                v.wait_ge(*at(f"full pt{l}_{n - 3}"))
            for c, (lo, hi) in enumerate(((0, P), (P, 3 * P))):
                v.tensor_tensor_reduce(sm[:, n % 3, lo:hi], b[:, lo:hi],
                                                 causal[:, P:N] if c == 0 else causal[:, :], 1.0, -3e38, ALU.add, ALU.max,
                                                 mxr[:, n % 3, c:c + 1]).then_inc(*DV.step("free " + key))
            v.wait_ge(*DV.last())
            v.tensor_scalar(mx[:, n % 3, :], mxr[:, n % 3, :], -HD ** -0.5, None, ALU.mult).then_inc(*DV.step(f"sm{l}_{n}"))

        def outputs(br):
            v.wait_ge(*at(f"P{l}_{8 * br + 7}"))
            for c in range(NC):
                w = wts[:, c, :]
                v.reciprocal(w, sums[:, c, 8 * br:8 * br + 8]).then_inc(*DV.step())
                v.wait_ge(*DV.last())
                if br < 2:
                    g = qkv[:, c, GATES2:GATES2 + 24].rearrange("p (h b) -> p h b", b=3)[:, :, br + 1]
                    v.tensor_tensor(w, w, g, ALU.mult).then_inc(*DV.step())
                    v.wait_ge(*DV.last())
                v.wait_ge(*at(f"full o{l}_{br}{c}"))
                b = bank_of(f"o{l}_{br}{c}")
                ob = b[:, :].rearrange("p (h e) -> p h e", h=8)
                if br == 2:
                    v.tensor_tensor(y2[:, c, 512:1024].rearrange("p (h e) -> p h e", h=8), ob, spread(w, 2, HD),
                                              ALU.mult).then_inc(*DV.step(f"free o{l}_{br}{c}", f"attended{l}"))
                else:
                    v.tensor_tensor(tmpo.rearrange("p (h e) -> p h e", h=8), ob, spread(w, 2, HD), ALU.mult).then_inc(*DV.step(f"free o{l}_{br}{c}"))
                    v.wait_ge(*DV.last())
                    v.tensor_tensor(y2[:, c, 0:512], y2[:, c, 0:512], tmpo, ALU.add).then_inc(*DV.step())

        softmax_in(0)
        v.wait_ge(*at(f"PC{l}"))
        v.tensor_reduce(suC, sC, AX, ALU.add).then_inc(*DV.step())
        v.wait_ge(*DV.last())
        v.reciprocal(suC, suC).then_inc(*DV.step())
        softmax_in(1)
        v.wait_ge(*at(f"head gates{l}"))
        for c in range(NC):
            w = wts[:, c, :]
            g = qkv[:, c, GATES2:GATES2 + 24].rearrange("p (h b) -> p h b", b=3)[:, :, 0]
            v.scalar_tensor_tensor(w, suC.rearrange("p (h c) -> p h c", c=2)[:, :, c], valid[:, c:c + 1], g,
                                             ALU.mult, ALU.mult).then_inc(*DV.step())
            v.wait_ge(*DV.last())
            v.wait_ge(*at(f"full oc{l}{c}"))
            b = bank_of(f"oc{l}{c}")
            v.tensor_tensor(y2[:, c, 0:512].rearrange("p (h e) -> p h e", h=8),
                                      b[:, :].rearrange("p (h e) -> p h e", h=8), spread(w, 2, HD), ALU.mult).then_inc(*DV.step(f"free oc{l}{c}"))
        for n in range(2, 24):
            softmax_in(n)
            if n in (10, 18):
                outputs(n // 8 - 1)
        outputs(2)

    mxr = view(arena, 23690, P, 3, 2)

    def pe_gates2(pe, l, t):
        pe_linear_T(pe, f"gt2{l}{t}", f"merge2_{l}{t}0", h2, N)

    def act_gates2(act, l, *ts):
        act.wait_ge(*at(f"x mixed{l}"))
        for t in ts:
            for i in range(2):
                key = f"gt2{l}{t}{i}"
                act.wait_ge(*at("full " + key))
                b = bank_of(key)
                blk = 4 * t + 2 * i
                act.activation(gates[:, blk % KD:blk % KD + 2, blk // KD, :],
                                           b[:, :].rearrange("p (j t) -> p j t", j=2), ACT.Sigmoid).then_inc(*AC.step("free " + key, f"gates{l + 1}"))

    def pe_ffn(pe, l):
        PE.stage("ffn")
        for i in range(6):
            nb = 4 if i < 5 else 2
            pe_linear_T(pe, f"g{l}{i}_", f"gt{l}_{i}_0", h2, N, nb, None if i else f"h ffn{l + 1}")
            pe_linear_T(pe, f"u{l}{i}_", f"up{l}_{i}_0", h2, N, nb)
        acc = [bank(pe, f"down{l}{i}") for i in range(4)]
        pe.wait_ge(*at(f"hidden{l}"))
        for t in range(6):
            w = tile(pe, f"down{l}_{t}")
            nk = 4 if t < 5 else 2
            for j in range(KD):
                for k in range(nk):
                    f = 4 * t + k
                    ins = pe.matmul(acc[j // 2][:, (j % 2) * N:(j % 2 + 1) * N], w[:, k, j * P:(j + 1) * P],
                                        ffT[:, f, :], start=f == 0 and j % 2 == 0, stop=f == FB - 1, skip_group_check=True)
                if t == 5 and j % 2:
                    ins.then_inc(*PE.step(f"full down{l}{j // 2}"))
            if t < 5:
                ins.then_inc(*PE.step())
            mark_used(pe, f"down{l}_{t}")
        book.where[f"ffn read{l}"] = PE.now

    def act_ffn(act, l):
        AC.stage("ffn")
        act.wait_ge(*at(f"h ffn{l + 1} done"))
        n = 0
        for i in range(6):
            for j in range(2 if i < 5 else 1):
                key = f"g{l}{i}_{j}"
                act.wait_ge(*at("full " + key))
                b = bank_of(key)
                if n >= 2:
                    act.wait_ge(*at(f"hid{l}_{n - 2}"))
                act.activation(sg[:, n % 2, :], b[:, :], ACT.Silu).then_inc(*AC.step("free " + key, f"sg{l}_{n}"))
                n += 1

    def dve_ffn(v, l):
        DV.stage("ffn")
        n = 0
        for i in range(6):
            for j in range(2 if i < 5 else 1):
                key = f"u{l}{i}_{j}"
                v.wait_ge(*at("full " + key))
                b = bank_of(key)
                v.wait_ge(*at(f"sg{l}_{n}"))
                f = 4 * i + 2 * j
                v.tensor_tensor(ffT[:, f:f + 2, :].rearrange("p a b -> p (a b)"), b[:, :], sg[:, n % 2, :],
                                          ALU.mult).then_inc(*DV.step("free " + key, f"hid{l}_{n}", f"hidden{l}"))
                n += 1
        for j in range(KD):
            v.wait_ge(*at(f"full down{l}{j // 2}"))
            b = bank_of(f"down{l}{j // 2}")
            v.scalar_tensor_tensor(xT[:, j, :], b[:, (j % 2) * N:(j % 2 + 1) * N],
                                             adaX[l + 1][:, 40 + j:41 + j], xT[:, j, :], ALU.mult, ALU.add).then_inc(*DV.step(f"free down{l}{j // 2}", f"x layer{l}", f"x layer{l} {j}"))

    def pe_result(pe):
        PE.stage("result")
        pe.wait_ge(*at("x layer1"))
        for c in range(NC):
            for i in range(2):
                key = f"res{c}{i}"
                b = bank(pe, key)
                for j in range(4):
                    ins = pe.transpose(b[:, j * P:(j + 1) * P], xT[:, 4 * i + j, c * P:(c + 1) * P], ident[:, :])
                ins.then_inc(*PE.step("full " + key))

    def act_result(act):
        AC.stage("result")
        act.wait_ge(*at("ffn read1"))
        for c in range(NC):
            for i in range(2):
                key = f"res{c}{i}"
                act.wait_ge(*at("full " + key))
                b = bank_of(key)
                act.copy(otok[:, c, 512 * i:512 * i + 512], b[:, :]).then_inc(*AC.step("free " + key, f"result{c}{i}"))

    scrc, scrx = view(scr, 0, P, KD, N), view(scr, 2048, P, KD, N)
    n_ctx = norm("hc", ctxT, N, hcx[:, :, 0:N], gsC, adaC[:, 0:8], lambda k: f"turnc in{k // 2}",
                 ("gain c",), scrc, mg[:, KD * 2 * N - N:])
    n_x = norm("hx", xT, N, hcx[:, :, N:2 * N], gs, adaX[0][:, 0:8], lambda k: f"turnx in{k // 2}",
               ("gain mix0",), scrx)
    n_ffn0 = norm("h ffn0", xT, N, h2, gs, adaX[0][:, 24:32], lambda k: f"x mixed0 {k}", ("gain ffn0",), scrx)
    n_fin = norm("fin", xT, N, xT, c_fin, None, lambda k: f"x moe {k}", (), scrx)
    n_mix = [norm(f"h mix{l + 1}", xT, N, h2, gs, adaX[l + 1][:, 0:8],
                  (lambda k: f"fin scaled{k}", lambda k: f"x layer0 {k}")[l], (f"gain mix{l + 1}",), scrx)
             for l in range(LAYERS)]
    n_ffn = [norm(f"h ffn{l + 1}", xT, N, h2, gs, adaX[l + 1][:, 24:32], lambda k, l=l: f"x mixed{l + 1} {k}",
                  (f"gain ffn{l + 1}",), scrx) for l in range(LAYERS)]
    m_out = [mixer_out(0, "branch_hy0", "branch_ml0", "out1_", sgo, adaX[0], "adaX0b")]
    m_out += [mixer_out(l + 1, f"upa{l}_0", f"upb{l}_0", f"out2_{l}", yT2[:, 4:8], adaX[l + 1], f"ada2{l}")
              for l in range(LAYERS)]


    @block.tensor
    def _(pe):
        pe_filter(pe, 0)
        pe_tables(pe)
        pe_filter(pe, 1)
        pe_turn_in(pe, "turnx", xin, xT)
        pe_turn_in(pe, "turnc", cin, ctxT)
        pe_filter_taps(pe)
        n_ctx[0](pe)
        n_x[0](pe)
        pe_ada(pe, "adaX0a", "ada_a", 0, 4)
        pe_spectra(pe)
        pe_project(pe)
        pe_mlstm(pe)
        pe_hyena(pe)
        m_out[0][0](pe)
        n_ffn0[0](pe)
        pe_route(pe)
        pe_experts(pe)
        n_fin[0](pe)
        for l in range(LAYERS):
            n_mix[l][0](pe)
            pe_in(pe, l)
            pe_compress(pe, l)
            pe_heads(pe, l)
            pe_attend(pe, l)
            m_out[l + 1][0](pe)
            n_ffn[l][0](pe)
            pe_ffn(pe, l)
        pe_result(pe)

    @block.scalar
    def _(act):
        act_loads(act)
        act_tables(act)
        act_filter(act, 0)
        act_filter(act, 1)
        act_turn_in(act, "turnx", xT)
        act_turn_in(act, "turnc", ctxT)
        act.wait_ge(*at("full filter h13"))
        n_ctx[3](act)
        n_x[3](act)
        n_ctx[4](act)
        n_x[4](act)
        act_ada(act, "adaX0a", 0, 4)
        n_ctx[5](act)
        n_x[5](act)
        act_spectra(act)
        act_project(act)
        act_mlstm(act)
        act_second_loads(act)
        act_hyena(act)
        act_rope(act)
        act_moe_loads(act)
        n_ffn0[1](act)
        act_route(act)
        act_experts(act)
        n_fin[1](act)
        for l in range(LAYERS):
            n_mix[l][1](act)
            act_in(act, l)
            act_compress(act, l)
            act_heads(act, l)
            act_attend(act, l)
            n_ffn[l][1](act)
            act_ffn(act, l)
        act_result(act)

    @block.vector
    def _(v):
        DV.stage("tables")
        v.memset(ones[:, :], 1.0).then_inc(*DV.step("ones"))
        v.memset(cT, 0.0).then_inc(*DV.step())
        v.wait_ge(*DV.last())
        dve_filter(v, 0)
        dve_tables(v)
        dve_filter(v, 1)
        dve_filter_taps(v)
        n_ctx[6](v)
        n_x[6](v)
        dve_ada(v, "adaX0a", 0, 4, both, c_bada)
        dve_gain(v, "gain c", gsC, c_mix[:, 0:8], adaC[:, 8:16], "adaX0a")
        dve_gain(v, "gain mix0", gs, c_mix[:, 0:8], adaX[0][:, 8:16], "adaX0a")
        n_ctx[7](v)
        n_x[7](v)
        dve_project(v)
        dve_mlstm(v)
        dve_hyena(v)
        dve_rope(v)
        m_out[0][1](v)
        dve_gain(v, "gain ffn0", gs, c_ffn[:, 0:8], adaX[0][:, 32:40], "adaX0b")
        n_ffn0[2](v)
        dve_route(v)
        dve_experts(v)
        n_fin[2](v)
        for l in range(LAYERS):
            dve_gain(v, f"gain mix{l + 1}", gs, c_mix2[:, 8 * l:8 * l + 8], adaX[l + 1][:, 8:16], f"ada2{l}")
            n_mix[l][2](v)
            if l == 0:
                v.memset(kp, 0.0).then_inc(*DV.step())
            dve_blocks(v, l)
            dve_in(v, l)
            dve_dup(v, l)
            dve_compress(v, l)
            dve_heads(v, l)
            dve_attend(v, l)
            m_out[l + 1][1](v)
            dve_gain(v, f"gain ffn{l + 1}", gs, c_ffn2[:, 8 * l:8 * l + 8], adaX[l + 1][:, 32:40])
            n_ffn[l][2](v)
            dve_ffn(v, l)

    @block.sync
    def _(sp):
        SP.stage("sync")

        def load(sem, dst, src):
            sp.dma_start(dst, src).then_inc(*K.load(sem))

        def one(n, item):
            _, (src, parts, a, b) = item
            if n >= RING:
                old = n - RING
                if N_PRE <= old < POST0:
                    sp.wait_ge(*at(f"expert used{(old - N_PRE) % N_EXP}"))
                else:
                    sp.wait_ge(*at(f"used {old}"))
            sp.dma_start(place(n, parts, a, b), src).then_inc(tile_sem(n), 16)

        load("load_x", xin, A["x"][0].rearrange("(c p) n -> p c n", p=P))
        load("load_x", cin, A["ctx"][0].rearrange("(c p) n -> p c n", p=P))
        load("load_ml", bvrow, A["b_in"][0:1, ML0 + 1024:ML0 + 1536])
        sp.wait_ge(*K.loaded("load_filter"))
        sp.wait_ge(*K.loaded("load_tables"))
        for n in range(N_PRE):
            one(n, stream[n])

        def expert_tile(i, t):
            n = N_PRE + t
            if t < 8:
                w = A["w_exp1" if t < 4 else "w_exp3"][0][i]
                src = w[256 * (t % 4):256 * (t % 4) + 256, :].rearrange("(k p) n -> p k n", p=P)
                dst = place(n, P, 2, 4 * 512)
            else:
                src = A["w_exp2"][0][i][512 * (t - 8):512 * (t - 8) + 512, :].rearrange("(k p) n -> p k n", p=P)
                dst = place(n, P, 4, D)
            sp.dma_start(dst, src).then_inc(tile_sem(n), 16)

        for t in range(RING):
            sp.wait_ge(*at(f"used {N_PRE + t - RING}"))
            expert_tile(0, t)
        with sp.Fori(0, EXPERTS - 1) as i:
            K.turn = i
            for t in range(RING, N_EXP):
                sp.wait_ge(*at(f"expert used{t - RING}"))
                expert_tile(i, t)
            for t in range(RING):
                sp.wait_ge(*at(f"expert used{N_EXP - RING + t}"))
                expert_tile(i + 1, t)
        K.turn = None
        for t in range(RING, N_EXP):
            sp.wait_ge(*at(f"expert used{t - RING}"))
            expert_tile(EXPERTS - 1, t)
        for i, item in enumerate(after_experts):
            one(POST0 + i, item)
        for c in range(NC):
            for i in range(2):
                sp.wait_ge(*at(f"result{c}{i}"))
                sp.dma_start(out[0, c * P:(c + 1) * P, 512 * i:512 * i + 512],
                             otok[:, c, 512 * i:512 * i + 512]).then_inc(*K.load("stored"))
        sp.wait_ge(*K.loaded("stored"))

    book.loads = K.loads


def constants():
    f32 = lambda a: np.ascontiguousarray(a, dtype=np.float32)
    L = N
    t = np.linspace(0.0, 1.0, L)
    bands = np.linspace(1e-4, 15, 16)
    an = (2.0 * np.pi / L) * np.arange(L)[:, None] * bands[None, :]
    z = np.concatenate([t[:, None], np.cos(an), np.sin(an)], axis=1)
    lo, hi = np.log(1e-2) / 1.5, np.log(1e-2) / 0.3
    dec = np.exp(-t[:, None] * np.abs(np.linspace(lo, hi, HY))[None, :])
    dec2 = dec.copy()
    dec2[0] = 0.0
    w = 2 * np.pi * np.outer(np.arange(L), np.arange(L)) / (2 * L)
    cos, msin = np.cos(w), -np.sin(w)
    nyq = np.cos(np.pi * np.arange(L))
    msin_u = msin.copy()
    msin_u[:, 0] = nyq
    msin_k, cos_k = msin[:, 0:128].copy(), cos[:, 0:128].copy()
    msin_k[:, 0] = 0.0
    cos_k[:, 0] = nyq
    inv_r, inv_i = 2 * np.cos(w).T / (2 * L), -2 * np.sin(w).T / (2 * L)
    inv_r[0] /= 2
    inv_i[0] = nyq / (2 * L)
    chunks = lambda a: a.reshape(2, P, *a.shape[1:]).swapaxes(0, 1)
    s, tt = np.arange(P)[:, None], np.arange(P)[None, :]
    fwd, bwd = np.where(s <= tt, 0.0, BIG), np.where(s >= tt, 0.0, BIG)
    zero = np.zeros((P, P))
    mask = np.stack([np.concatenate([fwd, zero], 1), np.concatenate([zero, bwd], 1)], 1)
    selh = np.zeros((4, 4, P))
    for h in range(4):
        selh[h, h] = 1.0
    causal = np.concatenate([zero, np.where(tt <= s, 0.0, NEG)], 1)
    ends = 16 * np.arange(16) + 31
    tok = np.arange(N)
    cm = np.where((ends[None, :] <= tok[:, None]) & (np.arange(16) < NCMP)[None, :], 0.0, NEG)
    inv = 1.0 / (10000.0 ** (np.arange(0, HD, 2, dtype=np.float32) / np.float32(HD)))
    return {
        "k_zT": f32(z.T), "k_decay": f32(chunks(np.stack([dec, dec2], 1))), "k_dftc": f32(chunks(cos)),
        "k_dfts": f32(chunks(msin_u)), "k_dftn": f32(chunks(np.stack([msin_k, cos_k], 1))),
        "k_idft": f32(np.concatenate([inv_r, inv_i], 0).reshape(4, P, N).swapaxes(0, 1)),
        "k_ident": f32(np.eye(P)), "k_mask": f32(mask), "k_selh": f32(selh), "k_causal": f32(causal),
        "k_cmask": f32(chunks(cm)), "k_valid": f32(chunks((tok >= 31).astype(float))),
        "k_inv": f32(np.broadcast_to(inv, (P, 32))), "k_iota": f32(np.broadcast_to(np.arange(CAP), (P, CAP))),
        "k_slot": f32((np.arange(P) % CAP)[:, None]),
    }


def kernel(**inputs):
    import concourse.bacc as bacc
    from concourse.bass_utils import run_bass_kernel_spmd

    arrays = {f"in_{k}": np.ascontiguousarray(v) for k, v in inputs.items()}
    arrays.update({f"in_{k}": v for k, v in constants().items()})

    book = Book()
    for turn in range(2):
        nc = bacc.Bacc("TRN2", target_bir_lowering=False, num_devices=1, dynamic_dma_scratch_size=1024)
        A = {k[3:]: nc.dram_tensor(k, v.shape, mybir.dt.from_np(v.dtype), kind="ExternalInput").ap()
             for k, v in arrays.items()}
        out = nc.dram_tensor("out_0", (1, N, D), F32, kind="ExternalOutput").ap()
        build(nc, A, out, book)
        book.known = True
    r = run_bass_kernel_spmd(nc, [arrays], core_ids=[0])
    return r.results[0]["out_0"]
```
